# Optimizing a Trainium2 kernel written in Bass

```python
import math, functools
import jax, jax.numpy as jnp
from jax import lax
import numpy as np

D_MODEL = 1024
BATCH = 1
SEQ = 256
DEPTH = 1
DEC_BATCH = 8
DEC_SEQ = 1
PAST_LEN = 2048
PAGE_SIZE = 128

A_HEADS = 8
QK_NOPE = 64
QK_ROPE = 32
V_DIM = 64
Q_LORA = 384
KV_LORA = 256
ROPE_BASE = 10000.0
Q_BLOCK = 128
ATTN_SCALE = (QK_NOPE + QK_ROPE) ** -0.5
S_HEADS = 16
S_HEAD_DIM = 64
D_INNER = S_HEADS * S_HEAD_DIM
S_GROUPS = 2
D_STATE = 128
CONV_W = 4
CONV_CH = D_INNER + 2 * S_GROUPS * D_STATE
CHUNK = 128
N_EXPERTS = 64
TOP_K = 6
N_EXP_GROUPS = 8
TOPK_GROUPS = 4
F_EXPERT = 256
F_SHARED = 256
ROUTE_SCALE = 2.5
EPS = 1e-6
IN_SPLITS = (Q_LORA, KV_LORA, QK_ROPE, D_INNER, CONV_CH, S_HEADS, D_MODEL, D_MODEL)
D_IN = Q_LORA + KV_LORA + QK_ROPE + D_INNER + CONV_CH + S_HEADS + 2 * D_MODEL

kernel_name = 'hybrid_mla_ssd_moe_step'

def rms_norm(x, g):
    xf = x.astype(jnp.float32)
    xf = xf * lax.rsqrt(jnp.mean(xf * xf, axis=-1, keepdims=True) + EPS)
    return (xf * g.astype(jnp.float32)).astype(x.dtype)

def rope_cos_sin(pos):
    half = QK_ROPE // 2
    inv = ROPE_BASE ** (-jnp.arange(half, dtype=jnp.float32) / half)
    ang = pos.astype(jnp.float32)[:, None] * inv[None, :]
    return jnp.cos(ang), jnp.sin(ang)

def apply_rope(x, cos, sin):
    x1, x2 = jnp.split(x.astype(jnp.float32), 2, axis=-1)
    return jnp.concatenate([x1 * cos - x2 * sin, x2 * cos + x1 * sin], axis=-1).astype(x.dtype)

def adaln(c, p):
    mod = jax.nn.silu(c) @ p['w_ada'] + p['b_ada']
    return jnp.split(mod[:, None, :], 6, axis=-1)

def mla_qkv(q_a, kv_a, kpe_raw, pos, p):
    b, s = q_a.shape[:2]
    q = (rms_norm(q_a, p['g_q_a']) @ p['w_q_b']).reshape(b, s, A_HEADS, QK_NOPE + QK_ROPE)
    cos, sin = rope_cos_sin(pos)
    q_nope = q[..., :QK_NOPE]
    q_pe = apply_rope(q[..., QK_NOPE:], cos[:, None, :], sin[:, None, :])
    k_pe = apply_rope(kpe_raw, cos, sin)
    ckv = rms_norm(kv_a, p['g_kv_a'])
    return q_nope, q_pe, ckv, k_pe

def mla_attend_prompt(q_nope, q_pe, ckv, k_pe, p):
    b, s = q_nope.shape[:2]
    k_nope = jnp.einsum('bkc,chd->bkhd', ckv, p['w_uk'])
    v = jnp.einsum('bkc,chd->bkhd', ckv, p['w_uv'])
    nb = s // Q_BLOCK
    qn = q_nope.reshape(b, nb, Q_BLOCK, A_HEADS, QK_NOPE).swapaxes(0, 1)
    qp = q_pe.reshape(b, nb, Q_BLOCK, A_HEADS, QK_ROPE).swapaxes(0, 1)
    key_pos = jnp.arange(s)

    def one_block(args):
        qn_b, qp_b, blk = args
        sc = (jnp.einsum('bqhd,bkhd->bhqk', qn_b, k_nope)
              + jnp.einsum('bqhr,bkr->bhqk', qp_b, k_pe)).astype(jnp.float32) * ATTN_SCALE
        q_pos = blk * Q_BLOCK + jnp.arange(Q_BLOCK)
        sc = jnp.where(key_pos[None, :] <= q_pos[:, None], sc, -jnp.inf)
        pr = jax.nn.softmax(sc, axis=-1).astype(v.dtype)
        return jnp.einsum('bhqk,bkhd->bqhd', pr, v)

    o = lax.map(one_block, (qn, qp, jnp.arange(nb)))
    return o.swapaxes(0, 1).reshape(b, s, A_HEADS * V_DIM)

def mla_attend_sample(q_nope, q_pe, ckv, k_pe, cache_ckv, cache_kpe, layer, page_table, p):
    b, s = q_nope.shape[:2]
    ckv_past = cache_ckv[layer, page_table].reshape(b, -1, KV_LORA)
    kpe_past = cache_kpe[layer, page_table].reshape(b, -1, QK_ROPE)
    n_past = ckv_past.shape[1]
    q_lat = jnp.einsum('bshd,chd->bshc', q_nope, p['w_uk'])
    sc_past = jnp.einsum('bshc,btc->bhst', q_lat, ckv_past) + jnp.einsum('bshr,btr->bhst', q_pe, kpe_past)
    sc_new = jnp.einsum('bshc,btc->bhst', q_lat, ckv) + jnp.einsum('bshr,btr->bhst', q_pe, k_pe)
    causal = jnp.tril(jnp.ones((s, s), dtype=bool))
    sc_new = jnp.where(causal, sc_new.astype(jnp.float32), -jnp.inf)
    sc = jnp.concatenate([sc_past.astype(jnp.float32), sc_new], axis=-1) * ATTN_SCALE
    pr = jax.nn.softmax(sc, axis=-1).astype(ckv.dtype)
    o_lat = (jnp.einsum('bhst,btc->bshc', pr[..., :n_past], ckv_past)
             + jnp.einsum('bhst,btc->bshc', pr[..., n_past:], ckv))
    return jnp.einsum('bshc,chd->bshd', o_lat, p['w_uv']).reshape(b, s, A_HEADS * V_DIM)

def causal_conv(xbc, conv_state, p):
    xpad = jnp.concatenate([conv_state.astype(xbc.dtype), xbc], axis=1)
    out = lax.conv_general_dilated(xpad, p['conv_w'][:, None, :], window_strides=(1,), padding='VALID',
                                   dimension_numbers=('NWC', 'WIO', 'NWC'), feature_group_count=CONV_CH)
    return jax.nn.silu(out + p['conv_b']), xpad[:, -(CONV_W - 1):]

def ssd_split(xbc, dt_raw, p):
    b, s = xbc.shape[:2]
    gn = S_GROUPS * D_STATE
    rep = S_HEADS // S_GROUPS
    xs = xbc[..., :D_INNER].reshape(b, s, S_HEADS, S_HEAD_DIM)
    bs = jnp.repeat(xbc[..., D_INNER:D_INNER + gn].reshape(b, s, S_GROUPS, D_STATE), rep, axis=2)
    cs = jnp.repeat(xbc[..., D_INNER + gn:].reshape(b, s, S_GROUPS, D_STATE), rep, axis=2)
    dt = jax.nn.softplus((dt_raw + p['dt_bias']).astype(jnp.float32))
    a = dt * (-jnp.exp(p['a_log'].astype(jnp.float32)))
    return xs, bs, cs, dt, a

def ssd_chunked(xs, bs, cs, dt, a, h0):
    b, s = xs.shape[:2]
    nc = s // CHUNK
    xdt = (xs.astype(jnp.float32) * dt[..., None]).reshape(b, nc, CHUNK, S_HEADS, S_HEAD_DIM)
    bc = bs.astype(jnp.float32).reshape(b, nc, CHUNK, S_HEADS, D_STATE)
    cc = cs.astype(jnp.float32).reshape(b, nc, CHUNK, S_HEADS, D_STATE)
    a_cum = jnp.cumsum(a.reshape(b, nc, CHUNK, S_HEADS), axis=2)
    seg = a_cum[:, :, :, None, :] - a_cum[:, :, None, :, :]
    causal = jnp.tril(jnp.ones((CHUNK, CHUNK), dtype=bool))[None, None, :, :, None]
    lmat = jnp.exp(jnp.where(causal, seg, -jnp.inf))
    y_diag = jnp.einsum('bclsh,bcshp->bclhp', jnp.einsum('bclhn,bcshn->bclsh', cc, bc) * lmat, xdt)
    decay_end = jnp.exp(a_cum[:, :, -1:, :] - a_cum)
    chunk_states = jnp.einsum('bclhn,bclh,bclhp->bchpn', bc, decay_end, xdt)
    chunk_decay = jnp.exp(a_cum[:, :, -1, :])

    def step(h, inp):
        st, dec = inp
        return h * dec[:, :, None, None] + st, h

    h_final, h_prev = lax.scan(step, h0, (chunk_states.swapaxes(0, 1), chunk_decay.swapaxes(0, 1)))
    h_prev = h_prev.swapaxes(0, 1)
    y_off = jnp.einsum('bclhn,bchpn,bclh->bclhp', cc, h_prev, jnp.exp(a_cum))
    return (y_diag + y_off).reshape(b, s, S_HEADS, S_HEAD_DIM), h_final

def ssd_recurrent(xs, bs, cs, dt, a, h0):
    def step(h, inp):
        x_t, b_t, c_t, dt_t, a_t = inp
        h = h * jnp.exp(a_t)[..., None, None] + jnp.einsum('bhp,bhn->bhpn', x_t * dt_t[..., None], b_t)
        return h, jnp.einsum('bhpn,bhn->bhp', h, c_t)

    seq = (xs.astype(jnp.float32).swapaxes(0, 1), bs.astype(jnp.float32).swapaxes(0, 1),
           cs.astype(jnp.float32).swapaxes(0, 1), dt.swapaxes(0, 1), a.swapaxes(0, 1))
    h_final, ys = lax.scan(step, h0, seq)
    return ys.swapaxes(0, 1), h_final

def ssd_output(y, xs, z, p):
    b, s = y.shape[:2]
    y = y + p['d_skip'].astype(jnp.float32)[:, None] * xs.astype(jnp.float32)
    y = y.reshape(b, s, D_INNER) * jax.nn.silu(z.astype(jnp.float32))
    y = rms_norm(y.reshape(b, s, S_GROUPS, D_INNER // S_GROUPS), p['g_ssd'].reshape(S_GROUPS, -1))
    return y.reshape(b, s, D_INNER).astype(z.dtype)

def mixer_core(h, pos, p, attend, conv_state, ssm_state, scan):
    u = h @ p['w_in']
    offs = tuple(int(o) for o in np.cumsum(IN_SPLITS)[:-1])
    q_a, kv_a, kpe_raw, z, xbc, dt_raw, gate_a, gate_b = jnp.split(u, offs, axis=-1)
    q_nope, q_pe, ckv, k_pe = mla_qkv(q_a, kv_a, kpe_raw, pos, p)
    o_attn = attend(q_nope, q_pe, ckv, k_pe) @ p['w_o_attn']
    xbc_c, new_conv = causal_conv(xbc, conv_state, p)
    xs, bs, cs, dt, a = ssd_split(xbc_c, dt_raw, p)
    y, new_ssm = scan(xs, bs, cs, dt, a, ssm_state.astype(jnp.float32))
    o_ssd = ssd_output(y, xs, z, p) @ p['w_o_ssd']
    merged = jax.nn.sigmoid(gate_a) * o_attn + jax.nn.sigmoid(gate_b) * o_ssd
    return merged @ p['w_out'], (ckv, k_pe, new_conv, new_ssm.astype(h.dtype))

def moe_ffn(h, p):
    b, s, d = h.shape
    t = h.reshape(b * s, d)
    scores = jax.nn.sigmoid((t @ p['w_router']).astype(jnp.float32))
    biased = scores + p['b_router'].astype(jnp.float32)
    grp = biased.reshape(-1, N_EXP_GROUPS, N_EXPERTS // N_EXP_GROUPS)
    grp_score = lax.top_k(grp, 2)[0].sum(-1)
    _, g_idx = lax.top_k(grp_score, TOPK_GROUPS)
    g_mask = jax.nn.one_hot(g_idx, N_EXP_GROUPS, dtype=jnp.float32).sum(-2) > 0
    e_mask = jnp.repeat(g_mask, N_EXPERTS // N_EXP_GROUPS, axis=-1)
    _, e_idx = lax.top_k(jnp.where(e_mask, biased, -jnp.inf), TOP_K)
    w = jnp.take_along_axis(scores, e_idx, axis=-1)
    w = w / jnp.sum(w, axis=-1, keepdims=True) * ROUTE_SCALE
    combine = jnp.einsum('tk,tke->te', w, jax.nn.one_hot(e_idx, N_EXPERTS, dtype=jnp.float32)).astype(h.dtype)
    gte = jnp.einsum('td,edf->tef', t, p['w_gate_e'])
    upe = jnp.einsum('td,edf->tef', t, p['w_up_e'])
    routed = jnp.einsum('tef,efd->td', jax.nn.silu(gte) * upe * combine[:, :, None], p['w_down_e'])
    shared = (jax.nn.silu(t @ p['w_gate_s']) * (t @ p['w_up_s'])) @ p['w_down_s']
    return (routed + shared).reshape(b, s, d)

def block(x, c, p, mix):
    sh1, sc1, g1, sh2, sc2, g2 = adaln(c, p)
    h = rms_norm(x, p['g_pre_mix']) * (1 + sc1) + sh1
    m, st = mix(h)
    x = x + g1 * rms_norm(m, p['g_post_mix'])
    h = rms_norm(x, p['g_pre_ffn']) * (1 + sc2) + sh2
    x = x + g2 * rms_norm(moe_ffn(h, p), p['g_post_ffn'])
    return x, st

def setup_inputs(seed: int = 0) -> dict:
    key = jax.random.key(seed)
    ks = iter(jax.random.split(key, 64))
    f32 = jnp.float32

    def nrm(shape, scale):
        return jax.random.normal(next(ks), shape, f32) * scale

    def gain(n):
        return 1.0 + 0.02 * jax.random.normal(next(ks), (DEPTH, n), f32)

    n_pages = PAST_LEN // PAGE_SIZE
    n_used = DEC_BATCH * n_pages
    n_pool = n_used + max(1, n_used // 4)
    perm = jax.random.permutation(next(ks), n_pool)
    page_table = perm[:n_used].reshape(DEC_BATCH, n_pages).astype(jnp.int32)
    dt0 = jnp.exp(jax.random.uniform(next(ks), (DEPTH, S_HEADS), f32, math.log(1e-3), math.log(1e-1)))
    dt_bias = dt0 + jnp.log(-jnp.expm1(-dt0))
    a_log = jnp.log(jax.random.uniform(next(ks), (DEPTH, S_HEADS), f32, 1.0, 16.0))
    inp = {
        'x_prompt': nrm((BATCH, SEQ, D_MODEL), 1.0),
        'x_sample': nrm((DEC_BATCH, DEC_SEQ, D_MODEL), 1.0),
        'cache_ckv': nrm((DEPTH, n_pool, PAGE_SIZE, KV_LORA), 1.0),
        'cache_kpe': nrm((DEPTH, n_pool, PAGE_SIZE, QK_ROPE), 1.0),
        'state_conv': nrm((DEPTH, DEC_BATCH, CONV_W - 1, CONV_CH), 1.0),
        'state_ssm': nrm((DEPTH, DEC_BATCH, S_HEADS, S_HEAD_DIM, D_STATE), 0.5),
        'page_table': page_table,
        'c_prompt': nrm((BATCH, D_MODEL), 1.0),
        'c_sample': nrm((DEC_BATCH, D_MODEL), 1.0),
        'w_ada': nrm((DEPTH, D_MODEL, 6 * D_MODEL), 0.3 * D_MODEL ** -0.5),
        'b_ada': nrm((DEPTH, 6 * D_MODEL), 0.02),
        'g_pre_mix': gain(D_MODEL),
        'g_post_mix': gain(D_MODEL),
        'g_pre_ffn': gain(D_MODEL),
        'g_post_ffn': gain(D_MODEL),
        'w_in': nrm((DEPTH, D_MODEL, D_IN), D_MODEL ** -0.5),
        'g_q_a': gain(Q_LORA),
        'w_q_b': nrm((DEPTH, Q_LORA, A_HEADS * (QK_NOPE + QK_ROPE)), Q_LORA ** -0.5),
        'g_kv_a': gain(KV_LORA),
        'w_uk': nrm((DEPTH, KV_LORA, A_HEADS, QK_NOPE), KV_LORA ** -0.5),
        'w_uv': nrm((DEPTH, KV_LORA, A_HEADS, V_DIM), KV_LORA ** -0.5),
        'w_o_attn': nrm((DEPTH, A_HEADS * V_DIM, D_MODEL), (A_HEADS * V_DIM) ** -0.5),
        'conv_w': nrm((DEPTH, CONV_W, CONV_CH), CONV_W ** -0.5),
        'conv_b': nrm((DEPTH, CONV_CH), 0.02),
        'dt_bias': dt_bias,
        'a_log': a_log,
        'd_skip': 1.0 + nrm((DEPTH, S_HEADS), 0.1),
        'g_ssd': gain(D_INNER),
        'w_o_ssd': nrm((DEPTH, D_INNER, D_MODEL), D_INNER ** -0.5),
        'w_out': nrm((DEPTH, D_MODEL, D_MODEL), D_MODEL ** -0.5),
        'w_router': nrm((DEPTH, D_MODEL, N_EXPERTS), D_MODEL ** -0.5),
        'b_router': nrm((DEPTH, N_EXPERTS), 0.01),
        'w_gate_e': nrm((DEPTH, N_EXPERTS, D_MODEL, F_EXPERT), D_MODEL ** -0.5),
        'w_up_e': nrm((DEPTH, N_EXPERTS, D_MODEL, F_EXPERT), D_MODEL ** -0.5),
        'w_down_e': nrm((DEPTH, N_EXPERTS, F_EXPERT, D_MODEL), F_EXPERT ** -0.5),
        'w_gate_s': nrm((DEPTH, D_MODEL, F_SHARED), D_MODEL ** -0.5),
        'w_up_s': nrm((DEPTH, D_MODEL, F_SHARED), D_MODEL ** -0.5),
        'w_down_s': nrm((DEPTH, F_SHARED, D_MODEL), F_SHARED ** -0.5),
    }
    return inp

def reference(x_prompt, x_sample, cache_ckv, cache_kpe, state_conv, state_ssm, page_table, c_prompt, c_sample,
              w_ada, b_ada, g_pre_mix, g_post_mix, g_pre_ffn, g_post_ffn, w_in, g_q_a, w_q_b, g_kv_a, w_uk, w_uv,
              w_o_attn, conv_w, conv_b, dt_bias, a_log, d_skip, g_ssd, w_o_ssd, w_out, w_router, b_router,
              w_gate_e, w_up_e, w_down_e, w_gate_s, w_up_s, w_down_s):
    bp, sp = x_prompt.shape[:2]
    ds = x_sample.shape[1]
    pos_p = jnp.arange(sp)
    pos_s = PAST_LEN + jnp.arange(ds)
    y_prompt, y_sample = x_prompt, x_sample
    new_p, new_s = [], []
    for l in range(DEPTH):
        p = {'w_ada': w_ada[l], 'b_ada': b_ada[l], 'g_pre_mix': g_pre_mix[l], 'g_post_mix': g_post_mix[l],
             'g_pre_ffn': g_pre_ffn[l], 'g_post_ffn': g_post_ffn[l], 'w_in': w_in[l], 'g_q_a': g_q_a[l],
             'w_q_b': w_q_b[l], 'g_kv_a': g_kv_a[l], 'w_uk': w_uk[l], 'w_uv': w_uv[l], 'w_o_attn': w_o_attn[l],
             'conv_w': conv_w[l], 'conv_b': conv_b[l], 'dt_bias': dt_bias[l], 'a_log': a_log[l],
             'd_skip': d_skip[l], 'g_ssd': g_ssd[l], 'w_o_ssd': w_o_ssd[l], 'w_out': w_out[l],
             'w_router': w_router[l], 'b_router': b_router[l], 'w_gate_e': w_gate_e[l], 'w_up_e': w_up_e[l],
             'w_down_e': w_down_e[l], 'w_gate_s': w_gate_s[l], 'w_up_s': w_up_s[l], 'w_down_s': w_down_s[l]}
        mix_p = functools.partial(
            mixer_core, pos=pos_p, p=p, attend=functools.partial(mla_attend_prompt, p=p),
            conv_state=jnp.zeros((bp, CONV_W - 1, CONV_CH), x_prompt.dtype),
            ssm_state=jnp.zeros((bp, S_HEADS, S_HEAD_DIM, D_STATE), jnp.float32), scan=ssd_chunked)
        y_prompt, st_p = block(y_prompt, c_prompt, p, mix_p)
        mix_s = functools.partial(
            mixer_core, pos=pos_s, p=p,
            attend=functools.partial(mla_attend_sample, cache_ckv=cache_ckv, cache_kpe=cache_kpe, layer=l,
                                     page_table=page_table, p=p),
            conv_state=state_conv[l], ssm_state=state_ssm[l], scan=ssd_recurrent)
        y_sample, st_s = block(y_sample, c_sample, p, mix_s)
        new_p.append(st_p)
        new_s.append(st_s)
    ckv_p = jnp.stack([t[0] for t in new_p])
    kpe_p = jnp.stack([t[1] for t in new_p])
    conv_p = jnp.stack([t[2] for t in new_p])
    ssm_p = jnp.stack([t[3] for t in new_p])
    ckv_s = jnp.stack([t[0] for t in new_s])
    kpe_s = jnp.stack([t[1] for t in new_s])
    conv_s = jnp.stack([t[2] for t in new_s])
    ssm_s = jnp.stack([t[3] for t in new_s])
    return (y_prompt, y_sample, ckv_p, kpe_p, conv_p, ssm_p, ckv_s, kpe_s, conv_s, ssm_s)


_drawn_inputs = setup_inputs


def setup_inputs(seed=0):
    import zlib

    import numpy as np

    out = dict(_drawn_inputs(seed))
    spreads = {}
    factors = {'cache_ckv': 3.177,
     'cache_kpe': 8.0,
     'g_post_mix': 6.032,
     'g_post_ffn': 8.0,
     'g_q_a': 8.0,
     'g_kv_a': 2.917,
     'd_skip': 4.202,
     'g_ssd': 6.03}
    for name, (base, spread) in spreads.items():
        noise = np.random.default_rng([zlib.crc32(name.encode()), seed]).standard_normal(out[name].shape)
        drawn = base * np.exp(spread * noise) if base else spread * noise
        out[name] = __import__('jax').numpy.asarray(drawn.astype(out[name].dtype))
    for name, factor in factors.items():
        out[name] = (out[name] * factor).astype(out[name].dtype)
    return out
```

```python
from contextlib import ExitStack

import numpy as np
import concourse.bass as bass
from concourse import mybir

F32 = mybir.dt.float32
I32 = mybir.dt.int32
U32 = mybir.dt.uint32
ALU = mybir.AluOpType
ACT = mybir.ActivationFunctionType
AX = mybir.AxisListType

P = 128
D = 1024
KD = D // P
TP, TS = 256, 8
T = TP + TS
ROWS = 1 + TS
NH, NOPE, ROPE, VD = 8, 64, 32, 64
QH = NOPE + ROPE
QL, KVL = 384, 256
SCALE = QH ** -0.5
PAST, PAGE = 2048, 128
NPG = PAST // PAGE
POOL = 160
PW = KVL + ROPE
SH, SP_, NS, SG = 16, 64, 128, 2
DI = SH * SP_
KI = DI // P
CH = 128
CW = 4
CC = DI + 2 * SG * NS
KC = CC // P
NE, TOPK, NG, TOPG, FE = 64, 6, 8, 4, 256
EPG = NE // NG
ROUTE = 2.5
EPS = 1e-6
BIG = 1e30
NT = 3
TILE_ROWS = (128, 128, 8)
LB = 64
ROUNDS = -(-T // LB)
NBLK = NE * ROUNDS
MAXOVER = TOPK * T // LB
SKIP = 1 << 20

RING = 3
UW = 4096
N_ADA, N_WIN = 12, 11
U_WIN = N_ADA
U_QB = U_WIN + N_WIN
U_OA = U_QB + 1
U_OS = U_OA + 1
U_OUT = U_OS + 2
U_SGU = U_OUT + 2
U_SDN = U_SGU + 1
N_UNITS = U_SDN + 1

PARAMS = {}
_at = 0
for _name, _n in (("b_ada", 48), ("g_pre_mix", 8), ("g_post_mix", 8), ("g_pre_ffn", 8), ("g_post_ffn", 8),
                  ("g_q_a", 3), ("g_kv_a", 2), ("g_ssd", 8), ("d_skip", 8), ("conv_w", 48), ("conv_b", 12),
                  ("heads", 2), ("b_router", 64)):
    PARAMS[_name] = (_at, _at + _n)
    _at += _n
NPAR = _at
CONSTS = {}
_at = 0
for _name, _n in (("ident", P), ("ones", P), ("causal_t", P), ("before", P), ("mask", P), ("cos", T), ("sin", T),
                  ("eps", 1), ("expert", NE), ("valid", NT), ("later", NBLK - NE),
                  ("count", MAXOVER)):
    CONSTS[_name] = (_at, _at + _n)
    _at += _n
NCON = _at


def build(nc, io):
    with ExitStack() as top:
        def sem(name, stack=top):
            return stack.enter_context(nc.semaphore(name))

        def sb(name, shape, dt=F32, stack=top):
            return stack.enter_context(nc.sbuf_tensor(name, shape, dt))

        bank = top.enter_context(nc.psum_tensor("bank", [P, 8, 512], F32))

        ring = sb("ring", [P, RING, UW])
        par = sb("par", [P, NPAR])
        con = sb("con", [P, NCON])
        x = sb("x", [P, KD, T])
        mod = sb("mod", [P, 48, ROWS])
        sq = sb("sq", [P, KD, T])
        root = sb("root", [P, T])
        rstd = sb("rstd", [P, T])
        gain = sb("gain", [P, KD, ROWS])
        norm_tmp = sq

        def pcol(name, lo=0, n=None):
            a, b = PARAMS[name]
            return par[:, a + lo:(b if n is None else a + lo + n)]

        def ccol(name):
            a, b = CONSTS[name]
            return con[:, a:b]
        ident, ones, eps = ccol("ident"), ccol("ones"), ccol("eps")

        small_in = sem("small_in")
        unit_in = [sem(f"unit_in{s}") for s in range(RING)]
        unit_used = sem("unit_used")
        squares_ready, sums_ready, root_ready, rstd_ready = (
            sem("squares_ready"), sem("sums_ready"), sem("root_ready"), sem("rstd_ready"))
        dve_order, pool_order, sp_order, pe_order = sem("dve_order"), sem("pool_order"), sem("sp_order"), sem("pe_order")
        stored = sem("stored")
        n_stored = [0]
        order = {"dve": 0}

        def link(ins):
            order["dve"] += 1
            ins.then_inc(dve_order, 1)
            nc.vector.wait_ge(dve_order, order["dve"])

        def store(eng, dst, src):
            eng.dma_start(dst, src).then_inc(stored, 16)
            n_stored[0] += 16

        loaded = [0]

        def load_units(sp, upto):
            while loaded[0] < min(upto, N_UNITS):
                u = loaded[0]
                if u >= RING:
                    sp.wait_ge(unit_used, u - RING + 1)
                sp.dma_start(ring[:, u % RING, :], io["w_units"][u]).then_inc(unit_in[u % RING], 16)
                loaded[0] += 1

        def unit(u, pattern, **sizes):
            n = int(np.prod(list(sizes.values())))
            return ring[:, u % RING, 0:n].rearrange(pattern, **sizes)

        def wait_unit(pe, u):
            pe.wait_ge(unit_in[u % RING], 16 * (u // RING + 1))

        def act_square(n, src, tiles):
            nc.scalar.activation(sq[:, 0:tiles, :], src, ACT.Square).then_inc(squares_ready, 1)

        def pe_norm(n, tiles, b):
            nc.tensor.wait_ge(squares_ready, n + 1)
            for k in range(tiles):
                mm = nc.tensor.matmul(bank[:, b, 0:T], ones, sq[:, k, :], start=(k == 0), stop=(k == tiles - 1))
            mm.then_inc(sums_ready, 1)

        def act_root(n, dim, b):
            nc.scalar.wait_ge(sums_ready, n + 1)
            if n:
                nc.scalar.wait_ge(rstd_ready, n)
            nc.scalar.activation(root[:, :], bank[:, b, 0:T], ACT.Sqrt, bias=eps, scale=1.0 / dim).then_inc(root_ready, 1)

        def dve_rstd(n):
            nc.vector.wait_ge(root_ready, n + 1)
            nc.vector.reciprocal(rstd[:, :], root[:, :]).then_inc(rstd_ready, 1)
            nc.vector.wait_ge(rstd_ready, n + 1)

        def dve_modulate(src, dst, g, shift, scale, done):
            v = nc.vector
            link(v.tensor_scalar(gain[:, :, :], mod[:, 8 * scale:8 * scale + 8, :], 1.0, None, ALU.add))
            link(v.tensor_tensor(gain[:, :, :], gain[:, :, :], g.unsqueeze(2).to_broadcast([P, KD, ROWS]), ALU.mult))
            link(v.tensor_tensor(norm_tmp[:, :, :], src, rstd[:, :].unsqueeze(1).to_broadcast([P, KD, T]), ALU.mult))
            for k in range(KD):
                v.tensor_scalar(dst[:, k, 0:TP], norm_tmp[:, k, 0:TP], gain[:, k, 0:1], mod[:, 8 * shift + k, 0:1],
                                ALU.mult, ALU.add)
            link(v.tensor_tensor(norm_tmp[:, :, TP:T], norm_tmp[:, :, TP:T], gain[:, :, 1:ROWS], ALU.mult))
            v.tensor_tensor(dst[:, :, TP:T], norm_tmp[:, :, TP:T], mod[:, 8 * shift:8 * shift + 8, 1:ROWS],
                            ALU.add).then_inc(done, 1)

        def dve_residual(src, dst, g, gate, done):
            v = nc.vector
            link(v.tensor_tensor(gain[:, :, :], mod[:, 8 * gate:8 * gate + 8, :],
                                 g.unsqueeze(2).to_broadcast([P, KD, ROWS]), ALU.mult))
            link(v.tensor_tensor(norm_tmp[:, :, :], src, rstd[:, :].unsqueeze(1).to_broadcast([P, KD, T]), ALU.mult))
            for k in range(KD):
                v.scalar_tensor_tensor(dst[:, k, 0:TP], norm_tmp[:, k, 0:TP], gain[:, k, 0:1], x[:, k, 0:TP],
                                       ALU.mult, ALU.add)
            link(v.tensor_tensor(norm_tmp[:, :, TP:T], norm_tmp[:, :, TP:T], gain[:, :, 1:ROWS], ALU.mult))
            v.tensor_tensor(dst[:, :, TP:T], norm_tmp[:, :, TP:T], x[:, :, TP:T], ALU.add).then_inc(done, 1)

        with ExitStack() as mix:
            w_uv = sb("w_uv", [P, 2, NH * VD], stack=mix)
            w_ukt = sb("w_ukt", [NOPE, NH, KVL], stack=mix)
            gate_z = sb("gate_z", [P, KI, T], stack=mix)
            gate_a = sb("gate_a", [P, KD, T], stack=mix)
            gate_b = sb("gate_b", [P, KD, T], stack=mix)
            xc = sb("xc", [P, KC, T], stack=mix)
            dt = sb("dt", [SH, T], stack=mix)
            o_attn = sb("o_attn", [P, 4, T], stack=mix)
            att_in = ExitStack()
            q_a = sb("q_a", [P, 3, T], stack=att_in)
            kv_a = sb("kv_a", [P, 2, T], stack=att_in)
            kpe = sb("kpe", [P, 2, T], stack=att_in)

            with ExitStack() as ph:
                c = sb("c", [P, KD, ROWS], stack=ph)
                sc = sb("sc", [P, KD, 32], stack=ph)
                raw = sb("raw", [P, 3, 4, P], stack=ph)
                h = sb("h", [P, KD, T], stack=ph)
                xpad = sb("xpad", [P, KC, CW - 1 + TP], stack=ph)
                xs4 = sb("xs4", [P, KC, CW, TS], stack=ph)
                conv = sb("conv", [P, KC, T], stack=ph)
                conv_s = sb("conv_s", [P, KC, CW, TS], stack=ph)
                last3 = sb("last3", [P, KC, CW - 1], stack=ph)
                cond_ready, mod_sums, raw_ready, h_ready = (sem("cond_ready", ph), sem("mod_sums", ph), sem("raw_ready", ph),
                                                            sem("h_ready", ph))
                mod_turned = sem("mod_turned", ph)
                with nc.Block() as block:
                    @block.sync
                    def _(sp):
                        sp.dma_start(par[:, :], io["params"]).then_inc(small_in, 16)
                        sp.dma_start(con[:, :], io["consts"]).then_inc(small_in, 16)
                        sp.dma_start(c[:, :, :], io["c_t"]).then_inc(small_in, 16)
                        load_units(sp, 2)
                        sp.dma_start(x[:, :, :], io["x_t"]).then_inc(small_in, 16)
                        sp.dma_start(w_uv[:, :, :], io["w_uv"]).then_inc(small_in, 16)
                        sp.dma_start(w_ukt[:, :, :], io["w_ukt"]).then_inc(small_in, 16)
                        sp.dma_start(xs4[:, :, 0:CW - 1, :], io["state_conv"]).then_inc(small_in, 16)
                        load_units(sp, N_ADA + RING)

                    @block.scalar
                    def _(act):
                        act.wait_ge(small_in, 16 * 7)
                        act.wait_ge(cond_ready, 1)
                        act.activation(sc[:, :, 0:ROWS], c[:, :, :], ACT.Silu).then_inc(cond_ready, 1)
                        act_square(0, x[:, :, :], KD)
                        act_root(0, D, 7)

                    @block.tensor
                    def _(pe):
                        pe.wait_ge(small_in, 16 * 7)
                        pe.wait_ge(cond_ready, 2)
                        for u in range(N_ADA):
                            w = unit(u, "p (k g c) -> p k g c", k=KD, g=4, c=P)
                            wait_unit(pe, u)
                            for k in range(KD):
                                for g in range(4):
                                    mm = pe.matmul(bank[32 * g:32 * g + 32, u // 4, (u % 4) * P:(u % 4 + 1) * P], sc[:, k, :],
                                                   w[:, k, g, :], start=(k == 0), stop=(k == KD - 1))
                            mm.then_inc(unit_used, 1)
                            if u == 1:
                                pe_norm(0, KD, 7)
                        for q in range(3):
                            pe.wait_ge(raw_ready, q + 1)
                            for i in range(4):
                                mm = pe.transpose(bank[:, 4 + q, i * P:(i + 1) * P], raw[:, q, i, :], ident)
                            mm.then_inc(mod_turned, 1)

                    @block.vector
                    def _(dve):
                        dve.wait_ge(small_in, 16 * 7)
                        dve.memset(xpad[:, :, 0:CW - 1], 0.0)
                        dve.memset(sc[:, :, :], 0.0).then_inc(cond_ready, 1)
                        dve_rstd(0)
                        for q in range(3):
                            dve.wait_ge(unit_used, 4 * q + 4)
                            dve.tensor_copy(raw[:, q, :, :], bank[:, q, :].rearrange("p (i c) -> p i c", c=P)).then_inc(raw_ready, 1)
                        for q in range(3):
                            dve.wait_ge(mod_turned, q + 1)
                            ins = dve.tensor_tensor(mod[:, 16 * q:16 * q + 16, :],
                                                    bank[:, 4 + q, :].rearrange("p (t r) -> p t r", r=32)[:, :, 0:ROWS],
                                                    pcol("b_ada", 16 * q, 16).unsqueeze(2).to_broadcast([P, 16, ROWS]), ALU.add)
                        link(ins)
                        dve_modulate(x[:, :, :], h, pcol("g_pre_mix"), 0, 1, h_ready)

                tiles = ([("q_a", i) for i in range(3)] + [("kv_a", i) for i in range(2)] + [("kpe", i) for i in range(2)]
                         + [("dt", 0)] + [("xbc", i) for i in range(KC)] + [("z", i) for i in range(KI)]
                         + [("ga", i) for i in range(KD)] + [("gb", i) for i in range(KD)])
                NB = 6
                n_dve = 8 + KC
                win_done, dve_took, act_took = sem("win_done", ph), sem("dve_took", ph), sem("act_took", ph)
                conv_ready, xc_ready = sem("conv_ready", ph), sem("xc_ready", ph)
                tails_ready = sem("tails_ready", ph)
                with nc.Block() as block:
                    @block.sync
                    def _(sp):
                        load_units(sp, U_WIN + N_WIN + RING)

                    @block.tensor
                    def _(pe):
                        for t, (kind, i) in enumerate(tiles):
                            u, j = U_WIN + t // 4, t % 4
                            if j == 0:
                                wait_unit(pe, u)
                            if t >= NB:
                                if t - NB < n_dve:
                                    pe.wait_ge(dve_took, t - NB + 1)
                                else:
                                    pe.wait_ge(act_took, t - NB - n_dve + 1)
                            w = unit(u, "p (j k c) -> p j k c", j=4, k=KD, c=P)
                            m = SH if kind == "dt" else P
                            for k in range(KD):
                                mm = pe.matmul(bank[0:m, t % NB, 0:T], w[:, j, k, 0:m], h[:, k, :],
                                               start=(k == 0), stop=(k == KD - 1))
                            mm.then_inc(win_done, 1)
                            if j == 3:
                                pe.wait_ge(win_done, t + 1)
                                pe.sem_inc(unit_used, 1)

                    @block.vector
                    def _(dve):
                        for t, (kind, i) in enumerate(tiles[:n_dve]):
                            dve.wait_ge(win_done, t + 1)
                            src = bank[:, t % NB, 0:T]
                            if kind == "xbc":
                                dve.tensor_copy(xpad[:, i, CW - 1:], src[:, 0:TP])
                                ins = dve.tensor_copy(xs4[:, i, CW - 1, :], src[:, TP:T])
                            elif kind == "dt":
                                ins = dve.tensor_copy(dt[:, :], src[0:SH, :])
                            else:
                                ins = dve.tensor_copy({"q_a": q_a, "kv_a": kv_a, "kpe": kpe}[kind][:, i, :], src)
                            ins.then_inc(dve_took, 1)
                        dve.wait_ge(dve_took, n_dve)
                        dve.tensor_copy(last3[:, :, :], xpad[:, :, TP:TP + CW - 1]).then_inc(tails_ready, 1)
                        for i in range(KC):
                            link(dve.tensor_scalar(conv[:, i, 0:TP], xpad[:, i, 0:TP], pcol("conv_w", i * CW, 1),
                                                   pcol("conv_b", i, 1), ALU.mult, ALU.add))
                            for w in range(1, CW):
                                link(dve.scalar_tensor_tensor(conv[:, i, 0:TP], xpad[:, i, w:w + TP],
                                                              pcol("conv_w", i * CW + w, 1), conv[:, i, 0:TP],
                                                              ALU.mult, ALU.add))
                        wc = pcol("conv_w").rearrange("p (i w) -> p i w", w=CW)
                        for w in range(1, CW):
                            dve.tensor_tensor(conv_s[:, :, w, :], xs4[:, :, w, :],
                                              wc[:, :, w:w + 1].to_broadcast([P, KC, TS]), ALU.mult)
                        link(dve.tensor_tensor(conv[:, :, TP:T], xs4[:, :, 0, :],
                                               wc[:, :, 0:1].to_broadcast([P, KC, TS]), ALU.mult))
                        for w in range(1, CW):
                            link(dve.tensor_tensor(conv[:, :, TP:T], conv[:, :, TP:T], conv_s[:, :, w, :], ALU.add))
                        dve.tensor_tensor(conv[:, :, TP:T], conv[:, :, TP:T],
                                          pcol("conv_b").unsqueeze(2).to_broadcast([P, KC, TS]),
                                          ALU.add).then_inc(conv_ready, 1)

                    @block.scalar
                    def _(act):
                        act.wait_ge(tails_ready, 1)
                        store(act, io["conv_p"], last3[:, :, :])
                        store(act, io["conv_s"], xs4[:, :, 1:CW, :])
                        for t, (kind, i) in enumerate(tiles[n_dve:]):
                            act.wait_ge(win_done, n_dve + t + 1)
                            dst = {"z": gate_z, "ga": gate_a, "gb": gate_b}[kind]
                            act.activation(dst[:, i, :], bank[:, (n_dve + t) % NB, 0:T],
                                           ACT.Silu if kind == "z" else ACT.Sigmoid).then_inc(act_took, 1)
                        act.wait_ge(conv_ready, 1)
                        act.activation(xc[:, :, :], conv[:, :, :], ACT.Silu).then_inc(xc_ready, 1)
                        act.wait_ge(stored, n_stored[0])

            with att_in:
                qh = sb("qh", [QH, NH, T], stack=att_in)
                ckv = sb("ckv", [P, 2, T], stack=att_in)
                kr = sb("kr", [P, T], stack=att_in)
                q_lat = sb("q_lat", [P, 2, TS, NH], stack=att_in)
                q_rot = sb("q_rot", [QH, TS, NH], stack=att_in)
                ckv_row = sb("ckv_row", [1, TS, KVL], stack=att_in)
                own = ExitStack()
                kh = sb("kh", [QH, NH, TP], stack=own)
                val = sb("val", [P, 2, NH * VD], stack=own)
                with ExitStack() as ph:
                    qn = sb("qn", [P, 3, T], stack=ph)
                    t1 = sb("t1", [P, T], stack=ph)
                    t2 = sb("t2", [P, 2, T], stack=ph)
                    qn_ready, ckv_ready, kr_ready = sem("qn_ready", ph), sem("ckv_ready", ph), sem("kr_ready", ph)
                    q_done, q_took, q_nope_took = sem("q_done", ph), sem("q_took", ph), sem("q_nope_took", ph)
                    k_done, k_took = sem("k_done", ph), sem("k_took", ph)
                    v_done, lat_done, row_done, tail_took = (sem("v_done", ph), sem("lat_done", ph),
                                                             sem("row_done", ph), sem("tail_took", ph))
                    cos, sin = ccol("cos"), ccol("sin")
                    with nc.Block() as block:
                        @block.sync
                        def _(sp):
                            sp.wait_ge(ckv_ready, 1)
                            store(sp, io["ckv"], ckv[:, :, :])
                            sp.wait_ge(kr_ready, 1)
                            store(sp, io["kpe"], kr[0:ROPE, :])
                            load_units(sp, U_QB + 1 + RING)

                        @block.scalar
                        def _(act):
                            act_square(1, q_a[:, :, :], 3)
                            act_root(1, QL, 0)
                            act_square(2, kv_a[:, :, :], 2)
                            act_root(2, KVL, 1)
                            for hd in range(NH):
                                act.wait_ge(q_done, hd + 1)
                                act.copy(qh[0:NOPE, hd, :], bank[0:NOPE, 2 * (hd % 3), 0:T]).then_inc(q_nope_took, 1)
                            for hd in range(NH):
                                act.wait_ge(k_done, hd + 1)
                                act.copy(kh[0:NOPE, hd, :], bank[0:NOPE, 6 + hd % 2, 0:TP]).then_inc(k_took, 1)

                        @block.tensor
                        def _(pe):
                            wq = unit(U_QB, "p (k s h c) -> p k s h c", k=3, s=1, h=NH, c=P)
                            wk = ring[:, U_QB % RING, 3 * NH * P:].rearrange("p (k c) -> p k c", k=2)
                            pe_norm(1, 3, 0)
                            pe_norm(2, 2, 1)
                            wait_unit(pe, U_QB)
                            pe.wait_ge(qn_ready, 1)
                            pe.wait_ge(rstd_ready, 3)
                            for hd in range(NH):
                                if hd >= 3:
                                    pe.wait_ge(q_took, hd - 2)
                                    pe.wait_ge(q_nope_took, hd - 2)
                                for k in range(3):
                                    pe.matmul(bank[0:QH, 2 * (hd % 3), 0:T], wq[:, k, 0, hd, 0:QH], qn[:, k, :],
                                              start=(k == 0), stop=(k == 2))
                                for k in range(3):
                                    mm = pe.matmul(bank[NOPE:QH, 2 * (hd % 3) + 1, 0:T], wq[:, k, 0, hd, QH:P],
                                                   qn[:, k, :], start=(k == 0), stop=(k == 2))
                                mm.then_inc(q_done, 1)
                            pe.wait_ge(ckv_ready, 1)
                            for hd in range(NH):
                                if hd >= 2:
                                    pe.wait_ge(k_took, hd - 1)
                                for k in range(2):
                                    mm = pe.matmul(bank[0:NOPE, 6 + hd % 2, 0:TP], wk[:, k, hd * NOPE:(hd + 1) * NOPE],
                                                   ckv[:, k, 0:TP], start=(k == 0), stop=(k == 1))
                                mm.then_inc(k_done, 1)
                            pe.wait_ge(k_done, NH)
                            pe.sem_inc(unit_used, 1)
                            pe.wait_ge(q_took, NH)
                            pe.wait_ge(q_nope_took, NH)
                            for tt in range(2):
                                for k in range(2):
                                    mm = pe.matmul(bank[:, tt, :], ckv[:, k, tt * P:(tt + 1) * P], w_uv[:, k, :],
                                                   start=(k == 0), stop=(k == 1))
                            mm.then_inc(v_done, 1)
                            for ct in range(2):
                                for hd in range(NH):
                                    at = (ct * NH + hd) * TS
                                    mm = pe.matmul(bank[:, 2, at:at + TS], w_ukt[:, hd, ct * P:(ct + 1) * P],
                                                   qh[0:NOPE, hd, TP:T], start=True, stop=True)
                            mm.then_inc(lat_done, 1)
                            pe.wait_ge(k_took, NH)
                            for b in range(TS):
                                for ct in range(2):
                                    at = (b * 2 + ct) * P
                                    mm = pe.matmul(bank[0:1, 3 + at // 512, at % 512:at % 512 + P],
                                                   ckv[:, ct, TP + b:TP + b + 1], ident, start=True, stop=True)
                            mm.then_inc(row_done, 1)

                        @block.vector
                        def _(dve):
                            dve_rstd(1)
                            for k in range(3):
                                ins = dve.scalar_tensor_tensor(qn[:, k, :], q_a[:, k, :], pcol("g_q_a", k, 1), rstd[:, :],
                                                               ALU.mult, ALU.mult)
                            ins.then_inc(qn_ready, 1)
                            dve.wait_ge(qn_ready, 1)
                            dve_rstd(2)
                            for k in range(2):
                                ins = dve.scalar_tensor_tensor(ckv[:, k, :], kv_a[:, k, :], pcol("g_kv_a", k, 1),
                                                               rstd[:, :], ALU.mult, ALU.mult)
                            ins.then_inc(ckv_ready, 1)
                            dve.tensor_tensor(t2[:, 0, :], kpe[:, 0, :], cos, ALU.mult)
                            link(dve.tensor_tensor(t2[:, 1, :], kpe[:, 1, :], sin, ALU.mult))
                            link(dve.tensor_tensor(kr[:, :], t2[:, 0, :], t2[:, 1, :], ALU.add))
                            dve.sem_inc(kr_ready, 1)
                            dve.tensor_copy(kh[NOPE:QH, :, :], kr[NOPE:QH, 0:TP].unsqueeze(1).to_broadcast([ROPE, NH, TP]))
                            dve.memset(q_rot[0:NOPE, :, :], 0.0)
                            for hd in range(NH):
                                dve.wait_ge(q_done, hd + 1)
                                dve.tensor_tensor(t2[NOPE:QH, 0, :], bank[NOPE:QH, 2 * (hd % 3), 0:T], cos[NOPE:QH, :], ALU.mult)
                                link(dve.tensor_tensor(t2[NOPE:QH, 1, :], bank[NOPE:QH, 2 * (hd % 3) + 1, 0:T],
                                                       sin[NOPE:QH, :], ALU.mult))
                                ins = dve.tensor_tensor(qh[NOPE:QH, hd, :], t2[NOPE:QH, 0, :], t2[NOPE:QH, 1, :], ALU.add)
                                ins.then_inc(q_took, 1)
                                dve.wait_ge(q_took, hd + 1)
                            dve.tensor_copy(q_rot[NOPE:QH, :, :], qh[NOPE:QH, :, TP:T].rearrange("p h b -> p b h"))
                            dve.wait_ge(v_done, 1)
                            dve.tensor_copy(val[:, :, :], bank[:, 0:2, :])
                            dve.wait_ge(lat_done, 1)
                            dve.tensor_copy(q_lat[:, :, :, :].rearrange("p c b h -> p c h b"),
                                            bank[:, 2, 0:2 * NH * TS].rearrange("p (c h b) -> p c h b", c=2, h=NH))
                            dve.wait_ge(row_done, 1)
                            link(dve.tensor_copy(ckv_row[:, :, :].rearrange("p b c -> p (b c)"),
                                                 bank[0:1, 3:7, :].rearrange("p a b -> p (a b)")))

                with ExitStack() as ph:
                    s = sb("s", [P, NH, 3 * P], stack=ph)
                    pt = sb("pt", [P, NH, 3 * P], stack=ph)
                    mx = sb("mx", [P, 2, NH], stack=ph)
                    sm = sb("sm", [P, 2, NH], stack=ph)
                    s_done, s_shifted, exp_done, prob_ready = (sem("s_done", ph), sem("s_shifted", ph),
                                                               sem("exp_done", ph), sem("prob_ready", ph))
                    pt_done, pt_took, o_done = sem("pt_done", ph), sem("pt_took", ph), sem("o_done", ph)
                    mask = ccol("mask").unsqueeze(1).to_broadcast([P, NH, P])
                    with nc.Block() as block:
                        @block.tensor
                        def _(pe):
                            for hd in range(NH):
                                pe.matmul(bank[:, hd // 4, (hd % 4) * P:(hd % 4 + 1) * P], qh[:, hd, 0:P], kh[:, hd, 0:P],
                                          start=True, stop=True)
                                mm = pe.matmul(bank[:, 2 + hd // 2, (hd % 2) * TP:(hd % 2 + 1) * TP],
                                               qh[:, hd, P:TP], kh[:, hd, :], start=True, stop=True)
                            mm.then_inc(s_done, 1)
                            pe.wait_ge(s_shifted, 1)
                            pe.wait_ge(prob_ready, 1)
                            for hd in range(NH):
                                if hd >= 4:
                                    pe.wait_ge(pt_took, hd - 3)
                                for i in range(3):
                                    mm = pe.transpose(bank[:, hd % 4, i * P:(i + 1) * P], s[:, hd, i * P:(i + 1) * P], ident)
                                mm.then_inc(pt_done, 1)
                            for hd in range(NH):
                                pe.wait_ge(pt_took, hd + 1)
                                lo = (hd % 2) * VD
                                out = bank[lo:lo + VD, 4 + hd // 2, 0:TP]
                                v = [val[:, tt, hd * VD:(hd + 1) * VD] for tt in range(2)]
                                pe.matmul(out[:, 0:P], v[0], pt[:, hd, 0:P], start=True, stop=True)
                                pe.matmul(out[:, P:TP], v[0], pt[:, hd, P:2 * P], start=True, stop=False)
                                mm = pe.matmul(out[:, P:TP], v[1], pt[:, hd, 2 * P:], start=False, stop=True)
                            mm.then_inc(o_done, 1)

                        @block.vector
                        def _(dve):
                            dve.wait_ge(s_done, 1)
                            b0 = bank[:, 0:2, :].rearrange("p b (h k) -> p (b h) k", k=P)
                            b1 = bank[:, 2:6, :].rearrange("p b (h k) -> p (b h) k", k=TP)
                            dve.scalar_tensor_tensor(s[:, :, 0:P], b0, SCALE, mask, ALU.mult, ALU.add)
                            dve.tensor_scalar(s[:, :, P:2 * P], b1[:, :, 0:P], SCALE, None, ALU.mult)
                            link(dve.scalar_tensor_tensor(s[:, :, 2 * P:], b1[:, :, P:], SCALE, mask, ALU.mult, ALU.add))
                            dve.tensor_reduce(mx[:, 0, :], s[:, :, 0:P], AX.X, ALU.max)
                            link(dve.tensor_reduce(mx[:, 1, :], s[:, :, P:], AX.X, ALU.max))
                            dve.tensor_tensor(s[:, :, 0:P], s[:, :, 0:P], mx[:, 0, :].unsqueeze(2).to_broadcast([P, NH, P]),
                                              ALU.subtract)
                            dve.tensor_tensor(s[:, :, P:], s[:, :, P:], mx[:, 1, :].unsqueeze(2).to_broadcast([P, NH, TP]),
                                              ALU.subtract).then_inc(s_shifted, 1)
                            dve.wait_ge(exp_done, 1)
                            dve.tensor_reduce(sm[:, 0, :], s[:, :, 0:P], AX.X, ALU.add)
                            link(dve.tensor_reduce(sm[:, 1, :], s[:, :, P:], AX.X, ALU.add))
                            link(dve.reciprocal(sm[:, :, :], sm[:, :, :]))
                            dve.tensor_tensor(s[:, :, 0:P], s[:, :, 0:P], sm[:, 0, :].unsqueeze(2).to_broadcast([P, NH, P]),
                                              ALU.mult)
                            dve.tensor_tensor(s[:, :, P:], s[:, :, P:], sm[:, 1, :].unsqueeze(2).to_broadcast([P, NH, TP]),
                                              ALU.mult).then_inc(prob_ready, 1)
                            dve.wait_ge(o_done, 1)
                            dve.tensor_copy(o_attn[:, :, 0:TP], bank[:, 4:8, 0:TP])

                        @block.scalar
                        def _(act):
                            act.wait_ge(s_shifted, 1)
                            act.activation(s[:, :, :], s[:, :, :], ACT.Exp).then_inc(exp_done, 1)
                            for hd in range(NH):
                                act.wait_ge(pt_done, hd + 1)
                                act.copy(pt[:, hd, :], bank[:, hd % 4, 0:3 * P]).then_inc(pt_took, 1)

                own.close()

                with ExitStack() as ph:
                    page = [sb(f"page{i}", [P, NPG, PW], stack=ph) for i in range(2)]
                    NPT = 4
                    page_t = sb("page_t", [P, NPT, 3, P], stack=ph)
                    ptab = sb("ptab", [1, TS * NPG], I32, stack=ph)
                    NK = (NPG + 1) * NH
                    sc5 = [sb(f"sc5_{i}", [P, NPG + 1, NH], stack=ph) for i in range(2)]
                    mx5 = sb("mx5", [P, NH], stack=ph)
                    gm5 = sb("gm5", [NH, 1], stack=ph)
                    dg5 = sb("dg5", [NH, NH], stack=ph)
                    rs5 = sb("rs5", [P, NH], stack=ph)
                    rd5 = sb("rd5", [P, NH], stack=ph)
                    lat = sb("lat", [P, 2, NH, TS], stack=ph)
                    page_in = [sem(f"page_in{i}", ph) for i in range(2)]
                    ptab_in, turned, turn_took, s_done5 = sem("ptab_in", ph), sem("turned", ph), sem("turn_took", ph), sem("s_done5", ph)
                    mx_ready, mxt_done, dg_ready, mxb_done = sem("mx_ready", ph), sem("mxt_done", ph), sem("dg_ready", ph), sem("mxb_done", ph)
                    shifted5, exp5, rs_ready, den5, probs5, lat_done, lat_took = (
                        sem("shifted5", ph), sem("exp5", ph), sem("rs_ready", ph), sem("den5", ph), sem("probs5", ph),
                        sem("lat_done5", ph), sem("lat_took", ph))
                    o5 = sem("o5", ph)
                    with nc.Block() as block:
                        @block.sync
                        def _(sp):
                            sp.dma_start(ptab[:, :], io["page_table"]).then_inc(ptab_in, 16)
                            sp.wait_ge(ptab_in, 16)

                            def load_pages(b, half):
                                for j in range(NPG):
                                    r = sp.value_load(ptab[0:1, bass.ds(b * NPG + j, 1)], min_val=0, max_val=POOL - 1)
                                    sp.dma_start(page[half][:, j, :],
                                                 io["cache"][bass.ds(r, 1)].rearrange("a p c -> (a p) c")
                                                 ).then_inc(page_in[half], 16)
                            load_pages(0, 0)
                            load_pages(1, 1)
                            with sp.Fori(1, TS // 2) as i:
                                for half in range(2):
                                    sp.wait_ge(lat_done, 2 * i + half - 1)
                                    load_pages(2 * i + half, half)
                            load_units(sp, U_QB + 1 + RING)

                        @block.tensor
                        def _(pe):
                            for b in range(TS):
                                half = b % 2
                                pe.wait_ge(page_in[half], 16 * NPG * (b // 2 + 1))

                                def turn(j):
                                    n = b * NPG + j
                                    if n >= NPT:
                                        pe.wait_ge(turn_took, n - NPT + 1)
                                    for i, (lo, hi) in enumerate(((0, P), (P, 2 * P), (PW - QH, PW))):
                                        mm = pe.transpose(bank[0:hi - lo, j % NPT, i * P:(i + 1) * P],
                                                          page[half][:, j, lo:hi], ident)
                                    mm.then_inc(turned, 1)

                                def score(j):
                                    n = b * NPG + j
                                    pe.wait_ge(turn_took, n + 1)
                                    out = bank[:, 4, j * NH:(j + 1) * NH]
                                    for i in range(2):
                                        pe.matmul(out, page_t[:, n % NPT, i, :], q_lat[:, i, b, :], start=(i == 0), stop=False)
                                    return pe.matmul(out, page_t[0:QH, n % NPT, 2, :], q_rot[:, b, :], start=False, stop=True)
                                if b >= 1:
                                    pe.wait_ge(shifted5, b)
                                for j in range(NPG + 2):
                                    if j < NPG:
                                        turn(j)
                                    if j >= 2:
                                        score(j - 2)
                                out = bank[0:1, 4, NPG * NH:NK]
                                for i in range(2):
                                    pe.matmul(out, ckv[:, i, TP + b:TP + b + 1], q_lat[:, i, b, :], start=(i == 0), stop=False)
                                pe.matmul(out, kr[0:QH, TP + b:TP + b + 1], q_rot[:, b, :],
                                          start=False, stop=True).then_inc(s_done5, 1)
                                pe.wait_ge(mx_ready, b + 1)
                                pe.transpose(bank[0:NH, 5, 0:P], mx5[:, :], ident).then_inc(mxt_done, 1)
                                pe.wait_ge(dg_ready, b + 1)
                                pe.matmul(bank[:, 5, P:P + NH], ones[0:NH, :], dg5[:, :], start=True, stop=True).then_inc(mxb_done, 1)
                                pe.wait_ge(rs_ready, b + 1)
                                pe.matmul(bank[:, 5, 2 * P:2 * P + NH], ones, rs5[:, :], start=True, stop=True).then_inc(den5, 1)
                                pe.wait_ge(probs5, b + 1)
                                for ct in range(2):
                                    out = bank[:, 6, ct * NH:(ct + 1) * NH]
                                    if b >= 1 and ct == 0:
                                        pe.wait_ge(lat_took, b)
                                    for j in range(NPG):
                                        pe.matmul(out, page[half][:, j, ct * P:(ct + 1) * P], sc5[half][:, j, :],
                                                  start=(j == 0), stop=False)
                                    mm = pe.matmul(out, ckv_row[0:1, b, ct * P:(ct + 1) * P], sc5[half][0:1, NPG, :],
                                                   start=False, stop=True)
                                mm.then_inc(lat_done, 1)
                            pe.wait_ge(lat_took, TS)
                            for hd in range(NH):
                                lo = (hd % 2) * VD
                                for ct in range(2):
                                    mm = pe.matmul(bank[lo:lo + VD, 7, (hd // 2) * TS:(hd // 2 + 1) * TS],
                                                   w_uv[:, ct, hd * VD:(hd + 1) * VD], lat[:, ct, hd, :],
                                                   start=(ct == 0), stop=(ct == 1))
                            mm.then_inc(o5, 1)

                        @block.scalar
                        def _(act):
                            for b in range(TS):
                                for j in range(NPG):
                                    n = b * NPG + j
                                    act.wait_ge(turned, n + 1)
                                    act.copy(page_t[:, n % NPT, 0:2, :], bank[:, j % NPT, 0:2 * P].rearrange("p (a c) -> p a c", a=2))
                                    act.copy(page_t[0:QH, n % NPT, 2, :], bank[0:QH, j % NPT, 2 * P:3 * P]).then_inc(turn_took, 1)
                                act.wait_ge(shifted5, b + 1)
                                act.activation(sc5[b % 2][:, :, :], sc5[b % 2][:, :, :], ACT.Exp).then_inc(exp5, 1)

                        @block.vector
                        def _(dve):
                            for b in range(TS):
                                half = b % 2
                                s5 = sc5[half]
                                dve.wait_ge(s_done5, b + 1)
                                if b >= 2:
                                    dve.wait_ge(lat_done, b - 1)
                                link(dve.memset(s5[:, NPG, :], -BIG))
                                dve.tensor_scalar(s5[:, 0:NPG, :], bank[:, 4, 0:NPG * NH].rearrange("p (j h) -> p j h", h=NH),
                                                  SCALE, None, ALU.mult)
                                link(dve.tensor_scalar(s5[0:1, NPG, :], bank[0:1, 4, NPG * NH:NK], SCALE, None, ALU.mult))
                                dve.tensor_reduce(mx5[:, :], s5[:, :, :].rearrange("p j h -> p h j"), AX.X, ALU.max).then_inc(mx_ready, 1)
                                dve.wait_ge(mxt_done, b + 1)
                                link(dve.tensor_reduce(gm5[:, :], bank[0:NH, 5, 0:P], AX.X, ALU.max))
                                dve.tensor_scalar(dg5[:, :], ident[0:NH, 0:NH], gm5[:, 0:1], None, ALU.mult).then_inc(dg_ready, 1)
                                dve.wait_ge(mxb_done, b + 1)
                                dve.tensor_tensor(s5[:, :, :], s5[:, :, :],
                                                  bank[:, 5, P:P + NH].unsqueeze(1).to_broadcast([P, NPG + 1, NH]),
                                                  ALU.subtract).then_inc(shifted5, 1)
                                dve.wait_ge(exp5, b + 1)
                                dve.tensor_reduce(rs5[:, :], s5[:, :, :].rearrange("p j h -> p h j"), AX.X, ALU.add).then_inc(rs_ready, 1)
                                dve.wait_ge(den5, b + 1)
                                link(dve.reciprocal(rd5[:, :], bank[:, 5, 2 * P:2 * P + NH]))
                                dve.tensor_tensor(s5[:, :, :], s5[:, :, :], rd5[:, :].unsqueeze(1).to_broadcast([P, NPG + 1, NH]),
                                                  ALU.mult).then_inc(probs5, 1)
                                dve.wait_ge(lat_done, b + 1)
                                dve.tensor_copy(lat[:, :, :, b], bank[:, 6, 0:2 * NH].rearrange("p (c h) -> p c h", c=2)).then_inc(lat_took, 1)
                            dve.wait_ge(o5, 1)
                            link(dve.tensor_copy(o_attn[:, :, TP:T], bank[:, 7, 0:4 * TS].rearrange("p (a b) -> p a b", a=4)))

                        @block.gpsimd
                        def _(pool):
                            pool.wait_ge(stored, n_stored[0])

            o_ssd = sb("o_ssd", [P, KI, T], stack=mix)
            with ExitStack() as ph:
                NC = TP // CH
                ea = sb("ea", [P, SH, TS], stack=ph)
                HG = SH // SG
                xdt_s = sb("xdt_s", [TS, DI], stack=ph)
                bm = sb("bm", [TS, TS, SG, NS], stack=ph)
                sel_in, st_in = sem("sel_in", ph), sem("st_in", ph)
                abs_ready, exp6, a_ready = sem("abs_ready", ph), sem("exp6", ph), sem("a_ready", ph)
                tm_done, tm_took, ea_done, ea_took = sem("tm_done", ph), sem("tm_took", ph), sem("ea_done", ph), sem("ea_took", ph)
                x_done, x_took, b_done, b_took = sem("x_done", ph), sem("x_took", ph), sem("b_done", ph), sem("b_took", ph)
                g_done, g_took = sem("g_done", ph), sem("g_took", ph)
                sx_done, sx_took, bm_ready = sem("sx_done", ph), sem("sx_took", ph), sem("bm_ready", ph)
                ac_done, last_ready, dec_ready = sem("ac_done", ph), sem("last_ready", ph), sem("dec_ready", ph)
                m_shifted, m_exp, m_ready, cs_exp, cs_ready = (sem("m_shifted", ph), sem("m_exp", ph), sem("m_ready", ph),
                                                               sem("cs_exp", ph), sem("cs_ready", ph))
                xdd_ready, st_done, h_ready6, y_done6, y_took = (sem("xdd_ready", ph), sem("st_done", ph), sem("h_ready6", ph),
                                                                 sem("y_done6", ph), sem("y_took", ph))
                outer_done, st_ready, st_scaled, ys_done = sem("outer_done", ph), sem("st_ready", ph), sem("st_scaled", ph), sem("ys_done", ph)
                with ExitStack() as pr:
                    sel = sb("sel", [SH, SH, P], stack=pr)
                    a = sb("a", [SH, T], stack=pr)
                    acum = sb("acum", [SH, TP], stack=pr)
                    w1 = sb("w1", [SH, T], stack=pr)
                    w2 = sb("w2", [SH, T], stack=pr)
                    w3 = sb("w3", [SH, T], stack=pr)
                    w4 = sb("w4", [SH, T], stack=pr)
                    nega = sb("nega", [SH, 1], stack=pr)
                    one_row = sb("one_row", [SH, TP], stack=pr)
                    tm = sb("tm", [P, 5, SH], stack=pr)
                    lastb = sb("lastb", [P, NC, SH], stack=pr)
                    dend = sb("dend", [P, NC, SH], stack=pr)
                    xdt = sb("xdt", [P, NC, SH, SP_], stack=pr)
                    b_tm = sb("b_tm", [P, SG, NC, NS], stack=pr)
                    h1 = sb("h1", [P, SH, SP_], stack=pr)
                    hf = sb("hf", [P, SH, SP_], stack=pr)
                    g_t = sb("g_t", [P, SG, NC, CH], stack=pr)
                    bs_tm = sb("bs_tm", [TS, SG, NS], stack=pr)
                    m = sb("m", [P, NC, HG, CH], stack=pr)
                    cs = sb("cs", [P, HG, CH], stack=pr)
                    xdd = sb("xdd", [P, NC, SH, SP_], stack=pr)
                    with nc.Block() as block:
                        @block.sync
                        def _(sp):
                            sp.dma_start(sel[:, :, :], io["sel"]).then_inc(sel_in, 16)
                            load_units(sp, U_OA + RING)
                            sp.wait_ge(h_ready6, 2)
                            store(sp, io["ssm_p"], hf[:, :, :])

                        @block.scalar
                        def _(act):
                            act.activation(nega[:, :], pcol("heads", 1, 1)[0:SH, :], ACT.Exp)
                            act.wait_ge(abs_ready, 1)
                            act.activation(w2[:, :], w1[:, :], ACT.Exp, scale=-1.0).then_inc(exp6, 1)
                            act.wait_ge(ea_done, 1)
                            act.activation(ea[:, :, :], bank[:, 1, 0:SH * TS].rearrange("p (h b) -> p h b", h=SH),
                                           ACT.Exp).then_inc(ea_took, 1)
                            act.wait_ge(b_done, 1)
                            act.copy(b_tm[:, :, :, :], bank[:, 6, :].rearrange("p (g c n) -> p g c n", g=SG, c=NC)).then_inc(b_took, 1)
                            for g in range(SG):
                                act.wait_ge(ac_done, g + 1)
                                act.wait_ge(last_ready, g + 1)
                                act.activation(lastb[:, :, g * HG:(g + 1) * HG], lastb[:, :, g * HG:(g + 1) * HG], ACT.Exp)
                                act.activation(dend[:, :, g * HG:(g + 1) * HG], dend[:, :, g * HG:(g + 1) * HG],
                                               ACT.Exp).then_inc(dec_ready, 1)
                                act.wait_ge(m_shifted, g + 1)
                                if g:
                                    act.wait_ge(y_done6, 1)
                                act.activation(cs[:, :, :], bank[:, 0:4, :].rearrange("p b (h l) -> p (b h) l", l=TP)[:, :, CH:],
                                               ACT.Exp).then_inc(cs_exp, 1)
                                act.activation(m[:, :, :, :], m[:, :, :, :], ACT.Exp).then_inc(m_exp, 1)

                        @block.tensor
                        def _(pe):
                            pe.wait_ge(sel_in, 16)
                            pe.wait_ge(a_ready, 1)
                            for i in range(NC):
                                pe.transpose(bank[:, 0, i * SH:(i + 1) * SH], dt[:, i * CH:(i + 1) * CH], ident[0:SH, 0:SH])
                            for i in range(NC):
                                pe.transpose(bank[:, 0, (2 + i) * SH:(3 + i) * SH], acum[:, i * CH:(i + 1) * CH], ident[0:SH, 0:SH])
                            pe.transpose(bank[0:TS, 0, 4 * SH:5 * SH], dt[:, TP:T], ident[0:SH, 0:SH]).then_inc(tm_done, 1)
                            for hd in range(SH):
                                mm = pe.matmul(bank[:, 1, hd * TS:(hd + 1) * TS], sel[:, hd, :], a[:, TP:T], start=True, stop=True)
                            mm.then_inc(ea_done, 1)
                            for i in range(NC):
                                for k in range(KI):
                                    at = (i * KI + k) * P
                                    mm = pe.transpose(bank[:, 2 + at // 512, at % 512:at % 512 + P],
                                                      xc[:, k, i * CH:(i + 1) * CH], ident)
                            mm.then_inc(x_done, 1)
                            for g in range(SG):
                                for i in range(NC):
                                    at = (g * NC + i) * NS
                                    mm = pe.transpose(bank[:, 6, at:at + NS], xc[:, KI + g, i * CH:(i + 1) * CH], ident)
                            mm.then_inc(b_done, 1)
                            for g in range(SG):
                                for i in range(NC):
                                    at = (g * NC + i) * CH
                                    mm = pe.matmul(bank[:, 7, at:at + CH], xc[:, KI + g, i * CH:(i + 1) * CH],
                                                   xc[:, KI + SG + g, i * CH:(i + 1) * CH], start=True, stop=True)
                            mm.then_inc(g_done, 1)
                            pe.wait_ge(ea_took, 1)
                            pe.wait_ge(b_took, 1)
                            pe.wait_ge(x_took, 1)
                            for k in range(KI):
                                pe.transpose(bank[0:TS, k // 4, (k % 4) * P:(k % 4 + 1) * P], xc[:, k, TP:T], ident)
                            for g in range(SG):
                                mm = pe.transpose(bank[0:TS, 6, g * NS:(g + 1) * NS], xc[:, KI + g, TP:T], ident)
                            mm.then_inc(sx_done, 1)
                            pe.wait_ge(sx_took, 1)
                            pe.wait_ge(g_took, 1)
                            for g in range(SG):
                                if g:
                                    pe.wait_ge(m_shifted, 1)
                                    pe.wait_ge(cs_exp, 1)
                                    pe.wait_ge(last_ready, 1)
                                for hd in range(HG):
                                    mm = pe.matmul(bank[:, hd // 2, (hd % 2) * TP:(hd % 2 + 1) * TP], sel[:, g * HG + hd, :],
                                                   acum[:, :], start=True, stop=True)
                                mm.then_inc(ac_done, 1)
                                pe.wait_ge(xdd_ready, g + 1)
                                if g:
                                    pe.wait_ge(h_ready6, 1)
                                    pe.wait_ge(y_took, 1)
                                for i in range(NC):
                                    mm = pe.matmul(bank[:, 4 + i, :], b_tm[:, g, i, :],
                                                   xdd[:, i, g * HG:(g + 1) * HG, :].rearrange("p h d -> p (h d)"),
                                                   start=True, stop=True)
                                mm.then_inc(st_done, 1)
                                pe.wait_ge(m_ready, g + 1)
                                pe.wait_ge(cs_ready, g + 1)
                                pe.wait_ge(h_ready6, g + 1)
                                for hd in range(HG):
                                    lo, hh = (hd % 2) * SP_, g * HG + hd
                                    at = (hd // 2) % 2 * TP
                                    out = bank[lo:lo + SP_, 6 + hd // 4, at:at + TP]
                                    pe.matmul(out[:, 0:CH], xdt[:, 0, hh, :], m[:, 0, hd, :], start=True, stop=True)
                                    pe.matmul(out[:, CH:], xdt[:, 1, hh, :], m[:, 1, hd, :], start=True, stop=False)
                                    mm = pe.matmul(out[:, CH:], h1[:, hh, :], cs[:, hd, :], start=False, stop=True)
                                mm.then_inc(y_done6, 1)

                        @block.vector
                        def _(dve):
                            link(dve.tensor_scalar(w4[:, :], dt[:, :], pcol("heads", 0, 1)[0:SH, :], None, ALU.add))
                            link(dve.tensor_scalar(w1[:, :], w4[:, :], -1.0, None, ALU.mult))
                            dve.tensor_tensor(w1[:, :], w1[:, :], w4[:, :], ALU.max).then_inc(abs_ready, 1)
                            dve.wait_ge(exp6, 1)
                            link(dve.tensor_scalar(w3[:, :], w2[:, :], 2.0, None, ALU.add))
                            link(dve.reciprocal(w3[:, :], w3[:, :]))
                            link(dve.tensor_tensor(w3[:, :], w3[:, :], w2[:, :], ALU.mult))
                            link(dve.tensor_tensor(w2[:, :], w3[:, :], w3[:, :], ALU.mult))
                            link(dve.memset(w1[:, :], 0.0))
                            for n in range(9, 0, -1):
                                link(dve.scalar_tensor_tensor(w1[:, :], w1[:, :], 1.0 / (2 * n + 1), w2[:, :], ALU.add, ALU.mult))
                            link(dve.scalar_tensor_tensor(w1[:, :], w1[:, :], 1.0, w3[:, :], ALU.add, ALU.mult))
                            link(dve.tensor_scalar(w4[:, :], w4[:, :], 0.0, None, ALU.max))
                            link(dve.scalar_tensor_tensor(dt[:, :], w1[:, :], 2.0, w4[:, :], ALU.mult, ALU.add))
                            dve.memset(one_row[:, :], 1.0)
                            link(dve.tensor_scalar(a[:, :], dt[:, :], nega[:, 0:1], -1.0, ALU.mult, ALU.mult))
                            for i in range(NC):
                                ins = dve.tensor_tensor_scan(acum[:, i * CH:(i + 1) * CH], one_row[:, 0:CH],
                                                             a[:, i * CH:(i + 1) * CH], 0.0, ALU.mult, ALU.add)
                            ins.then_inc(a_ready, 1)
                            dve.wait_ge(tm_done, 1)
                            dve.tensor_copy(tm[:, 0:4, :], bank[:, 0, 0:4 * SH].rearrange("p (a h) -> p a h", a=4))
                            link(dve.tensor_copy(tm[0:TS, 4, :], bank[0:TS, 0, 4 * SH:5 * SH]))
                            dve.wait_ge(x_done, 1)
                            dve.tensor_tensor(xdt[:, :, :, :].rearrange("p c h d -> p (c h) d"),
                                              bank[:, 2:6, :].rearrange("p b (h d) -> p (b h) d", d=SP_),
                                              tm[:, 0:NC, :].rearrange("p c h -> p (c h)").unsqueeze(2).to_broadcast([P, NC * SH, SP_]),
                                              ALU.mult).then_inc(x_took, 1)
                            dve.wait_ge(g_done, 1)
                            dve.tensor_tensor(g_t[:, :, :, :].rearrange("p g c l -> p (g c) l"),
                                              bank[:, 7, :].rearrange("p (a l) -> p a l", l=CH),
                                              ccol("causal_t").unsqueeze(1).to_broadcast([P, SG * NC, CH]),
                                              ALU.mult).then_inc(g_took, 1)
                            dve.wait_ge(sx_done, 1)
                            dve.tensor_tensor(xdt_s[:, :].rearrange("p (h d) -> p h d", d=SP_),
                                              bank[0:TS, 0:2, :].rearrange("p b (h d) -> p (b h) d", d=SP_),
                                              tm[0:TS, 4, :].unsqueeze(2).to_broadcast([TS, SH, SP_]), ALU.mult)
                            link(dve.tensor_copy(bs_tm[:, :, :], bank[0:TS, 6, 0:SG * NS].rearrange("p (g n) -> p g n", g=SG)))
                            dve.sem_inc(sx_took, 1)
                            dve.tensor_tensor(bm[:, :, :, :].rearrange("p b g n -> p b (g n)"),
                                              bs_tm[:, :, :].rearrange("p g n -> p (g n)").unsqueeze(1).to_broadcast([TS, TS, SG * NS]),
                                              ident[0:TS, 0:TS].unsqueeze(2).to_broadcast([TS, TS, SG * NS]),
                                              ALU.mult).then_inc(bm_ready, 1)
                            for g in range(SG):
                                hs = slice(g * HG, (g + 1) * HG)
                                ac = bank[:, 0:4, :].rearrange("p b (h l) -> p (b h) l", l=TP)
                                dve.wait_ge(ac_done, g + 1)
                                for i in range(NC):
                                    ins = dve.tensor_copy(lastb[:, i, hs], ac[:, :, (i + 1) * CH - 1])
                                link(ins)
                                dve.tensor_tensor(dend[:, :, hs], lastb[:, :, hs], tm[:, 2:4, hs], ALU.subtract).then_inc(last_ready, 1)
                                dve.wait_ge(last_ready, g + 1)
                                if g:
                                    dve.wait_ge(y_done6, 1)
                                for i in range(NC):
                                    for hd in range(HG):
                                        ins = dve.tensor_scalar(m[:, i, hd, :], ac[:, hd, i * CH:(i + 1) * CH],
                                                                tm[:, 2 + i, g * HG + hd:g * HG + hd + 1], 0.0,
                                                                ALU.subtract, ALU.min)
                                ins.then_inc(m_shifted, 1)
                                dve.wait_ge(dec_ready, g + 1)
                                dve.tensor_tensor(xdd[:, :, hs, :], xdt[:, :, hs, :],
                                                  dend[:, :, hs].unsqueeze(3).to_broadcast([P, NC, HG, SP_]),
                                                  ALU.mult).then_inc(xdd_ready, 1)
                                dve.wait_ge(cs_exp, g + 1)
                                dve.tensor_tensor(cs[:, :, :], cs[:, :, :],
                                                  xc[:, KI + SG + g, CH:TP].unsqueeze(1).to_broadcast([P, HG, CH]),
                                                  ALU.mult).then_inc(cs_ready, 1)
                                dve.wait_ge(m_exp, g + 1)
                                dve.tensor_tensor(m[:, :, :, :], m[:, :, :, :],
                                                  g_t[:, g, :, :].unsqueeze(2).to_broadcast([P, NC, HG, CH]),
                                                  ALU.mult).then_inc(m_ready, 1)
                                dve.wait_ge(st_done, g + 1)
                                st = [bank[:, 4 + i, :].rearrange("p (h d) -> p h d", d=SP_) for i in range(NC)]
                                link(dve.tensor_copy(h1[:, hs, :], st[0]))
                                link(dve.tensor_tensor(hf[:, hs, :], h1[:, hs, :],
                                                       lastb[:, 1, hs].unsqueeze(2).to_broadcast([P, HG, SP_]), ALU.mult))
                                dve.tensor_tensor(hf[:, hs, :], hf[:, hs, :], st[1], ALU.add).then_inc(h_ready6, 1)
                                dve.wait_ge(y_done6, g + 1)
                                for j in range(4):
                                    k = g * 4 + j
                                    ins = dve.scalar_tensor_tensor(o_ssd[:, k, 0:TP], xc[:, k, 0:TP], pcol("d_skip", k, 1),
                                                                   bank[:, 6 + j // 2, (j % 2) * TP:(j % 2 + 1) * TP],
                                                                   ALU.mult, ALU.add)
                                ins.then_inc(y_took, 1)
                            dve.wait_ge(stored, n_stored[0])

                st = sb("st", [P, TS, SH, SP_], stack=ph)
                yt = sb("yt", [P, KI, TS], stack=ph)
                gated = sem("gated", ph)
                with nc.Block() as block:
                    @block.sync
                    def _(sp):
                        for b in range(TS):
                            sp.dma_start(st[:, b, :, :], io["state_ssm"][:, b]).then_inc(st_in, 16)
                        for b in range(TS):
                            sp.wait_ge(st_ready, b + 1)
                            store(sp, io["ssm_s"][:, b], st[:, b, :, :])

                    @block.tensor
                    def _(pe):
                        for b in range(TS):
                            if b >= 2:
                                pe.wait_ge(st_ready, b - 1)
                            for g in range(SG):
                                mm = pe.matmul(bank[:, (b % 2) * 2 + g, :], bm[:, b, g, :], xdt_s[:, g * 512:(g + 1) * 512],
                                               start=True, stop=True)
                            mm.then_inc(outer_done, 1)
                        for b in range(TS):
                            pe.wait_ge(st_ready, b + 1)
                            for k in range(KI):
                                mm = pe.matmul(bank[:, 4, k * TS + b:k * TS + b + 1],
                                               st[:, b, 2 * k:2 * k + 2, :].rearrange("p h d -> p (h d)"),
                                               xc[:, KI + SG + k // 4, TP + b:TP + b + 1], start=True, stop=True)
                        mm.then_inc(ys_done, 1)
                        for g in range(SG):
                            pe_norm(3 + g, 4, 5 + g)

                    @block.vector
                    def _(dve):
                        for b in range(TS):
                            dve.wait_ge(st_in, 16 * TS)
                            link(dve.tensor_tensor(st[:, b, :, :], st[:, b, :, :],
                                                   ea[:, :, b:b + 1].to_broadcast([P, SH, SP_]), ALU.mult))
                            dve.wait_ge(outer_done, b + 1)
                            dve.tensor_tensor(st[:, b, :, :], st[:, b, :, :],
                                              bank[:, (b % 2) * 2:(b % 2) * 2 + 2, :].rearrange("p a (h d) -> p (a h) d", d=SP_),
                                              ALU.add).then_inc(st_ready, 1)
                        link(dve.tensor_tensor(yt[:, :, :], xc[:, 0:KI, TP:T],
                                               pcol("d_skip").unsqueeze(2).to_broadcast([P, KI, TS]), ALU.mult))
                        dve.wait_ge(ys_done, 1)
                        link(dve.tensor_tensor(o_ssd[:, :, TP:T], yt[:, :, :],
                                               bank[:, 4, 0:KI * TS].rearrange("p (k b) -> p k b", b=TS), ALU.add))
                        dve.tensor_tensor(o_ssd[:, :, :], o_ssd[:, :, :], gate_z[:, :, :], ALU.mult).then_inc(gated, 1)
                        dve.wait_ge(gated, 1)
                        for g in range(SG):
                            dve_rstd(3 + g)
                            for k in range(4 * g, 4 * g + 4):
                                ins = dve.scalar_tensor_tensor(o_ssd[:, k, :], o_ssd[:, k, :], pcol("g_ssd", k, 1), rstd[:, :],
                                                               ALU.mult, ALU.mult)
                            link(ins)
                        dve.wait_ge(stored, n_stored[0])

                    @block.scalar
                    def _(act):
                        act.wait_ge(gated, 1)
                        for g in range(SG):
                            act_square(3 + g, o_ssd[:, 4 * g:4 * g + 4, :], 4)
                            act_root(3 + g, DI // SG, 5 + g)

            with ExitStack() as ph:
                merged = sb("merged", [P, KD, T], stack=ph)
                mtmp = sb("mtmp", [P, 2, T], stack=ph)
                mo = sb("mo", [P, KD, T], stack=ph)
                oo_done, merged_took, out_done, out_took, x1_ready = (sem("oo_done", ph), sem("merged_took", ph),
                                                                      sem("out_done", ph), sem("out_took", ph), sem("x1_ready", ph))
                mo_ready = sem("mo_ready", ph)
                with nc.Block() as block:
                    @block.gpsimd
                    def _(pool):
                        pool.sem_clear(range(cond_ready.num, o5.num + 1))

                    @block.sync
                    def _(sp):
                        load_units(sp, N_UNITS)

                    @block.tensor
                    def _(pe):
                        w_oa = unit(U_OA, "p (k c) -> p k c", k=4, c=D)
                        w_os = [unit(U_OS + i, "p (k c) -> p k c", k=4, c=D) for i in range(2)]
                        w_out = [unit(U_OUT + i, "p (j k c) -> p j k c", j=4, k=KD, c=P) for i in range(2)]
                        for u in (U_OA, U_OS, U_OS + 1):
                            wait_unit(pe, u)
                        for d in range(KD):
                            if d >= 3:
                                pe.wait_ge(merged_took, d - 2)
                            ba, bb = 2 * (d % 3), 2 * (d % 3) + 1
                            for k in range(4):
                                pe.matmul(bank[:, ba, 0:T], w_oa[:, k, d * P:(d + 1) * P], o_attn[:, k, :],
                                          start=(k == 0), stop=(k == 3))
                            for k in range(KI):
                                mm = pe.matmul(bank[:, bb, 0:T], w_os[k // 4][:, k % 4, d * P:(d + 1) * P], o_ssd[:, k, :],
                                               start=(k == 0), stop=(k == KI - 1))
                            mm.then_inc(oo_done, 1)
                        pe.wait_ge(oo_done, KD)
                        pe.sem_inc(unit_used, 3)
                        pe.wait_ge(merged_took, KD)
                        for d in range(KD):
                            if d % 4 == 0:
                                wait_unit(pe, U_OUT + d // 4)
                            if d >= 4:
                                pe.wait_ge(out_took, d - 3)
                            for k in range(KD):
                                mm = pe.matmul(bank[:, d % 4, 0:T], w_out[d // 4][:, d % 4, k, :], merged[:, k, :],
                                               start=(k == 0), stop=(k == KD - 1))
                            mm.then_inc(out_done, 1)
                        pe.wait_ge(out_done, KD)
                        pe.sem_inc(unit_used, 2)
                        pe_norm(5, KD, 4)

                    @block.vector
                    def _(dve):
                        for d in range(KD):
                            dve.wait_ge(oo_done, d + 1)
                            dve.tensor_tensor(mtmp[:, 0, :], gate_a[:, d, :], bank[:, 2 * (d % 3), 0:T], ALU.mult)
                            link(dve.tensor_tensor(mtmp[:, 1, :], gate_b[:, d, :], bank[:, 2 * (d % 3) + 1, 0:T], ALU.mult))
                            dve.tensor_tensor(merged[:, d, :], mtmp[:, 0, :], mtmp[:, 1, :], ALU.add).then_inc(merged_took, 1)
                            dve.wait_ge(merged_took, d + 1)
                        dve_rstd(5)
                        dve_residual(mo[:, :, :], x, pcol("g_post_mix"), 2, x1_ready)

                    @block.scalar
                    def _(act):
                        for d in range(KD):
                            act.wait_ge(out_done, d + 1)
                            act.copy(mo[:, d, :], bank[:, d % 4, 0:T]).then_inc(out_took, 1)
                        act.wait_ge(out_took, KD)
                        act_square(5, mo[:, :, :], KD)
                        act_root(5, D, 4)

        tok_rows = nc.dram_tensor("tok_rows", [T, D], F32, kind="Internal").ap()
        choice_rows = nc.dram_tensor("choice_rows", [T * TOPK, D], F32, kind="Internal").ap()
        lists = nc.dram_tensor("lists", [LB * NBLK, 2], I32, kind="Internal").ap()
        with ExitStack() as moe:
            w6 = sb("w6", [P, NT, TOPK], stack=moe)
            shared = sb("shared", [P, KD, T], stack=moe)
            tab = sb("tab", [LB, NBLK, 2], I32, stack=moe)
            over = sb("over", [1, 1], I32, stack=moe)
            behind = sb("behind", [1, NBLK - NE], stack=moe)
            behind_n = sb("behind_n", [1, NBLK - NE], stack=moe)
            one_r = sb("one_r", [1, NBLK - NE], stack=moe)
            gu_in = [sem(f"gu_in{i}", moe) for i in range(2)]
            dn_in = [sem(f"dn_in{i}", moe) for i in range(2)]
            gu_w = [ring[:, i, :].rearrange("p (k c) -> p k c", k=KD) for i in range(2)]
            dn_w = [ring[:, 2, i * 2048:(i + 1) * 2048].rearrange("p (k c) -> p k c", k=2) for i in range(2)]

            with ExitStack() as ph:
                h2 = sb("h2", [P, KD, T], stack=ph)
                rows = sb("rows", [P, NT, D], stack=ph)
                sg = sb("sg", [P, 2, T], stack=ph)
                hs = sb("hs", [P, 2, T], stack=ph)
                score = sb("score", [P, NT, NE], stack=ph)
                biased = sb("biased", [P, NT, NE], stack=ph)
                vals = sb("vals", [P, NT, TOPK, 2], I32, stack=ph)
                fill = sb("fill", [LB, NBLK, 2], I32, stack=ph)
                m8 = sb("m8", [P, NT, NG, 8], stack=ph)
                gs = sb("gs", [P, NT, NG], stack=ph)
                g8 = sb("g8", [P, NT, 8], stack=ph)
                ga1 = sb("ga1", [P, NT, NG], stack=ph)
                ga2 = sb("ga2", [P, NT, NG], stack=ph)
                ga3 = sb("ga3", [P, NT, NG], stack=ph)
                need = sb("need", [P, NT], stack=ph)
                one_c = sb("one_c", [P, NE], stack=ph)
                e1 = sb("e1", [P, NT, NE], stack=ph)
                e2 = sb("e2", [P, NT, NE], stack=ph)
                e3 = sb("e3", [P, NT, NE], stack=ph)
                chosen = sb("chosen", [P, NT, NE], stack=ph)
                rank = sb("rank", [P, NT, NE], stack=ph)
                pos = sb("pos", [P, NT, NE], stack=ph)
                wgt = sb("wgt", [P, NT, NE], stack=ph)
                ek = sb("ek", [P, NT, TOPK], stack=ph)
                pk = sb("pk", [P, NT, TOPK], stack=ph)
                ck = sb("ck", [P, NT, TOPK], stack=ph)
                addr = sb("addr", [P, NT, TOPK], I32, stack=ph)
                h2_ready, route_in, logits_done, scores_ready = (sem("h2_ready", ph), sem("route_in", ph),
                                                                 sem("logits_done", ph), sem("scores_ready", ph))
                rows_done, rows_took = sem("rows_done", ph), sem("rows_took", ph)
                rows_stored, lists_filled, lists_set, tab_in = (sem("rows_stored", ph), sem("lists_filled", ph),
                                                                sem("lists_set", ph), sem("tab_in", ph))
                sgu_done, sg_ready9, hs_ready, sdn_done = (sem("sgu_done", ph), sem("sg_ready9", ph), sem("hs_ready", ph),
                                                           sem("sdn_done", ph))
                shared_took = sem("shared_took", ph)
                chosen_ready, pos_done, addr_ready = sem("chosen_ready", ph), sem("pos_done", ph), sem("addr_ready", ph)
                with nc.Block() as block:
                    @block.sync
                    def _(sp):
                        sp.dma_start(vals[:, :, :, :], io["vals"]).then_inc(route_in, 16)
                        sp.dma_start(fill[:, :, :], io["fill"]).then_inc(route_in, 16)
                        sp.wait_ge(route_in, 32)
                        sp.dma_start(lists.rearrange("(p b) c -> p b c", p=LB), fill[:, :, :]).then_inc(lists_filled, 16)
                        sp.wait_ge(unit_used, N_UNITS - 1)
                        sp.dma_start(gu_w[1], io["w_gu"][1]).then_inc(gu_in[1], 16)
                        for i in range(2):
                            sp.dma_start(dn_w[i], io["w_dn"][i]).then_inc(dn_in[i], 16)
                        sp.wait_ge(unit_used, N_UNITS)
                        sp.dma_start(gu_w[0], io["w_gu"][0]).then_inc(gu_in[0], 16)
                        for j in range(NT):
                            sp.wait_ge(rows_took, j + 1)
                            n = TILE_ROWS[j]
                            sp.dma_start(tok_rows[j * P:j * P + n, :], rows[0:n, j, :]).then_inc(rows_stored, 16)
                        sp.wait_ge(rows_stored, 16 * NT)
                        sp.wait_ge(lists_set, 16 * NT * TOPK)
                        sp.dma_start(tab[:, :, :], lists.rearrange("(p b) c -> p b c", p=LB)).then_inc(tab_in, 16)
                        sp.wait_ge(tab_in, 16)

                    @block.scalar
                    def _(act):
                        act_square(6, x[:, :, :], KD)
                        act_root(6, D, 0)
                        act.wait_ge(logits_done, 1)
                        act.wait_ge(scores_ready, 1)
                        act.activation(score[:, 0:2, :], bank[:, 1, 0:2 * NE].rearrange("p (a e) -> p a e", a=2), ACT.Sigmoid)
                        act.activation(score[0:TS, 2, :], bank[0:TS, 1, 2 * NE:3 * NE], ACT.Sigmoid).then_inc(scores_ready, 1)
                        for i in range(2):
                            act.wait_ge(sgu_done, i + 1)
                            act.activation(sg[:, i, :], bank[:, 2 + i, 0:T], ACT.Silu).then_inc(sg_ready9, 1)
                        for j in range(NT):
                            n = TILE_ROWS[j]
                            act.wait_ge(rows_done, j + 1)
                            act.copy(rows[0:n, j, :], bank[0:n, 6:8, :].rearrange("p a b -> p (a b)")).then_inc(rows_took, 1)
                        for d in range(KD):
                            act.wait_ge(sdn_done, d + 1)
                            act.copy(shared[:, d, :], bank[:, 2 + d % 4, 0:T]).then_inc(shared_took, 1)

                    @block.tensor
                    def _(pe):
                        pe_norm(6, KD, 0)
                        pe.wait_ge(h2_ready, 1)
                        wr = ring[:, U_SDN % RING, 2 * D:2 * D + KD * NE].rearrange("p (k e) -> p k e", k=KD)
                        wd = ring[:, U_SDN % RING, 0:2 * D].rearrange("p (k c) -> p k c", k=2)
                        wait_unit(pe, U_SDN)
                        for j in range(NT):
                            n = TILE_ROWS[j]
                            for k in range(KD):
                                mm = pe.matmul(bank[0:n, 1, j * NE:(j + 1) * NE], h2[:, k, j * P:j * P + n], wr[:, k, :],
                                               start=(k == 0), stop=(k == KD - 1))
                        mm.then_inc(logits_done, 1)
                        w = unit(U_SGU, "p (j k c) -> p j k c", j=4, k=KD, c=P)
                        wait_unit(pe, U_SGU)
                        for i in range(2):
                            for half in range(2):
                                for k in range(KD):
                                    mm = pe.matmul(bank[:, 2 + i + 2 * half, 0:T], w[:, 2 * half + i, k, :], h2[:, k, :],
                                                   start=(k == 0), stop=(k == KD - 1))
                            mm.then_inc(sgu_done, 1)
                        pe.wait_ge(sgu_done, 2)
                        pe.sem_inc(unit_used, 1)
                        for j in range(NT):
                            n = TILE_ROWS[j]
                            if j:
                                pe.wait_ge(rows_took, j)
                            for k in range(KD):
                                mm = pe.transpose(bank[0:n, 6 + k // 4, (k % 4) * P:(k % 4 + 1) * P], h2[:, k, j * P:j * P + n], ident)
                            mm.then_inc(rows_done, 1)
                        pe.wait_ge(chosen_ready, 1)
                        before = ccol("before")
                        for j in range(NT):
                            for i in range(j):
                                pe.matmul(bank[:, 0, j * NE:(j + 1) * NE], ones, chosen[:, i, :], start=(i == 0), stop=False)
                            pe.matmul(bank[:, 0, j * NE:(j + 1) * NE], before, chosen[:, j, :], start=(j == 0), stop=True)
                        for i in range(NT):
                            mm = pe.matmul(bank[0:1, 0, NT * NE:(NT + 1) * NE], ones[:, 0:1], chosen[:, i, :],
                                           start=(i == 0), stop=(i == NT - 1))
                        mm.then_inc(pos_done, 1)
                        pe.wait_ge(hs_ready, 2)
                        for d in range(KD):
                            if d >= 4:
                                pe.wait_ge(shared_took, d - 3)
                            for k in range(2):
                                mm = pe.matmul(bank[:, 2 + d % 4, 0:T], wd[:, k, d * P:(d + 1) * P], hs[:, k, :],
                                               start=(k == 0), stop=(k == 1))
                            mm.then_inc(sdn_done, 1)
                        pe.wait_ge(sdn_done, KD)
                        pe.sem_inc(unit_used, 1)

                    @block.vector
                    def _(dve):
                        dve.memset(score[:, :, :], 0.0).then_inc(scores_ready, 1)
                        dve.memset(one_c[:, :], 1.0)
                        dve_rstd(6)
                        dve_modulate(x[:, :, :], h2, pcol("g_pre_ffn"), 3, 4, h2_ready)
                        dve.wait_ge(scores_ready, 2)
                        link(dve.tensor_tensor(biased[:, :, :], score[:, :, :],
                                               pcol("b_router").unsqueeze(1).to_broadcast([P, NT, NE]), ALU.add))
                        for j in range(NT):
                            for g in range(NG):
                                ins = dve.max(m8[:, j, g, :], biased[:, j, g * EPG:(g + 1) * EPG])
                        link(ins)
                        link(dve.tensor_tensor(gs[:, :, :], m8[:, :, :, 0], m8[:, :, :, 1], ALU.add))

                        def top(src, a1, a2, a3, n, k, dst):
                            for j in range(NT):
                                ins = dve.max(g8[:, j, :], src[:, j, :])
                            link(ins)
                            kth = g8[:, :, k - 1:k].to_broadcast([P, NT, n])
                            dve.tensor_tensor(a1[:, :, :], src[:, :, :], kth, ALU.is_gt)
                            link(dve.tensor_tensor(a2[:, :, :], src[:, :, :], kth, ALU.is_equal))
                            dve.tensor_reduce(need[:, :], a1[:, :, :], AX.X, ALU.add)
                            for j in range(NT):
                                ins = dve.tensor_tensor_scan(a3[:, j, :], one_c[:, 0:n], a2[:, j, :], 0.0, ALU.mult, ALU.add)
                            link(ins)
                            link(dve.tensor_tensor(a3[:, :, :], a3[:, :, :], need[:, :].unsqueeze(2).to_broadcast([P, NT, n]), ALU.add))
                            link(dve.scalar_tensor_tensor(a3[:, :, :], a3[:, :, :], float(k), a2[:, :, :], ALU.is_le, ALU.mult))
                            link(dve.tensor_tensor(dst[:, :, :], a1[:, :, :], a3[:, :, :], ALU.add))

                        top(gs, ga1, ga2, ga3, NG, TOPG, ga1)
                        link(dve.tensor_scalar(ga2[:, :, :], ga1[:, :, :], BIG, -BIG, ALU.mult, ALU.add))
                        for j in range(NT):
                            link(dve.tensor_tensor(e1[:, j, :].rearrange("p (g e) -> p g e", g=NG),
                                                   biased[:, j, :].rearrange("p (g e) -> p g e", g=NG),
                                                   ga1[:, j, :].unsqueeze(2).to_broadcast([P, NG, EPG]), ALU.mult))
                            ins = dve.tensor_tensor(biased[:, j, :].rearrange("p (g e) -> p g e", g=NG),
                                                    e1[:, j, :].rearrange("p (g e) -> p g e", g=NG),
                                                    ga2[:, j, :].unsqueeze(2).to_broadcast([P, NG, EPG]), ALU.add)
                        link(ins)
                        top(biased, e1, e2, e3, NE, TOPK, chosen)
                        valid = ccol("valid")
                        dve.tensor_tensor(chosen[:, :, :], chosen[:, :, :], valid.unsqueeze(2).to_broadcast([P, NT, NE]),
                                          ALU.mult).then_inc(chosen_ready, 1)
                        dve.wait_ge(chosen_ready, 1)
                        link(dve.tensor_tensor(wgt[:, :, :], chosen[:, :, :], score[:, :, :], ALU.mult))
                        link(dve.tensor_reduce(need[:, :], wgt[:, :, :], AX.X, ALU.add))
                        link(dve.tensor_tensor(need[:, :], need[:, :], valid, ALU.subtract))
                        link(dve.tensor_scalar(need[:, :], need[:, :], 1.0, None, ALU.add))
                        link(dve.reciprocal(need[:, :], need[:, :]))
                        dve.tensor_tensor(wgt[:, :, :], wgt[:, :, :], need[:, :].unsqueeze(2).to_broadcast([P, NT, NE]), ALU.mult)
                        for j in range(NT):
                            ins = dve.tensor_tensor_scan(rank[:, j, :], one_c[:, :], chosen[:, j, :], 0.0, ALU.mult, ALU.add)
                        link(ins)
                        dve.wait_ge(pos_done, 1)
                        link(dve.tensor_copy(pos[:, :, :], bank[:, 0, 0:NT * NE].rearrange("p (a e) -> p a e", a=NT)))
                        expert = ccol("expert").unsqueeze(1).to_broadcast([P, NT, NE])
                        for k in range(TOPK):
                            link(dve.scalar_tensor_tensor(e1[:, :, :], rank[:, :, :], float(k + 1), chosen[:, :, :],
                                                          ALU.is_equal, ALU.mult))
                            for src, dst in ((expert, ek), (pos[:, :, :], pk), (wgt[:, :, :], w6)):
                                link(dve.tensor_tensor(e2[:, :, :], e1[:, :, :], src, ALU.mult))
                                link(dve.tensor_reduce(dst[:, :, k], e2[:, :, :], AX.X, ALU.add))
                        link(dve.tensor_scalar(w6[:, :, :], w6[:, :, :], ROUTE, None, ALU.mult))
                        link(dve.tensor_scalar(ck[:, :, :], pk[:, :, :], float(LB), None, ALU.is_ge))
                        for r in range(2, ROUNDS):
                            link(dve.scalar_tensor_tensor(ck[:, :, :], pk[:, :, :], float(r * LB), ck[:, :, :], ALU.is_ge, ALU.add))
                        link(dve.scalar_tensor_tensor(ek[:, :, :], ck[:, :, :], float(NE - LB * NBLK), ek[:, :, :], ALU.mult, ALU.add))
                        link(dve.scalar_tensor_tensor(ek[:, :, :], pk[:, :, :], float(NBLK), ek[:, :, :], ALU.mult, ALU.add))
                        link(dve.tensor_scalar(need[:, :], valid, -float(SKIP), float(SKIP), ALU.mult, ALU.add))
                        dve.tensor_tensor(addr[:, :, :], ek[:, :, :], need[:, :].unsqueeze(2).to_broadcast([P, NT, TOPK]),
                                          ALU.add).then_inc(addr_ready, 1)
                        dve.memset(one_r[:, :], 1.0)
                        for r in range(1, ROUNDS):
                            ins = dve.tensor_scalar(behind[:, (r - 1) * NE:r * NE], bank[0:1, 0, NT * NE:(NT + 1) * NE],
                                                    float(r * LB), None, ALU.is_gt)
                        link(ins)
                        link(dve.tensor_tensor_scan(behind_n[:, :], one_r[:, :], behind[:, :], 0.0, ALU.mult, ALU.add))
                        link(dve.tensor_copy(over[:, :], behind_n[:, NBLK - NE - 1:]))
                        for i in range(2):
                            dve.wait_ge(sg_ready9, i + 1)
                            dve.tensor_tensor(hs[:, i, :], sg[:, i, :], bank[:, 4 + i, 0:T], ALU.mult).then_inc(hs_ready, 1)

                    @block.gpsimd
                    def _(pool):
                        pool.wait_ge(addr_ready, 1)
                        pool.wait_ge(route_in, 32)
                        pool.wait_ge(lists_filled, 16)
                        for j in range(NT):
                            n = TILE_ROWS[j]
                            for k in range(TOPK):
                                pool.indirect_dma_start(lists, bass.IndirectOffsetOnAxis(ap=addr[0:n, j, k:k + 1].bitcast(U32), axis=0),
                                                        vals[0:n, j, k, :], None, bounds_check=LB * NBLK - 1,
                                                        oob_is_err=False).then_inc(lists_set, 16)

            with ExitStack() as ph:
                xg = [sb(f"xg{i}", [LB, D], stack=ph) for i in range(2)]
                xt = [sb(f"xt{i}", [P, KD, LB], stack=ph) for i in range(2)]
                sg = [sb(f"sg{i}", [LB, FE], stack=ph) for i in range(2)]
                hh = [sb(f"hh{i}", [LB, FE], stack=ph) for i in range(2)]
                ht = [sb(f"ht{i}", [P, 2, LB], stack=ph) for i in range(2)]
                yo = [sb(f"yo{i}", [LB, D], stack=ph) for i in range(2)]
                gi = [sb(f"gi{i}", [LB, 1], I32, stack=ph) for i in range(2)]
                si = [sb(f"si{i}", [LB, 1], I32, stack=ph) for i in range(2)]
                x_in = [sem(f"x_in{i}", ph) for i in range(2)]
                y_out = [sem(f"y_out{i}", ph) for i in range(2)]
                clear, idx_ready = sem("clear", ph), sem("idx_ready", ph)
                xt_done, xt_ready, gu_done, sg_ready, hh_ready = (sem("xt_done", ph), sem("xt_ready", ph), sem("gu_done", ph),
                                                                  sem("sg_ready", ph), sem("hh_ready", ph))
                ht_done, ht_ready, y_done, y_ready = sem("ht_done", ph), sem("ht_ready", ph), sem("y_done", ph), sem("y_ready", ph)

                with nc.Block() as block:
                    @block.sync
                    def _(sp):
                        with sp.Fori(1, NE // 2) as i:
                            for half in range(2):
                                e = 2 * i + half
                                sp.wait_ge(gu_done, e - 1)
                                sp.dma_start(gu_w[half], io["w_gu"][bass.ds(e, 1)].rearrange("a p k c -> (a p) k c")
                                             ).then_inc(gu_in[half], 16)
                                sp.wait_ge(y_done, e - 1)
                                sp.dma_start(dn_w[half], io["w_dn"][bass.ds(e, 1)].rearrange("a p k c -> (a p) k c")
                                             ).then_inc(dn_in[half], 16)

                    @block.gpsimd
                    def _(pool):
                        for half in range(2):
                            pool.memset(xg[half][:, :], 0.0).then_inc(clear, 1)
                        pool.wait_ge(clear, 2)
                        def step(e, half, r, gathers, scatters, count):
                            n = count
                            if gathers:
                                if e >= 2:
                                    pool.wait_ge(xt_done, r - 1)
                                    pool.sem_inc(pool_order, 1)
                                pool.tensor_copy(gi[half][:, :], tab[:, bass.ds(r, 1), 0]).then_inc(idx_ready, 1)
                                n = n + 1
                                pool.wait_ge(idx_ready, n)
                                pool.sem_inc(pool_order, 1)
                                pool.indirect_dma_start(xg[half][:, :], None, tok_rows,
                                                        bass.IndirectOffsetOnAxis(ap=gi[half][:, :].bitcast(U32), axis=0),
                                                        bounds_check=T - 1, oob_is_err=False).then_inc(x_in[half], 16)
                            if scatters:
                                other = 1 - half
                                pool.wait_ge(y_ready, r - 2)
                                pool.sem_inc(pool_order, 1)
                                pool.tensor_copy(si[other][:, :], tab[:, bass.ds(r - 3, 1), 1]).then_inc(idx_ready, 1)
                                n = n + 1
                                pool.wait_ge(idx_ready, n)
                                pool.sem_inc(pool_order, 1)
                                pool.indirect_dma_start(choice_rows,
                                                        bass.IndirectOffsetOnAxis(ap=si[other][:, :].bitcast(U32), axis=0),
                                                        yo[other][:, :], None, bounds_check=T * TOPK - 1,
                                                        oob_is_err=False).then_inc(y_out[other], 16)
                            return n
                        n = 0
                        for e in range(4):
                            n = step(e, e % 2, e, True, e >= 3, n)
                        with pool.Fori(2, NE // 2) as i:
                            for half in range(2):
                                step(4, half, 2 * i + half, True, True, 4 * i + 2 * half - 3)
                        n = 2 * NE - 3
                        for e in range(NE, NE + 3):
                            n = step(e, e % 2, e, False, True, n)
                        for half in range(2):
                            pool.wait_ge(y_out[half], 16 * NE // 2)

                    @block.tensor
                    def _(pe):
                        def turn_rows(e1, half, i1):
                            pe.wait_ge(x_in[half], 16 * i1 + 16)
                            pe.sem_inc(pe_order, 1)
                            for k in range(KD):
                                mm = pe.transpose(bank[:, 2 + half, k * LB:(k + 1) * LB],
                                                  xg[half][:, k * P:(k + 1) * P], ident[0:LB, 0:LB])
                            mm.then_inc(xt_done, 1)

                        def outputs(half, e0, i0):
                            pe.wait_ge(ht_ready, e0 + 1)
                            pe.wait_ge(dn_in[half], 16 * i0 + 16)
                            for k in range(2):
                                for c in range(2):
                                    mm = pe.matmul(bank[c * LB:(c + 1) * LB, 6 + half, :], ht[half][:, k, :],
                                                   dn_w[half][:, k, c * 512:(c + 1) * 512], start=(k == 0), stop=(k == 1))
                            mm.then_inc(y_done, 1)

                        def step(half, e, i, first=False, last=False, second=False):
                            pe.wait_ge(gu_in[half], 16 * i + 16)
                            pe.wait_ge(xt_ready, e + 1)
                            for k in range(KD):
                                for c in range(2):
                                    mm = pe.matmul(bank[c * LB:(c + 1) * LB, half, 0:FE], xt[half][:, k, :],
                                                   gu_w[half][:, k, c * FE:(c + 1) * FE], start=(k == 0), stop=(k == KD - 1))
                            mm.then_inc(gu_done, 1)
                            if not last:
                                turn_rows(e + 1, 1 - half, i + half)
                            if not first:
                                if not second:
                                    pe.wait_ge(y_ready, e - 1)
                                outputs(1 - half, e - 1, i - 1 + half)
                            pe.wait_ge(hh_ready, e + 1)
                            pe.sem_inc(pe_order, 1)
                            for k in range(2):
                                mm = pe.transpose(bank[:, 4, k * LB:(k + 1) * LB], hh[half][:, k * P:(k + 1) * P], ident[0:LB, 0:LB])
                            mm.then_inc(ht_done, 1)
                        pe.wait_ge(clear, 2)
                        turn_rows(0, 0, 0)
                        step(0, 0, 0, first=True)
                        step(1, 1, 0, second=True)
                        with pe.Fori(1, NE // 2 - 1) as i:
                            for half in range(2):
                                step(half, 2 * i + half, i)
                        step(0, NE - 2, NE // 2 - 1)
                        step(1, NE - 1, NE // 2 - 1, last=True)
                        pe.wait_ge(y_ready, NE - 1)
                        outputs(1, NE - 1, NE // 2 - 1)

                    @block.scalar
                    def _(act):
                        def rows_t(half, e):
                            act.wait_ge(xt_done, e + 1)
                            act.copy(xt[half][:, :, :], bank[:, 2 + half, :].rearrange("p (k n) -> p k n", n=LB)).then_inc(xt_ready, 1)

                        def step(half, e, first=False, last=False):
                            act.wait_ge(gu_done, e + 1)
                            if not first:
                                act.wait_ge(hh_ready, e - 1)
                            act.activation(sg[half][:, :], bank[0:LB, half, 0:FE], ACT.Silu).then_inc(sg_ready, 1)
                            if not last:
                                rows_t(1 - half, e + 1)
                        rows_t(0, 0)
                        step(0, 0, first=True)
                        step(1, 1, first=True)
                        with act.Fori(1, NE // 2 - 1) as i:
                            for half in range(2):
                                step(half, 2 * i + half)
                        step(0, NE - 2)
                        step(1, NE - 1, last=True)

                    @block.vector
                    def _(dve):
                        def rows_out(half, e, i, waits):
                            dve.wait_ge(y_done, e + 1)
                            if waits:
                                dve.wait_ge(y_out[half], 16 * i)
                            dve.tensor_copy(yo[half][:, 0:512], bank[0:LB, 6 + half, :])
                            dve.tensor_copy(yo[half][:, 512:], bank[LB:2 * LB, 6 + half, :]).then_inc(y_ready, 1)

                        def step(half, e, i, first=False, early=False):
                            dve.wait_ge(sg_ready, e + 1)
                            if not first and not early:
                                dve.wait_ge(ht_done, e - 1)
                            dve.tensor_tensor(hh[half][:, :], sg[half][:, :], bank[LB:2 * LB, half, 0:FE], ALU.mult).then_inc(hh_ready, 1)
                            if not first:
                                rows_out(1 - half, e - 1, i - 1 + half, not early)
                            dve.wait_ge(ht_done, e + 1)
                            dve.tensor_copy(ht[half][:, :, :], bank[:, 4, 0:2 * LB].rearrange("p (k n) -> p k n", k=2)).then_inc(ht_ready, 1)
                        step(0, 0, 0, first=True)
                        step(1, 1, 0, early=True)
                        dve.wait_ge(sg_ready, 3)
                        dve.wait_ge(ht_done, 1)
                        dve.tensor_tensor(hh[0][:, :], sg[0][:, :], bank[LB:2 * LB, 0, 0:FE], ALU.mult).then_inc(hh_ready, 1)
                        rows_out(1, 1, 0, False)
                        dve.wait_ge(ht_done, 3)
                        dve.tensor_copy(ht[0][:, :, :], bank[:, 4, 0:2 * LB].rearrange("p (k n) -> p k n", k=2)).then_inc(ht_ready, 1)
                        step(1, 3, 1)
                        with dve.Fori(2, NE // 2) as i:
                            for half in range(2):
                                step(half, 2 * i + half, i)
                        rows_out(1, NE - 1, NE // 2 - 1, True)

                blocks = sb("blocks", [1, MAXOVER], I32, stack=ph)
                owners = sb("owners", [1, MAXOVER], I32, stack=ph)
                found = sb("found", [1, MAXOVER], stack=ph)
                found_e = sb("found_e", [1, MAXOVER], stack=ph)
                pick = sb("pick", [1, MAXOVER, NBLK - NE], stack=ph)
                w_in2, x_in2, y_out2 = sem("w_in2", ph), sem("x_in2", ph), sem("y_out2", ph)
                idx2, xt_done2, xt_ready2, gu_done2, sg_ready2, hh_ready2 = (
                    sem("idx2", ph), sem("xt_done2", ph), sem("xt_ready2", ph), sem("gu_done2", ph), sem("sg_ready2", ph),
                    sem("hh_ready2", ph))
                ht_done2, ht_ready2, y_done2, y_ready2 = (sem("ht_done2", ph), sem("ht_ready2", ph), sem("y_done2", ph),
                                                          sem("y_ready2", ph))
                listed, list_order = sem("listed", ph), sem("list_order", ph)

                def behind_first(eng):
                    return eng.value_load(over[0:1, 0:1], min_val=0, max_val=MAXOVER)

                with nc.Block() as block:
                    @block.sync
                    def _(sp):
                        more = behind_first(sp)
                        with sp.If(more > 0):
                            sp.wait_ge(listed, 1)
                            with sp.Fori(0, more) as n:
                                e = sp.value_load(owners[0:1, bass.ds(n, 1)], min_val=0, max_val=NE - 1)
                                sp.dma_start(gu_w[0], io["w_gu"][bass.ds(e, 1)].rearrange("a p k c -> (a p) k c")).then_inc(w_in2, 16)
                                sp.dma_start(dn_w[0], io["w_dn"][bass.ds(e, 1)].rearrange("a p k c -> (a p) k c")).then_inc(w_in2, 16)
                                sp.wait_ge(y_done2, n + 1)
                                sp.sem_inc(sp_order, 1)

                    @block.gpsimd
                    def _(pool):
                        more = behind_first(pool)
                        with pool.If(more > 0):
                            pool.wait_ge(listed, 1)
                            with pool.Fori(0, more) as n:
                                blk = pool.value_load(blocks[0:1, bass.ds(n, 1)], min_val=NE, max_val=NBLK - 1)
                                pool.tensor_copy(gi[0][:, :], tab[:, bass.ds(blk, 1), 0]).then_inc(idx2, 1)
                                pool.tensor_copy(si[0][:, :], tab[:, bass.ds(blk, 1), 1]).then_inc(idx2, 1)
                                pool.wait_ge(idx2, 2 * n + 2)
                                pool.sem_inc(pool_order, 1)
                                pool.indirect_dma_start(xg[0][:, :], None, tok_rows,
                                                        bass.IndirectOffsetOnAxis(ap=gi[0][:, :].bitcast(U32), axis=0),
                                                        bounds_check=T - 1, oob_is_err=False).then_inc(x_in2, 16)
                                pool.wait_ge(y_ready2, n + 1)
                                pool.sem_inc(pool_order, 1)
                                pool.indirect_dma_start(choice_rows,
                                                        bass.IndirectOffsetOnAxis(ap=si[0][:, :].bitcast(U32), axis=0),
                                                        yo[0][:, :], None, bounds_check=T * TOPK - 1,
                                                        oob_is_err=False).then_inc(y_out2, 16)
                                pool.wait_ge(y_out2, 16 * n + 16)
                                pool.sem_inc(pool_order, 1)

                    @block.tensor
                    def _(pe):
                        more = behind_first(pe)
                        with pe.If(more > 0):
                            with pe.Fori(0, more) as n:
                                pe.wait_ge(x_in2, 16 * n + 16)
                                pe.sem_inc(pe_order, 1)
                                for k in range(KD):
                                    mm = pe.transpose(bank[:, 2, k * LB:(k + 1) * LB], xg[0][:, k * P:(k + 1) * P],
                                                      ident[0:LB, 0:LB])
                                mm.then_inc(xt_done2, 1)
                                pe.wait_ge(xt_ready2, n + 1)
                                pe.wait_ge(w_in2, 32 * n + 32)
                                for k in range(KD):
                                    for c in range(2):
                                        mm = pe.matmul(bank[c * LB:(c + 1) * LB, 0, 0:FE], xt[0][:, k, :],
                                                       gu_w[0][:, k, c * FE:(c + 1) * FE], start=(k == 0), stop=(k == KD - 1))
                                mm.then_inc(gu_done2, 1)
                                pe.wait_ge(hh_ready2, n + 1)
                                pe.sem_inc(pe_order, 1)
                                for k in range(2):
                                    mm = pe.transpose(bank[:, 4, k * LB:(k + 1) * LB], hh[0][:, k * P:(k + 1) * P],
                                                      ident[0:LB, 0:LB])
                                mm.then_inc(ht_done2, 1)
                                pe.wait_ge(ht_ready2, n + 1)
                                for k in range(2):
                                    for c in range(2):
                                        mm = pe.matmul(bank[c * LB:(c + 1) * LB, 6, :], ht[0][:, k, :],
                                                       dn_w[0][:, k, c * 512:(c + 1) * 512], start=(k == 0), stop=(k == 1))
                                mm.then_inc(y_done2, 1)

                    @block.scalar
                    def _(act):
                        more = behind_first(act)
                        with act.If(more > 0):
                            with act.Fori(0, more) as n:
                                act.wait_ge(xt_done2, n + 1)
                                act.copy(xt[0][:, :, :], bank[:, 2, :].rearrange("p (k n) -> p k n", n=LB)).then_inc(xt_ready2, 1)
                                act.wait_ge(gu_done2, n + 1)
                                act.activation(sg[0][:, :], bank[0:LB, 0, 0:FE], ACT.Silu).then_inc(sg_ready2, 1)

                    @block.vector
                    def _(dve):
                        more = behind_first(dve)
                        with dve.If(more > 0):
                            later = con[0:1, CONSTS["later"][0]:CONSTS["later"][1]]
                            count = con[0:1, CONSTS["count"][0]:CONSTS["count"][1]]
                            wide = [1, MAXOVER, NBLK - NE]
                            steps = [0]

                            def step2(ins):
                                steps[0] += 1
                                ins.then_inc(list_order, 1)
                                dve.wait_ge(list_order, steps[0])
                            step2(dve.tensor_tensor(pick[:, :, :], behind_n[:, :].unsqueeze(1).to_broadcast(wide),
                                                   count.unsqueeze(2).to_broadcast(wide), ALU.is_equal))
                            step2(dve.tensor_tensor(pick[:, :, :], pick[:, :, :], behind[:, :].unsqueeze(1).to_broadcast(wide), ALU.mult))
                            step2(dve.tensor_tensor(pick[:, :, :], pick[:, :, :], later.unsqueeze(1).to_broadcast(wide), ALU.mult))
                            step2(dve.tensor_reduce(found[:, :], pick[:, :, :], AX.X, ALU.add))
                            step2(dve.tensor_scalar(found_e[:, :], found[:, :], float(NE), None, ALU.subtract))
                            for r in range(2, ROUNDS):
                                step2(dve.tensor_scalar(pick[:, :, 0], found[:, :], float(r * NE), -float(NE), ALU.is_ge, ALU.mult))
                                step2(dve.tensor_tensor(found_e[:, :], found_e[:, :], pick[:, :, 0], ALU.add))
                            dve.tensor_copy(owners[:, :], found_e[:, :])
                            dve.tensor_copy(blocks[:, :], found[:, :]).then_inc(listed, 1)
                            with dve.Fori(0, more) as n:
                                dve.wait_ge(sg_ready2, n + 1)
                                dve.tensor_tensor(hh[0][:, :], sg[0][:, :], bank[LB:2 * LB, 0, 0:FE], ALU.mult).then_inc(hh_ready2, 1)
                                dve.wait_ge(ht_done2, n + 1)
                                dve.tensor_copy(ht[0][:, :, :], bank[:, 4, 0:2 * LB].rearrange("p (k n) -> p k n", k=2)).then_inc(ht_ready2, 1)
                                dve.wait_ge(y_done2, n + 1)
                                dve.tensor_copy(yo[0][:, 0:512], bank[0:LB, 6, :])
                                dve.tensor_copy(yo[0][:, 512:], bank[LB:2 * LB, 6, :]).then_inc(y_ready2, 1)

            with ExitStack() as ph:
                cr = [sb(f"cr{i}", [P, TOPK, D], stack=ph) for i in range(2)]
                cr_s = sb("cr_s", [TS, TOPK, D], stack=ph)
                diag = sb("diag", [P, NT, TOPK, P], stack=ph)
                ff = sb("ff", [P, KD, T], stack=ph)
                y = sb("y", [P, KD, T], stack=ph)
                rows_in, diag_ready, sum_done, ff_ready, y_ready11 = (sem("rows_in", ph), sem("diag_ready", ph), sem("sum_done", ph),
                                                                      sem("ff_ready", ph), sem("y_ready11", ph))
                with nc.Block() as block:
                    @block.sync
                    def _(sp):
                        for j in range(NT):
                            n = TILE_ROWS[j]
                            dst = (cr[0], cr[1], cr_s)[j]
                            sp.dma_start(dst[:, :, :], choice_rows.rearrange("(t k) d -> t k d", k=TOPK)[j * P:j * P + n]
                                         ).then_inc(rows_in, 16)
                        sp.wait_ge(y_ready11, 1)
                        store(sp, io["y"], y[:, :, :])
                        sp.wait_ge(stored, n_stored[0])

                    @block.vector
                    def _(dve):
                        for j in range(NT):
                            for k in range(TOPK):
                                ins = dve.tensor_scalar(diag[:, j, k, :], ident, w6[:, j, k:k + 1], None, ALU.mult)
                        ins.then_inc(diag_ready, 1)
                        for d in range(KD):
                            dve.wait_ge(sum_done, d + 1)
                            dve.tensor_tensor(ff[:, d, :], bank[:, d % 4, 0:T], shared[:, d, :], ALU.add).then_inc(ff_ready, 1)
                        dve_rstd(7)
                        dve_residual(ff[:, :, :], y, pcol("g_post_ffn"), 5, y_ready11)

                    @block.scalar
                    def _(act):
                        act.wait_ge(ff_ready, KD)
                        act_square(7, ff[:, :, :], KD)
                        act_root(7, D, 4)

                    @block.tensor
                    def _(pe):
                        pe.wait_ge(diag_ready, 1)
                        pe.wait_ge(rows_in, 16 * NT)
                        for d in range(KD):
                            if d >= 4:
                                pe.wait_ge(ff_ready, d - 3)
                            for j in range(NT):
                                n = TILE_ROWS[j]
                                src = (cr[0], cr[1], cr_s)[j]
                                for k in range(TOPK):
                                    mm = pe.matmul(bank[:, d % 4, j * P:j * P + n], src[:, k, d * P:(d + 1) * P],
                                                   diag[0:n, j, k, 0:n], start=(k == 0), stop=(k == TOPK - 1))
                            mm.then_inc(sum_done, 1)
                        pe_norm(7, KD, 4)


OUTPUTS = {"y": [P, KD, T], "ckv": [P, 2, T], "kpe": [ROPE, T], "conv_p": [P, KC, CW - 1], "conv_s": [P, KC, CW - 1, TS],
           "ssm_p": [P, SH, SP_], "ssm_s": [P, TS, SH, SP_]}


def tiles_of(w, n, k=KD, c=P):
    return w.reshape(k, P, n, c).transpose(2, 1, 0, 3)


def by_partition(v):
    v = v.reshape(v.shape[:-1] + (v.shape[-1] // P, P))
    return np.moveaxis(v, -1, 0)


def lay_out(i):
    f = {k: np.asarray(v) for k, v in i.items()}
    a = {}
    xs = np.concatenate([f["x_prompt"][0], f["x_sample"][:, 0]], 0)
    a["x_t"] = by_partition(xs).transpose(0, 2, 1)
    a["c_t"] = by_partition(np.concatenate([f["c_prompt"], f["c_sample"]], 0)).transpose(0, 2, 1)
    units = np.zeros((N_UNITS, P, UW), np.float32)
    units[0:N_ADA] = tiles_of(f["w_ada"][0], N_ADA, c=4 * P).reshape(N_ADA, P, UW)
    w = f["w_in"][0]
    at = np.cumsum([0, QL, KVL, ROPE, DI, CC, SH, D, D])
    part = [w[:, at[n]:at[n + 1]] for n in range(8)]
    half = ROPE // 2
    kp = part[2]
    kp_sw = np.concatenate([kp[:, half:], kp[:, :half]], 1)
    dt = np.concatenate([part[5], np.zeros((D, P - SH), np.float32)], 1)
    w = np.concatenate([part[0], part[1], kp, kp, kp, kp, kp_sw, kp_sw, kp_sw, kp_sw, dt, part[4], part[3], part[6], part[7]], 1)
    units[U_WIN:U_WIN + N_WIN] = tiles_of(w, 44).reshape(N_WIN, 4, P, KD * P).transpose(0, 2, 1, 3).reshape(N_WIN, P, UW)
    qb = f["w_q_b"][0].reshape(3, P, NH, QH)
    qb = np.concatenate([qb, qb[..., NOPE + half:], qb[..., NOPE:NOPE + half]], -1)
    uk = f["w_uk"][0].reshape(2, P, NH * NOPE)
    units[U_QB] = np.concatenate([qb.transpose(1, 0, 2, 3).reshape(P, -1), uk.transpose(1, 0, 2).reshape(P, -1)], 1)
    units[U_OA] = f["w_o_attn"][0].reshape(4, P, D).transpose(1, 0, 2).reshape(P, UW)
    units[U_OS:U_OS + 2] = f["w_o_ssd"][0].reshape(2, 4, P, D).transpose(0, 2, 1, 3).reshape(2, P, UW)
    units[U_OUT:U_OUT + 2] = tiles_of(f["w_out"][0], 8).reshape(2, 4, P, KD * P).transpose(0, 2, 1, 3).reshape(2, P, UW)
    sgu = np.concatenate([f["w_gate_s"][0], f["w_up_s"][0]], 1)
    units[U_SGU] = tiles_of(sgu, 4).transpose(1, 0, 2, 3).reshape(P, UW)
    units[U_SDN, :, 0:2 * D] = f["w_down_s"][0].reshape(2, P, D).transpose(1, 0, 2).reshape(P, -1)
    units[U_SDN, :, 2 * D:2 * D + KD * NE] = f["w_router"][0].reshape(KD, P, NE).transpose(1, 0, 2).reshape(P, -1)
    a["w_units"] = units
    a["w_uv"] = f["w_uv"][0].reshape(2, P, NH * VD).transpose(1, 0, 2)
    a["w_ukt"] = f["w_uk"][0].transpose(2, 1, 0)
    a["state_conv"] = by_partition(f["state_conv"][0]).transpose(0, 3, 2, 1)
    a["state_ssm"] = f["state_ssm"][0].transpose(3, 0, 1, 2)
    a["cache"] = np.concatenate([f["cache_ckv"][0], f["cache_kpe"][0]], -1)
    a["page_table"] = f["page_table"].reshape(1, -1)
    a["w_gu"] = np.concatenate([f["w_gate_e"][0].reshape(NE, KD, P, FE), f["w_up_e"][0].reshape(NE, KD, P, FE)],
                               -1).transpose(0, 2, 1, 3)
    a["w_dn"] = f["w_down_e"][0].reshape(NE, 2, P, D).transpose(0, 2, 1, 3)
    par = np.zeros((P, NPAR), np.float32)

    def put(name, v):
        lo, hi = PARAMS[name]
        par[:, lo:hi] = v
    put("b_ada", by_partition(f["b_ada"][0]))
    for name in ("g_pre_mix", "g_post_mix", "g_pre_ffn", "g_post_ffn", "g_q_a", "g_kv_a", "g_ssd"):
        put(name, by_partition(f[name][0]))
    put("d_skip", by_partition(np.repeat(f["d_skip"][0], SP_)))
    put("conv_w", by_partition(f["conv_w"][0]).transpose(0, 2, 1).reshape(P, -1))
    put("conv_b", by_partition(f["conv_b"][0]))
    lo = PARAMS["heads"][0]
    par[0:SH, lo] = f["dt_bias"][0]
    par[0:SH, lo + 1] = f["a_log"][0]
    put("b_router", np.broadcast_to(f["b_router"][0], (P, NE)))
    a["params"] = par
    return a


def constants():
    con = np.zeros((P, NCON), np.float32)

    def put(name, v):
        lo, hi = CONSTS[name]
        con[:, lo:hi] = v
    r = np.arange(P)
    put("ident", np.eye(P))
    put("ones", 1.0)
    put("causal_t", r[:, None] <= r[None, :])
    put("before", r[:, None] < r[None, :])
    put("mask", np.where(r[None, :] <= r[:, None], 0.0, -BIG))
    half = ROPE // 2
    place = np.concatenate([np.arange(TP), np.full(TS, PAST)]).astype(np.float32)
    inv = (np.float32(10000.0) ** (-np.arange(half, dtype=np.float32) / half)).astype(np.float32)
    ang = (place[None, :] * inv[:, None]).astype(np.float32)
    put("cos", np.tile(np.cos(ang), (P // half, 1)))
    put("sin", np.tile(np.concatenate([-np.sin(ang), np.sin(ang)]), (P // ROPE, 1)))
    put("eps", EPS)
    put("expert", np.arange(NE)[None, :])
    put("later", np.arange(NE, NBLK)[None, :])
    put("count", np.arange(1, MAXOVER + 1)[None, :])
    put("valid", (np.arange(NT)[None, :] * P + r[:, None] < T))
    sel = np.zeros((SH, SH, P), np.float32)
    for hd in range(SH):
        sel[hd, hd] = 1.0
    tok = np.minimum(np.arange(NT)[None, :] * P + r[:, None], T - 1)
    vals = np.stack([np.broadcast_to(tok[..., None], (P, NT, TOPK)), tok[..., None] * TOPK + np.arange(TOPK)], -1).astype(np.int32)
    return {"consts": con, "sel": sel, "vals": vals, "fill": np.full((LB, NBLK, 2), SKIP, np.int32)}


def kernel(**inputs):
    import concourse.bacc as bacc
    from concourse.bass_utils import run_bass_kernel_spmd

    nc = bacc.Bacc("TRN2", target_bir_lowering=False, num_devices=1)
    arrays = {k: np.ascontiguousarray(v) for k, v in {**lay_out(inputs), **constants()}.items()}
    io = {k: nc.dram_tensor(f"in_{k}", v.shape, mybir.dt.from_np(v.dtype), kind="ExternalInput").ap() for k, v in arrays.items()}
    for k, shape in OUTPUTS.items():
        io[k] = nc.dram_tensor(f"out_{k}", shape, F32, kind="ExternalOutput").ap()
    build(nc, io)
    r = run_bass_kernel_spmd(nc, [{f"in_{k}": v for k, v in arrays.items()}], core_ids=[0]).results[0]
    o = {k: np.asarray(r[f"out_{k}"]) for k in OUTPUTS}

    def rows(v):
        return np.ascontiguousarray(v.transpose(2, 1, 0).reshape(v.shape[2], -1))
    y, ckv = rows(o["y"]), rows(o["ckv"])
    kpe = np.ascontiguousarray(o["kpe"].T)
    conv_p = o["conv_p"].transpose(2, 1, 0).reshape(1, 1, CW - 1, CC)
    conv_s = o["conv_s"].transpose(3, 2, 1, 0).reshape(1, TS, CW - 1, CC)
    ssm_p = o["ssm_p"].transpose(1, 2, 0)[None, None]
    ssm_s = o["ssm_s"].transpose(1, 2, 3, 0)[None]
    return (y[None, 0:TP], y[TP:, None], ckv[None, None, 0:TP], kpe[None, None, 0:TP], np.ascontiguousarray(conv_p),
            np.ascontiguousarray(ssm_p), ckv[None, TP:, None], kpe[None, TP:, None], np.ascontiguousarray(conv_s),
            np.ascontiguousarray(ssm_s))
```

```python
from contextlib import ExitStack

import numpy as np
import concourse.bass as bass
from concourse import mybir

F32 = mybir.dt.float32
I32 = mybir.dt.int32
U32 = mybir.dt.uint32
ALU = mybir.AluOpType
ACT = mybir.ActivationFunctionType
AX = mybir.AxisListType

P = 128
D = 1024
KD = D // P
TP, TS = 256, 8
T = TP + TS
ROWS = 1 + TS
NH, NOPE, ROPE, VD = 8, 64, 32, 64
QH = NOPE + ROPE
QL, KVL = 384, 256
SCALE = QH ** -0.5
PAST, PAGE = 2048, 128
NPG = PAST // PAGE
POOL = 160
PW = KVL + ROPE
SH, SP_, NS, SG = 16, 64, 128, 2
DI = SH * SP_
KI = DI // P
CH = 128
CW = 4
CC = DI + 2 * SG * NS
KC = CC // P
NE, TOPK, NG, TOPG, FE = 64, 6, 8, 4, 256
EPG = NE // NG
ROUTE = 2.5
EPS = 1e-6
BIG = 1e30
NT = 3
TILE_ROWS = (128, 128, 8)
LB = 64
ROUNDS = -(-T // LB)
NBLK = NE * ROUNDS
MAXOVER = TOPK * T // LB
SKIP = 1 << 20

RING = 3
UW = 4096
N_ADA, N_WIN = 12, 11
EARLY_ADA = 4
ADA_AT = list(range(EARLY_ADA)) + [EARLY_ADA + 1 + 2 * i for i in range(N_ADA - EARLY_ADA)]
WIN_AT = [u for u in range(N_ADA + N_WIN) if u not in ADA_AT]
U_QB = N_ADA + N_WIN
U_OA = U_QB + 1
U_OS = U_OA + 1
U_SGU = U_OS + 2
U_SDN = U_SGU + 1
N_UNITS = U_SDN + 1
U_OUT = N_UNITS

PARAMS = {}
_at = 0
for _name, _n in (("b_ada", 48), ("g_pre_mix", 8), ("g_post_mix", 8), ("g_pre_ffn", 8), ("g_post_ffn", 8),
                  ("g_q_a", 3), ("g_kv_a", 2), ("g_ssd", 8), ("d_skip", 8), ("conv_w", 48), ("conv_b", 12),
                  ("heads", 2), ("b_router", 64)):
    PARAMS[_name] = (_at, _at + _n)
    _at += _n
NPAR = _at
CONSTS = {}
_at = 0
for _name, _n in (("ident", P), ("ones", P), ("causal_t", P), ("before", P), ("mask", P), ("cos", T), ("sin", T),
                  ("eps", 1), ("expert", NE), ("valid", NT), ("later", NBLK - NE),
                  ("count", MAXOVER), ("same_head", NH)):
    CONSTS[_name] = (_at, _at + _n)
    _at += _n
NCON = _at


def build(nc, io):
    with ExitStack() as top:
        def sem(name, stack=top):
            return stack.enter_context(nc.semaphore(name))

        def sb(name, shape, dt=F32, stack=top):
            return stack.enter_context(nc.sbuf_tensor(name, shape, dt))

        bank = top.enter_context(nc.psum_tensor("bank", [P, 8, 512], F32))

        ring = sb("ring", [P, RING, UW])
        par = sb("par", [P, NPAR])
        con = sb("con", [P, NCON])
        x = sb("x", [P, KD, T])
        mod = sb("mod", [P, 48, ROWS])
        sq = sb("sq", [P, KD, T])
        root = sb("root", [P, T])
        rstd = sb("rstd", [P, T])
        gain = sb("gain", [P, KD, ROWS])
        norm_tmp = sq

        def pcol(name, lo=0, n=None):
            a, b = PARAMS[name]
            return par[:, a + lo:(b if n is None else a + lo + n)]

        def ccol(name):
            a, b = CONSTS[name]
            return con[:, a:b]
        ident, ones, eps = ccol("ident"), ccol("ones"), ccol("eps")

        small_in = sem("small_in")
        unit_in = [sem(f"unit_in{s}") for s in range(RING)]
        unit_used = sem("unit_used")
        squares_ready, sums_ready, root_ready, rstd_ready = (
            sem("squares_ready"), sem("sums_ready"), sem("root_ready"), sem("rstd_ready"))
        dve_order, pool_order, sp_order, pe_order = sem("dve_order"), sem("pool_order"), sem("sp_order"), sem("pe_order")
        stored = sem("stored")
        n_stored = [0]
        order = {"dve": 0}

        def link(ins):
            order["dve"] += 1
            ins.then_inc(dve_order, 1)
            nc.vector.wait_ge(dve_order, order["dve"])

        def store(eng, dst, src):
            eng.dma_start(dst, src).then_inc(stored, 16)
            n_stored[0] += 16

        loaded = [0]

        def load_units(sp, upto):
            while loaded[0] < min(upto, N_UNITS):
                u = loaded[0]
                if u >= RING:
                    sp.wait_ge(unit_used, u - RING + 1)
                sp.dma_start(ring[:, u % RING, :], io["w_units"][u]).then_inc(unit_in[u % RING], 16)
                loaded[0] += 1

        def unit(u, pattern, **sizes):
            n = int(np.prod(list(sizes.values())))
            return ring[:, u % RING, 0:n].rearrange(pattern, **sizes)

        def wait_unit(pe, u):
            pe.wait_ge(unit_in[u % RING], 16 * (u // RING + 1))

        def act_square(n, src, tiles):
            nc.scalar.activation(sq[:, 0:tiles, :], src, ACT.Square).then_inc(squares_ready, 1)

        def pe_norm(n, tiles, b):
            nc.tensor.wait_ge(squares_ready, n + 1)
            for k in range(tiles):
                mm = nc.tensor.matmul(bank[:, b, 0:T], ones, sq[:, k, :], start=(k == 0), stop=(k == tiles - 1))
            mm.then_inc(sums_ready, 1)

        def act_root(n, dim, b):
            nc.scalar.wait_ge(sums_ready, n + 1)
            if n:
                nc.scalar.wait_ge(rstd_ready, n)
            nc.scalar.activation(root[:, :], bank[:, b, 0:T], ACT.Sqrt, bias=eps, scale=1.0 / dim).then_inc(root_ready, 1)

        def dve_rstd(n):
            nc.vector.wait_ge(root_ready, n + 1)
            nc.vector.reciprocal(rstd[:, :], root[:, :]).then_inc(rstd_ready, 1)
            nc.vector.wait_ge(rstd_ready, n + 1)

        def dve_modulate(src, dst, g, shift, scale, done):
            v = nc.vector
            link(v.tensor_scalar(gain[:, :, :], mod[:, 8 * scale:8 * scale + 8, :], 1.0, None, ALU.add))
            link(v.tensor_tensor(gain[:, :, :], gain[:, :, :], g.unsqueeze(2).to_broadcast([P, KD, ROWS]), ALU.mult))
            link(v.tensor_tensor(norm_tmp[:, :, :], src, rstd[:, :].unsqueeze(1).to_broadcast([P, KD, T]), ALU.mult))
            for k in range(KD):
                v.tensor_scalar(dst[:, k, 0:TP], norm_tmp[:, k, 0:TP], gain[:, k, 0:1], mod[:, 8 * shift + k, 0:1],
                                ALU.mult, ALU.add)
            link(v.tensor_tensor(norm_tmp[:, :, TP:T], norm_tmp[:, :, TP:T], gain[:, :, 1:ROWS], ALU.mult))
            v.tensor_tensor(dst[:, :, TP:T], norm_tmp[:, :, TP:T], mod[:, 8 * shift:8 * shift + 8, 1:ROWS],
                            ALU.add).then_inc(done, 1)

        def dve_residual(src, dst, g, gate, done):
            v = nc.vector
            link(v.tensor_tensor(gain[:, :, :], mod[:, 8 * gate:8 * gate + 8, :],
                                 g.unsqueeze(2).to_broadcast([P, KD, ROWS]), ALU.mult))
            link(v.tensor_tensor(norm_tmp[:, :, :], src, rstd[:, :].unsqueeze(1).to_broadcast([P, KD, T]), ALU.mult))
            for k in range(KD):
                v.scalar_tensor_tensor(dst[:, k, 0:TP], norm_tmp[:, k, 0:TP], gain[:, k, 0:1], x[:, k, 0:TP],
                                       ALU.mult, ALU.add)
            link(v.tensor_tensor(norm_tmp[:, :, TP:T], norm_tmp[:, :, TP:T], gain[:, :, 1:ROWS], ALU.mult))
            v.tensor_tensor(dst[:, :, TP:T], norm_tmp[:, :, TP:T], x[:, :, TP:T], ALU.add).then_inc(done, 1)

        def pe_ada(pe, u, b, sc):
            at = ADA_AT[u]
            w = unit(at, "p (k g c) -> p k g c", k=KD, g=4, c=P)
            wait_unit(pe, at)
            for k in range(KD):
                for g in range(4):
                    mm = pe.matmul(bank[32 * g:32 * g + 32, b, (u % 4) * P:(u % 4 + 1) * P], sc[:, k, :],
                                   w[:, k, g, :], start=(k == 0), stop=(k == KD - 1))
            mm.then_inc(unit_used, 1)

        def mod_rows(q, b, dst):
            return nc.vector.tensor_tensor(dst, bank[:, b, :].rearrange("p (t r) -> p t r", r=32)[:, :, 0:ROWS],
                                           pcol("b_ada", 16 * q, 16).unsqueeze(2).to_broadcast([P, 16, ROWS]), ALU.add)

        with ExitStack() as mix:
            w_uv = sb("w_uv", [P, 2, NH * VD], stack=mix)
            gate_z = sb("gate_z", [P, KI, T], stack=mix)
            gate_a = sb("gate_a", [P, KD, T], stack=mix)
            gate_b = sb("gate_b", [P, KD, T], stack=mix)
            xc = sb("xc", [P, KC, T], stack=mix)
            dt = sb("dt", [SH, T], stack=mix)
            o_attn = sb("o_attn", [P, 4, T], stack=mix)
            att_in = ExitStack()
            early = sb("early", [P, 7 * T + NH * KVL], stack=att_in)
            q_a = early[:, 0:3 * T].rearrange("p (k t) -> p k t", t=T)
            kv_a = early[:, 3 * T:5 * T].rearrange("p (k t) -> p k t", t=T)
            kpe = early[:, 5 * T:7 * T].rearrange("p (k t) -> p k t", t=T)
            w_ukt = early[0:NOPE, 7 * T:].rearrange("p (h c) -> p h c", c=KVL)

            with ExitStack() as ph:
                c = sb("c", [P, KD, ROWS], stack=ph)
                sc = sb("sc", [P, KD, 32], stack=ph)
                raw = sb("raw", [P, 3, 4, P], stack=ph)
                h = sb("h", [P, KD, T], stack=ph)
                xpad = sb("xpad", [P, KC, CW - 1 + TP], stack=ph)
                xs4 = sb("xs4", [P, KC, CW, TS], stack=ph)
                conv = sb("conv", [P, KC, T], stack=ph)
                conv_s = sb("conv_s", [P, KC, CW, TS], stack=ph)
                last3 = sb("last3", [P, KC, CW - 1], stack=ph)
                cond_ready, raw_ready, h_ready = sem("cond_ready", ph), sem("raw_ready", ph), sem("h_ready", ph)
                mod_turned = sem("mod_turned", ph)
                with nc.Block() as block:
                    @block.sync
                    def _(sp):
                        sp.dma_start(par[:, :], io["params"]).then_inc(small_in, 16)
                        sp.dma_start(con[:, :], io["consts"]).then_inc(small_in, 16)
                        sp.dma_start(c[:, :, :], io["c_t"]).then_inc(small_in, 16)
                        load_units(sp, 2)
                        sp.dma_start(x[:, :, :], io["x_t"]).then_inc(small_in, 16)
                        sp.dma_start(w_uv[:, :, :], io["w_uv"]).then_inc(small_in, 16)
                        sp.dma_start(w_ukt[:, :, :], io["w_ukt"]).then_inc(small_in, 16)
                        sp.dma_start(xs4[:, :, 0:CW - 1, :], io["state_conv"]).then_inc(small_in, 16)
                        load_units(sp, EARLY_ADA + RING)

                    @block.scalar
                    def _(act):
                        act.wait_ge(small_in, 16 * 7)
                        act.wait_ge(cond_ready, 1)
                        act.activation(sc[:, :, 0:ROWS], c[:, :, :], ACT.Silu).then_inc(cond_ready, 1)
                        act_square(0, x[:, :, :], KD)
                        act_root(0, D, 7)

                    @block.tensor
                    def _(pe):
                        pe.wait_ge(small_in, 16 * 7)
                        pe.wait_ge(cond_ready, 2)
                        for u in range(EARLY_ADA):
                            pe_ada(pe, u, 0, sc)
                            if u == 1:
                                pe_norm(0, KD, 7)
                        pe.wait_ge(raw_ready, 1)
                        for i in range(4):
                            mm = pe.transpose(bank[:, 4, i * P:(i + 1) * P], raw[:, 0, i, :], ident)
                        mm.then_inc(mod_turned, 1)

                    @block.vector
                    def _(dve):
                        dve.wait_ge(small_in, 16 * 7)
                        dve.memset(xpad[:, :, 0:CW - 1], 0.0)
                        dve.memset(sc[:, :, :], 0.0).then_inc(cond_ready, 1)
                        dve_rstd(0)
                        dve.wait_ge(unit_used, EARLY_ADA)
                        dve.tensor_copy(raw[:, 0, :, :], bank[:, 0, :].rearrange("p (i c) -> p i c", c=P)).then_inc(raw_ready, 1)
                        dve.wait_ge(mod_turned, 1)
                        link(mod_rows(0, 4, mod[:, 0:16, :]))
                        dve_modulate(x[:, :, :], h, pcol("g_pre_mix"), 0, 1, h_ready)

                tiles = ([("q_a", i) for i in range(3)] + [("kv_a", i) for i in range(2)] + [("kpe", i) for i in range(2)]
                         + [("dt", 0)] + [("xbc", i) for i in range(KC)] + [("z", i) for i in range(KI)]
                         + [("ga", i) for i in range(KD)] + [("gb", i) for i in range(KD)])
                NB = 6
                n_dve = 8 + KC
                win_done, dve_took, act_took = sem("win_done", ph), sem("dve_took", ph), sem("act_took", ph)
                conv_ready, xc_ready = sem("conv_ready", ph), sem("xc_ready", ph)
                tails_ready = sem("tails_ready", ph)
                with nc.Block() as block:
                    @block.sync
                    def _(sp):
                        load_units(sp, U_QB + RING)

                    @block.tensor
                    def _(pe):
                        for t, (kind, i) in enumerate(tiles):
                            u, j = WIN_AT[t // 4], t % 4
                            if j == 0:
                                wait_unit(pe, u)
                            if t >= NB:
                                if t - NB < n_dve:
                                    pe.wait_ge(dve_took, t - NB + 1)
                                else:
                                    pe.wait_ge(act_took, t - NB - n_dve + 1)
                            w = unit(u, "p (j k c) -> p j k c", j=4, k=KD, c=P)
                            m = SH if kind == "dt" else P
                            for k in range(KD):
                                mm = pe.matmul(bank[0:m, t % NB, 0:T], w[:, j, k, 0:m], h[:, k, :],
                                               start=(k == 0), stop=(k == KD - 1))
                            mm.then_inc(win_done, 1)
                            if j == 3:
                                pe.wait_ge(win_done, t + 1)
                                pe.sem_inc(unit_used, 1)
                                ada = EARLY_ADA + t // 4
                                if ada < N_ADA:
                                    pe_ada(pe, ada, 5 + ada // 4, sc)
                        for q in (1, 2):
                            pe.wait_ge(raw_ready, q + 1)
                            for i in range(4):
                                mm = pe.transpose(bank[:, 5 + q, i * P:(i + 1) * P], raw[:, q, i, :], ident)
                            mm.then_inc(mod_turned, 1)

                    @block.vector
                    def _(dve):
                        for t, (kind, i) in enumerate(tiles[:n_dve]):
                            dve.wait_ge(win_done, t + 1)
                            src = bank[:, t % NB, 0:T]
                            if kind == "xbc":
                                dve.tensor_copy(xpad[:, i, CW - 1:], src[:, 0:TP])
                                ins = dve.tensor_copy(xs4[:, i, CW - 1, :], src[:, TP:T])
                            elif kind == "dt":
                                ins = dve.tensor_copy(dt[:, :], src[0:SH, :])
                            else:
                                ins = dve.tensor_copy({"q_a": q_a, "kv_a": kv_a, "kpe": kpe}[kind][:, i, :], src)
                            ins.then_inc(dve_took, 1)
                        dve.wait_ge(unit_used, ADA_AT[7] + 1)
                        dve.tensor_copy(raw[:, 1, :, :], bank[:, 6, :].rearrange("p (i c) -> p i c", c=P)).then_inc(raw_ready, 1)
                        dve.wait_ge(dve_took, n_dve)
                        dve.tensor_copy(last3[:, :, :], xpad[:, :, TP:TP + CW - 1]).then_inc(tails_ready, 1)
                        for i in range(KC):
                            link(dve.tensor_scalar(conv[:, i, 0:TP], xpad[:, i, 0:TP], pcol("conv_w", i * CW, 1),
                                                   pcol("conv_b", i, 1), ALU.mult, ALU.add))
                            for w in range(1, CW):
                                link(dve.scalar_tensor_tensor(conv[:, i, 0:TP], xpad[:, i, w:w + TP],
                                                              pcol("conv_w", i * CW + w, 1), conv[:, i, 0:TP],
                                                              ALU.mult, ALU.add))
                        wc = pcol("conv_w").rearrange("p (i w) -> p i w", w=CW)
                        for w in range(1, CW):
                            dve.tensor_tensor(conv_s[:, :, w, :], xs4[:, :, w, :],
                                              wc[:, :, w:w + 1].to_broadcast([P, KC, TS]), ALU.mult)
                        link(dve.tensor_tensor(conv[:, :, TP:T], xs4[:, :, 0, :],
                                               wc[:, :, 0:1].to_broadcast([P, KC, TS]), ALU.mult))
                        for w in range(1, CW):
                            link(dve.tensor_tensor(conv[:, :, TP:T], conv[:, :, TP:T], conv_s[:, :, w, :], ALU.add))
                        dve.tensor_tensor(conv[:, :, TP:T], conv[:, :, TP:T],
                                          pcol("conv_b").unsqueeze(2).to_broadcast([P, KC, TS]),
                                          ALU.add).then_inc(conv_ready, 1)
                        dve.wait_ge(unit_used, ADA_AT[11] + 1)
                        dve.tensor_copy(raw[:, 2, :, :], bank[:, 7, :].rearrange("p (i c) -> p i c", c=P)).then_inc(raw_ready, 1)
                        for q in (1, 2):
                            dve.wait_ge(mod_turned, q + 1)
                            link(mod_rows(q, 5 + q, mod[:, 16 * q:16 * q + 16, :]))

                    @block.scalar
                    def _(act):
                        act.wait_ge(tails_ready, 1)
                        store(act, io["conv_p"], last3[:, :, :])
                        store(act, io["conv_s"], xs4[:, :, 1:CW, :])
                        for t, (kind, i) in enumerate(tiles[n_dve:]):
                            act.wait_ge(win_done, n_dve + t + 1)
                            dst = {"z": gate_z, "ga": gate_a, "gb": gate_b}[kind]
                            act.activation(dst[:, i, :], bank[:, (n_dve + t) % NB, 0:T],
                                           ACT.Silu if kind == "z" else ACT.Sigmoid).then_inc(act_took, 1)
                        act.wait_ge(conv_ready, 1)
                        act.activation(xc[:, :, :], conv[:, :, :], ACT.Silu).then_inc(xc_ready, 1)
                        act.wait_ge(stored, n_stored[0])

            with att_in:
                qh = sb("qh", [QH, NH, T], stack=att_in)
                ckv = sb("ckv", [P, 2, T], stack=att_in)
                kr = sb("kr", [P, T], stack=att_in)
                q_lat = sb("q_lat", [P, 2, TS, 32], stack=att_in)
                q_rot = sb("q_rot", [QH, TS, 32], stack=att_in)
                ckv_row = sb("ckv_row", [TS, KVL], stack=att_in)
                NBUF, GR = 3, NPG // 4
                page = [sb(f"page{i}", [P, NPG, PW], stack=att_in) for i in range(NBUF - 1)]
                ptab = sb("ptab", [1, TS * NPG], I32, stack=att_in)
                ptab_in, weighed = sem("ptab_in", att_in), sem("weighed", att_in)
                page_in = [[sem(f"page_in{i}_{q}", att_in) for q in range(2)] for i in range(NBUF)]

                def load_pages(eng, q, b):
                    if b >= NBUF:
                        eng.wait_ge(weighed, b - NBUF + 1)
                    for j in range(q, NPG, 2):
                        at = b * NPG + j
                        r = eng.value_load(ptab[0:1, at:at + 1], min_val=0, max_val=POOL - 1)
                        eng.dma_start(page[b % NBUF][:, j, :], io["cache"][bass.ds(r, 1)].rearrange("a p c -> (a p) c")
                                      ).then_inc(page_in[b % NBUF][q], 16)
                own = ExitStack()
                kh = sb("kh", [QH, NH, TP], stack=own)
                val = sb("val", [P, 2, NH * VD], stack=own)
                with ExitStack() as ph:
                    qn = sb("qn", [P, 3, T], stack=ph)
                    t1 = sb("t1", [P, T], stack=ph)
                    t2 = sb("t2", [P, 2, T], stack=ph)
                    qn_ready, ckv_ready, kr_ready = sem("qn_ready", ph), sem("ckv_ready", ph), sem("kr_ready", ph)
                    q_done, q_took, q_nope_took = sem("q_done", ph), sem("q_took", ph), sem("q_nope_took", ph)
                    k_done, k_took = sem("k_done", ph), sem("k_took", ph)
                    v_done, lat_done, row_done, tail_took = (sem("v_done", ph), sem("lat_done", ph),
                                                             sem("row_done", ph), sem("tail_took", ph))
                    cos, sin = ccol("cos"), ccol("sin")
                    with nc.Block() as block:
                        @block.gpsimd
                        def _(pool):
                            pool.wait_ge(ptab_in, 16)
                            for b in range(NBUF - 1):
                                load_pages(pool, 1, b)

                        @block.sync
                        def _(sp):
                            sp.dma_start(ptab[:, :], io["page_table"]).then_inc(ptab_in, 16)
                            sp.wait_ge(ptab_in, 16)
                            for b in range(NBUF - 1):
                                load_pages(sp, 0, b)
                            sp.wait_ge(ckv_ready, 1)
                            store(sp, io["ckv"], ckv[:, :, :])
                            sp.wait_ge(kr_ready, 1)
                            store(sp, io["kpe"], kr[0:ROPE, :])
                            load_units(sp, U_OS + 1)

                        @block.scalar
                        def _(act):
                            act_square(1, q_a[:, :, :], 3)
                            act_root(1, QL, 0)
                            act_square(2, kv_a[:, :, :], 2)
                            act_root(2, KVL, 1)
                            for hd in range(NH):
                                act.wait_ge(q_done, hd + 1)
                                act.copy(qh[0:NOPE, hd, :], bank[0:NOPE, 2 * (hd % 3), 0:T]).then_inc(q_nope_took, 1)
                            for hd in range(NH):
                                act.wait_ge(k_done, hd + 1)
                                act.copy(kh[0:NOPE, hd, :], bank[0:NOPE, 6 + hd % 2, 0:TP]).then_inc(k_took, 1)

                        @block.tensor
                        def _(pe):
                            wq = unit(U_QB, "p (k s h c) -> p k s h c", k=3, s=1, h=NH, c=P)
                            wk = ring[:, U_QB % RING, 3 * NH * P:].rearrange("p (k c) -> p k c", k=2)
                            pe_norm(1, 3, 0)
                            pe_norm(2, 2, 1)
                            wait_unit(pe, U_QB)
                            pe.wait_ge(qn_ready, 1)
                            pe.wait_ge(rstd_ready, 3)
                            for hd in range(NH):
                                if hd >= 3:
                                    pe.wait_ge(q_took, hd - 2)
                                    pe.wait_ge(q_nope_took, hd - 2)
                                for k in range(3):
                                    pe.matmul(bank[0:QH, 2 * (hd % 3), 0:T], wq[:, k, 0, hd, 0:QH], qn[:, k, :],
                                              start=(k == 0), stop=(k == 2))
                                for k in range(3):
                                    mm = pe.matmul(bank[NOPE:QH, 2 * (hd % 3) + 1, 0:T], wq[:, k, 0, hd, QH:P],
                                                   qn[:, k, :], start=(k == 0), stop=(k == 2))
                                mm.then_inc(q_done, 1)
                            pe.wait_ge(ckv_ready, 1)
                            for hd in range(NH):
                                if hd >= 2:
                                    pe.wait_ge(k_took, hd - 1)
                                for k in range(2):
                                    mm = pe.matmul(bank[0:NOPE, 6 + hd % 2, 0:TP], wk[:, k, hd * NOPE:(hd + 1) * NOPE],
                                                   ckv[:, k, 0:TP], start=(k == 0), stop=(k == 1))
                                mm.then_inc(k_done, 1)
                            pe.wait_ge(k_done, NH)
                            pe.sem_inc(unit_used, 1)
                            pe.wait_ge(q_took, NH)
                            pe.wait_ge(q_nope_took, NH)
                            for tt in range(2):
                                for k in range(2):
                                    mm = pe.matmul(bank[:, tt, :], ckv[:, k, tt * P:(tt + 1) * P], w_uv[:, k, :],
                                                   start=(k == 0), stop=(k == 1))
                            mm.then_inc(v_done, 1)
                            for ct in range(2):
                                for hd in range(NH):
                                    at = (ct * NH + hd) * TS
                                    mm = pe.matmul(bank[:, 2, at:at + TS], w_ukt[:, hd, ct * P:(ct + 1) * P],
                                                   qh[0:NOPE, hd, TP:T], start=True, stop=True)
                            mm.then_inc(lat_done, 1)
                            pe.wait_ge(k_took, NH)
                            for ct in range(2):
                                mm = pe.transpose(bank[0:TS, 3, ct * P:(ct + 1) * P], ckv[:, ct, TP:T], ident)
                            mm.then_inc(row_done, 1)

                        @block.vector
                        def _(dve):
                            dve_rstd(1)
                            for k in range(3):
                                ins = dve.scalar_tensor_tensor(qn[:, k, :], q_a[:, k, :], pcol("g_q_a", k, 1), rstd[:, :],
                                                               ALU.mult, ALU.mult)
                            ins.then_inc(qn_ready, 1)
                            dve.wait_ge(qn_ready, 1)
                            dve_rstd(2)
                            for k in range(2):
                                ins = dve.scalar_tensor_tensor(ckv[:, k, :], kv_a[:, k, :], pcol("g_kv_a", k, 1),
                                                               rstd[:, :], ALU.mult, ALU.mult)
                            ins.then_inc(ckv_ready, 1)
                            dve.tensor_tensor(t2[:, 0, :], kpe[:, 0, :], cos, ALU.mult)
                            link(dve.tensor_tensor(t2[:, 1, :], kpe[:, 1, :], sin, ALU.mult))
                            link(dve.tensor_tensor(kr[:, :], t2[:, 0, :], t2[:, 1, :], ALU.add))
                            dve.sem_inc(kr_ready, 1)
                            dve.tensor_copy(kh[NOPE:QH, :, :], kr[NOPE:QH, 0:TP].unsqueeze(1).to_broadcast([ROPE, NH, TP]))
                            dve.memset(q_rot[:, :, :], 0.0)
                            link(dve.memset(q_lat[:, :, :, :], 0.0))
                            for hd in range(NH):
                                dve.wait_ge(q_done, hd + 1)
                                dve.tensor_tensor(t2[NOPE:QH, 0, :], bank[NOPE:QH, 2 * (hd % 3), 0:T], cos[NOPE:QH, :], ALU.mult)
                                link(dve.tensor_tensor(t2[NOPE:QH, 1, :], bank[NOPE:QH, 2 * (hd % 3) + 1, 0:T],
                                                       sin[NOPE:QH, :], ALU.mult))
                                ins = dve.tensor_tensor(qh[NOPE:QH, hd, :], t2[NOPE:QH, 0, :], t2[NOPE:QH, 1, :], ALU.add)
                                ins.then_inc(q_took, 1)
                                dve.wait_ge(q_took, hd + 1)
                            dve.tensor_copy(q_rot[NOPE:QH, :, 0:NH], qh[NOPE:QH, :, TP:T].rearrange("p h b -> p b h"))
                            dve.wait_ge(v_done, 1)
                            dve.tensor_copy(val[:, :, :], bank[:, 0:2, :])
                            dve.wait_ge(lat_done, 1)
                            dve.tensor_copy(q_lat[:, :, :, 0:NH].rearrange("p c b h -> p c h b"),
                                            bank[:, 2, 0:2 * NH * TS].rearrange("p (c h b) -> p c h b", c=2, h=NH))
                            dve.wait_ge(row_done, 1)
                            dve.tensor_copy(ckv_row[:, :], bank[0:TS, 3, 0:KVL])

                with ExitStack() as ph:
                    s = ring[:, (U_OS + 1) % RING, 0:NH * 3 * P].rearrange("p (h k) -> p h k", h=NH)
                    pt = early[:, 0:NH * 3 * P].rearrange("p (h k) -> p h k", h=NH)
                    mx = sb("mx", [P, 2, NH], stack=ph)
                    sm = sb("sm", [P, 2, NH], stack=ph)
                    s_done, s_shifted, exp_done, prob_ready = (sem("s_done", ph), sem("s_shifted", ph),
                                                               sem("exp_done", ph), sem("prob_ready", ph))
                    pt_done, pt_took, o_done = sem("pt_done", ph), sem("pt_took", ph), sem("o_done", ph)
                    mask = ccol("mask").unsqueeze(1).to_broadcast([P, NH, P])
                    with nc.Block() as block:
                        @block.tensor
                        def _(pe):
                            for hd in range(NH):
                                pe.matmul(bank[:, hd // 4, (hd % 4) * P:(hd % 4 + 1) * P], qh[:, hd, 0:P], kh[:, hd, 0:P],
                                          start=True, stop=True)
                                mm = pe.matmul(bank[:, 2 + hd // 2, (hd % 2) * TP:(hd % 2 + 1) * TP],
                                               qh[:, hd, P:TP], kh[:, hd, :], start=True, stop=True)
                            mm.then_inc(s_done, 1)
                            pe.wait_ge(s_shifted, 1)
                            pe.wait_ge(prob_ready, 1)
                            for hd in range(NH):
                                if hd >= 4:
                                    pe.wait_ge(pt_took, hd - 3)
                                for i in range(3):
                                    mm = pe.transpose(bank[:, hd % 4, i * P:(i + 1) * P], s[:, hd, i * P:(i + 1) * P], ident)
                                mm.then_inc(pt_done, 1)
                            for hd in range(NH):
                                pe.wait_ge(pt_took, hd + 1)
                                lo = (hd % 2) * VD
                                out = bank[lo:lo + VD, 4 + hd // 2, 0:TP]
                                v = [val[:, tt, hd * VD:(hd + 1) * VD] for tt in range(2)]
                                pe.matmul(out[:, 0:P], v[0], pt[:, hd, 0:P], start=True, stop=True)
                                pe.matmul(out[:, P:TP], v[0], pt[:, hd, P:2 * P], start=True, stop=False)
                                mm = pe.matmul(out[:, P:TP], v[1], pt[:, hd, 2 * P:], start=False, stop=True)
                            mm.then_inc(o_done, 1)

                        @block.vector
                        def _(dve):
                            dve.wait_ge(s_done, 1)
                            b0 = bank[:, 0:2, :].rearrange("p b (h k) -> p (b h) k", k=P)
                            b1 = bank[:, 2:6, :].rearrange("p b (h k) -> p (b h) k", k=TP)
                            dve.scalar_tensor_tensor(s[:, :, 0:P], b0, SCALE, mask, ALU.mult, ALU.add)
                            dve.tensor_scalar(s[:, :, P:2 * P], b1[:, :, 0:P], SCALE, None, ALU.mult)
                            link(dve.scalar_tensor_tensor(s[:, :, 2 * P:], b1[:, :, P:], SCALE, mask, ALU.mult, ALU.add))
                            dve.tensor_reduce(mx[:, 0, :], s[:, :, 0:P], AX.X, ALU.max)
                            link(dve.tensor_reduce(mx[:, 1, :], s[:, :, P:], AX.X, ALU.max))
                            dve.tensor_tensor(s[:, :, 0:P], s[:, :, 0:P], mx[:, 0, :].unsqueeze(2).to_broadcast([P, NH, P]),
                                              ALU.subtract)
                            dve.tensor_tensor(s[:, :, P:], s[:, :, P:], mx[:, 1, :].unsqueeze(2).to_broadcast([P, NH, TP]),
                                              ALU.subtract).then_inc(s_shifted, 1)
                            dve.wait_ge(exp_done, 1)
                            dve.tensor_reduce(sm[:, 0, :], s[:, :, 0:P], AX.X, ALU.add)
                            link(dve.tensor_reduce(sm[:, 1, :], s[:, :, P:], AX.X, ALU.add))
                            link(dve.reciprocal(sm[:, :, :], sm[:, :, :]))
                            dve.tensor_tensor(s[:, :, 0:P], s[:, :, 0:P], sm[:, 0, :].unsqueeze(2).to_broadcast([P, NH, P]),
                                              ALU.mult)
                            dve.tensor_tensor(s[:, :, P:], s[:, :, P:], sm[:, 1, :].unsqueeze(2).to_broadcast([P, NH, TP]),
                                              ALU.mult).then_inc(prob_ready, 1)
                            dve.wait_ge(o_done, 1)
                            dve.tensor_copy(o_attn[:, :, 0:TP], bank[:, 4:8, 0:TP])

                        @block.scalar
                        def _(act):
                            act.wait_ge(s_shifted, 1)
                            act.activation(s[:, :, :], s[:, :, :], ACT.Exp).then_inc(exp_done, 1)
                            for hd in range(NH):
                                act.wait_ge(pt_done, hd + 1)
                                act.copy(pt[:, hd, :], bank[:, hd % 4, 0:3 * P]).then_inc(pt_took, 1)

                own.close()

                with ExitStack() as ph:
                    page.append(sb(f"page{NBUF - 1}", [P, NPG, PW], stack=ph))
                    page_t = early[:, 0:24 * P].rearrange("p (a g i t) -> p a g i t", a=2, g=4, i=3)
                    free = (U_OS + 1) % RING
                    prob = [ring[:, free, i * 512:(i + 1) * 512] for i in range(2)]
                    prob_t = [ring[:, free, (2 + i) * 512:(3 + i) * 512].rearrange("p (m c) -> p m c", c=P) for i in range(2)]
                    neg_max = sb("neg_max", [P, TS], stack=ph)
                    total = sb("total", [P, TS], stack=ph)
                    part = sq[:, :, :].rearrange("p k t -> p (k t)")[:, 0:TS * KVL].rearrange("p (b c) -> p b c", c=KVL)
                    lat = sb("lat", [P, 2, TS, NH], stack=ph)
                    wsc = sb("wsc", [P, TS], stack=ph)
                    rest = early[0:TS, 24 * P:]
                    taken = [0]

                    def small(*dims):
                        n, at = int(np.prod(dims)), taken[0]
                        taken[0] += n
                        names = "abc"[:len(dims)]
                        return rest[:, at:at + n].rearrange(f"p ({' '.join(names)}) -> p {' '.join(names)}",
                                                            **dict(zip(names, dims)))
                    sc8, wn, wfull = small(TS, NH), small(TS, NH), small(4, 32)
                    sn, nm, z5 = rest[:, 600:608], rest[:, 608:616], rest[:, 616:624]
                    st5 = small(2, 128).rearrange("p a (g h) -> p a g h", h=32)
                    ex5 = small(5, NH)
                    zz = small(5, NH)
                    turned, turn_took_a, turn_took_d = sem("turned", ph), sem("turn_took_a", ph), sem("turn_took_d", ph)
                    scored, max_ready, exp5, prob_turned, prob_took = (sem("scored", ph), sem("max_ready", ph), sem("exp5", ph),
                                                                       sem("prob_turned", ph), sem("prob_took", ph))
                    part_took = sem("part_took", ph)
                    stats_done, new_exp, new_ready, wt_done, scaled5, lat_done, lat_took, o5 = (
                        sem("stats_done", ph), sem("new_exp", ph), sem("new_ready", ph), sem("wt_done", ph),
                        sem("scaled5", ph), sem("lat_done5", ph), sem("lat_took", ph), sem("o5", ph))
                    exp_in = sem("exp_in", ph)
                    with nc.Block() as block:
                        @block.sync
                        def _(sp):
                            for b in range(NBUF - 1, TS):
                                load_pages(sp, 0, b)

                        @block.tensor
                        def _(pe):
                            def score_pages(b):
                                pg = page[b % NBUF]
                                for q in range(2):
                                    pe.wait_ge(page_in[b % NBUF][q], 16 * NPG // 2 * (b // NBUF + 1))
                                if b >= 2:
                                    pe.wait_ge(exp5, b - 1)
                                for m in range(GR + 1):
                                    if m < GR:
                                        for g in range(4):
                                            n = (b * GR + m) * 2
                                            if n:
                                                pe.wait_ge(*((turn_took_a, n - 1 + g // 2) if g % 2 == 0 else
                                                             (turn_took_d, n - 1 + g // 2)))
                                            for i, (lo, hi) in enumerate(((0, P), (P, 2 * P), (PW - QH, PW))):
                                                mm = pe.transpose(bank[0:hi - lo, g, i * P:(i + 1) * P], pg[:, 4 * m + g, lo:hi], ident)
                                            mm.then_inc(turned, 1)
                                    if m >= 1:
                                        n = (b * GR + m) * 2
                                        pe.wait_ge(turn_took_a, n)
                                        pe.wait_ge(turn_took_d, n)
                                        for i in range(3):
                                            k = P if i < 2 else QH
                                            q = q_lat[:, i, b, :] if i < 2 else q_rot[:, b, :]
                                            for g in range(4):
                                                mm = pe.matmul(bank[32 * g:32 * g + 32, 4 + b % 2, (m - 1) * P:m * P], q,
                                                               page_t[0:k, (m - 1) % 2, g, i, :], start=(i == 0), stop=(i == 2))
                                mm.then_inc(scored, 1)

                            def weigh(b):
                                pe.wait_ge(exp5, b + 1)
                                if b:
                                    pe.wait_ge(prob_took, b)
                                for m in range(GR):
                                    mm = pe.transpose(bank[:, 6, m * P:(m + 1) * P], prob[b % 2][:, m * P:(m + 1) * P], ident)
                                mm.then_inc(prob_turned, 1)
                                pe.wait_ge(prob_took, b + 1)
                                if b:
                                    pe.wait_ge(part_took, b)
                                for m in range(GR):
                                    for g in range(4):
                                        mm = pe.matmul(bank[32 * g:32 * g + 32, 7, 0:KVL], prob_t[b % 2][:, m, 32 * g:32 * g + 32],
                                                       page[b % NBUF][:, 4 * m + g, 0:KVL], start=(m == 0), stop=(m == GR - 1))
                                mm.then_inc(weighed, 1)
                            for b in range(TS):
                                score_pages(b)
                                if b:
                                    weigh(b - 1)
                            weigh(TS - 1)
                            pe.wait_ge(part_took, TS)
                            pe.transpose(bank[0:TS, 0, 0:P], neg_max[:, :], ident)
                            pe.transpose(bank[0:TS, 0, P:2 * P], total[:, :], ident)
                            out = bank[0:TS, 1, 0:TS * 32]
                            for i in range(2):
                                pe.matmul(out, ckv[:, i, TP:T], q_lat[:, i, :, :].rearrange("p b h -> p (b h)"),
                                          start=(i == 0), stop=False)
                            pe.matmul(out, kr[0:QH, TP:T], q_rot[:, :, :].rearrange("p b h -> p (b h)"),
                                      start=False, stop=True).then_inc(stats_done, 1)
                            pe.wait_ge(new_ready, 1)
                            pe.transpose(bank[:, 2, 0:TS], wfull[:, :, :].rearrange("p g h -> p (g h)"), ident[0:TS, 0:TS]).then_inc(wt_done, 1)
                            pe.wait_ge(scaled5, 1)
                            for ct in range(2):
                                out = bank[:, 3, ct * TS * NH:(ct + 1) * TS * NH]
                                pe.matmul(out, ckv_row[:, ct * P:(ct + 1) * P], wn[:, :, :].rearrange("p b h -> p (b h)"),
                                          start=True, stop=False)
                                for b in range(TS):
                                    mm = pe.matmul(out[:, b * NH:(b + 1) * NH], part[:, b, ct * P:(ct + 1) * P],
                                                   ccol("same_head"), start=False, stop=(b == TS - 1))
                            mm.then_inc(lat_done, 1)
                            pe.wait_ge(lat_took, 1)
                            for hd in range(NH):
                                lo = (hd % 2) * VD
                                for ct in range(2):
                                    mm = pe.matmul(bank[lo:lo + VD, 4, (hd // 2) * TS:(hd // 2 + 1) * TS],
                                                   w_uv[:, ct, hd * VD:(hd + 1) * VD], lat[:, ct, :, hd],
                                                   start=(ct == 0), stop=(ct == 1))
                            mm.then_inc(o5, 1)

                        def take_page(eng, copy, b, m, g, done):
                            eng.wait_ge(turned, (b * GR + m) * 4 + g + 1)
                            copy(page_t[:, m % 2, g, 0:2, :], bank[:, g, 0:2 * P].rearrange("p (a c) -> p a c", a=2))
                            copy(page_t[0:QH, m % 2, g, 2, :], bank[0:QH, g, 2 * P:3 * P]).then_inc(done, 1)

                        @block.scalar
                        def _(act):
                            for b in range(TS):
                                for m in range(GR):
                                    for g in (0, 2):
                                        take_page(act, act.copy, b, m, g, turn_took_a)
                                if b >= 2:
                                    act.wait_ge(prob_turned, b - 1)
                                act.wait_ge(max_ready, b + 1)
                                act.activation(prob[b % 2][:, :], bank[:, 4 + b % 2, :], ACT.Exp, bias=neg_max[:, b:b + 1],
                                               scale=SCALE, accum_out=total[:, b:b + 1]).then_inc(exp5, 1)
                            act.wait_ge(exp_in, 1)
                            act.activation(ex5[:, :, :], ex5[:, :, :], ACT.Exp).then_inc(new_exp, 1)

                        @block.vector
                        def _(dve):
                            dve.memset(wfull[:, :, :], 0.0)

                            def take_probs(b):
                                dve.wait_ge(prob_turned, b + 1)
                                if b >= 2:
                                    dve.wait_ge(weighed, b - 1)
                                dve.tensor_copy(prob_t[b % 2][:, :, :], bank[:, 6, :].rearrange("p (m c) -> p m c", c=P)).then_inc(prob_took, 1)
                                dve.wait_ge(weighed, b + 1)
                                dve.tensor_copy(part[:, b, :], bank[:, 7, 0:KVL]).then_inc(part_took, 1)
                            for b in range(TS):
                                for m in range(GR):
                                    for g in (1, 3):
                                        take_page(dve, dve.tensor_copy, b, m, g, turn_took_d)
                                dve.wait_ge(scored, b + 1)
                                link(dve.tensor_reduce(neg_max[:, b:b + 1], bank[:, 4 + b % 2, :], AX.X, ALU.max))
                                dve.tensor_scalar(neg_max[:, b:b + 1], neg_max[:, b:b + 1], -SCALE, None, ALU.mult).then_inc(max_ready, 1)
                                if b:
                                    take_probs(b - 1)
                            take_probs(TS - 1)
                            dve.wait_ge(stats_done, 1)
                            dve.tensor_copy(st5[:, :, :, :].rearrange("p a g h -> p (a g h)"), bank[0:TS, 0, 0:2 * P])
                            link(dve.scalar_tensor_tensor(sc8[:, :, :], bank[0:TS, 1, 0:TS * 32].rearrange("p (b h) -> p b h", h=32)[:, :, 0:NH],
                                                          SCALE, ident[0:TS, 0:TS].unsqueeze(2).to_broadcast([TS, TS, NH]),
                                                          ALU.mult, ALU.mult))
                            link(dve.tensor_reduce(sn[:, :], sc8[:, :, :].rearrange("p b h -> p h b"), AX.X, ALU.add))
                            link(dve.tensor_reduce(nm[:, :], st5[:, 0, :, 0:NH].rearrange("p g h -> p h g"), AX.X, ALU.min))
                            link(dve.tensor_scalar(z5[:, :], sn[:, :], -1.0, None, ALU.mult))
                            link(dve.tensor_tensor(nm[:, :], nm[:, :], z5[:, :], ALU.min))
                            dve.tensor_tensor(ex5[:, 0:4, :], nm[:, :].unsqueeze(1).to_broadcast([TS, 4, NH]), st5[:, 0, :, 0:NH],
                                              ALU.subtract)
                            dve.tensor_tensor(ex5[:, 4, :], sn[:, :], nm[:, :], ALU.add).then_inc(exp_in, 1)
                            dve.wait_ge(new_exp, 1)
                            dve.tensor_tensor(zz[:, 0:4, :], ex5[:, 0:4, :], st5[:, 1, :, 0:NH], ALU.mult)
                            link(dve.tensor_copy(zz[:, 4, :], ex5[:, 4, :]))
                            link(dve.tensor_reduce(z5[:, :], zz[:, :, :].rearrange("p g h -> p h g"), AX.X, ALU.add))
                            link(dve.reciprocal(z5[:, :], z5[:, :]))
                            link(dve.tensor_tensor(ex5[:, :, :], ex5[:, :, :], z5[:, :].unsqueeze(1).to_broadcast([TS, 5, NH]), ALU.mult))
                            dve.tensor_copy(wfull[:, :, 0:NH], ex5[:, 0:4, :])
                            dve.tensor_tensor(wn[:, :, :], ex5[:, 4:5, :].to_broadcast([TS, TS, NH]),
                                              ident[0:TS, 0:TS].unsqueeze(2).to_broadcast([TS, TS, NH]), ALU.mult).then_inc(new_ready, 1)
                            dve.wait_ge(wt_done, 1)
                            link(dve.tensor_copy(wsc[:, :], bank[:, 2, 0:TS]))
                            dve.tensor_tensor(part[:, :, :], part[:, :, :], wsc[:, :].unsqueeze(2).to_broadcast([P, TS, KVL]),
                                              ALU.mult).then_inc(scaled5, 1)
                            dve.wait_ge(lat_done, 1)
                            dve.tensor_copy(lat[:, :, :, :].rearrange("p c b h -> p (c b h)"), bank[:, 3, 0:2 * TS * NH]).then_inc(lat_took, 1)
                            dve.wait_ge(o5, 1)
                            link(dve.tensor_copy(o_attn[:, :, TP:T], bank[:, 4, 0:4 * TS].rearrange("p (a b) -> p a b", a=4)))

                        @block.gpsimd
                        def _(pool):
                            for b in range(NBUF - 1, TS):
                                load_pages(pool, 1, b)
                            pool.wait_ge(stored, n_stored[0])

            o_ssd = sb("o_ssd", [P, KI, T], stack=mix)
            with ExitStack() as ph:
                NC = TP // CH
                ea = sb("ea", [P, SH, TS], stack=ph)
                HG = SH // SG
                xdt_s = sb("xdt_s", [TS, DI], stack=ph)
                bm = sb("bm", [TS, TS, SG, NS], stack=ph)
                sel_in, st_in = sem("sel_in", ph), [sem(f"st_in{i}", ph) for i in range(TS // 2)]
                abs_ready, exp6, a_ready = sem("abs_ready", ph), sem("exp6", ph), sem("a_ready", ph)
                tm_done, tm_took, ea_done, ea_took = sem("tm_done", ph), sem("tm_took", ph), sem("ea_done", ph), sem("ea_took", ph)
                x_done, x_took, b_done, b_took = sem("x_done", ph), sem("x_took", ph), sem("b_done", ph), sem("b_took", ph)
                g_done, g_took = sem("g_done", ph), sem("g_took", ph)
                sx_done, sx_took, bm_ready = sem("sx_done", ph), sem("sx_took", ph), sem("bm_ready", ph)
                ac_done, last_ready, dec_ready = sem("ac_done", ph), sem("last_ready", ph), sem("dec_ready", ph)
                m_shifted, m_exp, m_ready, cs_exp, cs_ready = (sem("m_shifted", ph), sem("m_exp", ph), sem("m_ready", ph),
                                                               sem("cs_exp", ph), sem("cs_ready", ph))
                xdd_ready, st_done, h_ready6, y_done6, y_took = (sem("xdd_ready", ph), sem("st_done", ph), sem("h_ready6", ph),
                                                                 sem("y_done6", ph), sem("y_took", ph))
                outer_done, st_ready, st_scaled, ys_done = sem("outer_done", ph), sem("st_ready", ph), sem("st_scaled", ph), sem("ys_done", ph)
                with ExitStack() as pr:
                    sel = sb("sel", [SH, SH, P], stack=pr)
                    a = sb("a", [SH, T], stack=pr)
                    acum = sb("acum", [SH, TP], stack=pr)
                    w1 = sb("w1", [SH, T], stack=pr)
                    w2 = sb("w2", [SH, T], stack=pr)
                    w3 = sb("w3", [SH, T], stack=pr)
                    w4 = sb("w4", [SH, T], stack=pr)
                    nega = sb("nega", [SH, 1], stack=pr)
                    one_row = sb("one_row", [SH, TP], stack=pr)
                    tm = sb("tm", [P, 5, SH], stack=pr)
                    lastb = sb("lastb", [P, NC, SH], stack=pr)
                    dend = sb("dend", [P, NC, SH], stack=pr)
                    xdt = sb("xdt", [P, NC, SH, SP_], stack=pr)
                    b_tm = sb("b_tm", [P, SG, NC, NS], stack=pr)
                    h1 = sb("h1", [P, SH, SP_], stack=pr)
                    hf = sb("hf", [P, SH, SP_], stack=pr)
                    g_t = sb("g_t", [P, SG, NC, CH], stack=pr)
                    bs_tm = sb("bs_tm", [TS, SG, NS], stack=pr)
                    m = sb("m", [P, NC, HG, CH], stack=pr)
                    cs = sb("cs", [P, HG, CH], stack=pr)
                    xdd = sb("xdd", [P, NC, SH, SP_], stack=pr)
                    with nc.Block() as block:
                        @block.sync
                        def _(sp):
                            sp.dma_start(sel[:, :, :], io["sel"]).then_inc(sel_in, 16)
                            load_units(sp, U_OA + RING)
                            sp.wait_ge(h_ready6, 2)
                            store(sp, io["ssm_p"], hf[:, :, :])

                        @block.scalar
                        def _(act):
                            act.activation(nega[:, :], pcol("heads", 1, 1)[0:SH, :], ACT.Exp)
                            act.wait_ge(abs_ready, 1)
                            act.activation(w2[:, :], w1[:, :], ACT.Exp, scale=-1.0).then_inc(exp6, 1)
                            act.wait_ge(ea_done, 1)
                            act.activation(ea[:, :, :], bank[:, 1, 0:SH * TS].rearrange("p (h b) -> p h b", h=SH),
                                           ACT.Exp).then_inc(ea_took, 1)
                            act.wait_ge(b_done, 1)
                            act.copy(b_tm[:, :, :, :], bank[:, 6, :].rearrange("p (g c n) -> p g c n", g=SG, c=NC)).then_inc(b_took, 1)
                            for g in range(SG):
                                act.wait_ge(ac_done, g + 1)
                                act.wait_ge(last_ready, g + 1)
                                act.activation(lastb[:, :, g * HG:(g + 1) * HG], lastb[:, :, g * HG:(g + 1) * HG], ACT.Exp)
                                act.activation(dend[:, :, g * HG:(g + 1) * HG], dend[:, :, g * HG:(g + 1) * HG],
                                               ACT.Exp).then_inc(dec_ready, 1)
                                act.wait_ge(m_shifted, g + 1)
                                if g:
                                    act.wait_ge(y_done6, 1)
                                act.activation(cs[:, :, :], bank[:, 0:4, :].rearrange("p b (h l) -> p (b h) l", l=TP)[:, :, CH:],
                                               ACT.Exp).then_inc(cs_exp, 1)
                                act.activation(m[:, :, :, :], m[:, :, :, :], ACT.Exp).then_inc(m_exp, 1)

                        @block.tensor
                        def _(pe):
                            pe.wait_ge(sel_in, 16)
                            pe.wait_ge(a_ready, 1)
                            for i in range(NC):
                                pe.transpose(bank[:, 0, i * SH:(i + 1) * SH], dt[:, i * CH:(i + 1) * CH], ident[0:SH, 0:SH])
                            for i in range(NC):
                                pe.transpose(bank[:, 0, (2 + i) * SH:(3 + i) * SH], acum[:, i * CH:(i + 1) * CH], ident[0:SH, 0:SH])
                            pe.transpose(bank[0:TS, 0, 4 * SH:5 * SH], dt[:, TP:T], ident[0:SH, 0:SH]).then_inc(tm_done, 1)
                            for hd in range(SH):
                                mm = pe.matmul(bank[:, 1, hd * TS:(hd + 1) * TS], sel[:, hd, :], a[:, TP:T], start=True, stop=True)
                            mm.then_inc(ea_done, 1)
                            for i in range(NC):
                                for k in range(KI):
                                    at = (i * KI + k) * P
                                    mm = pe.transpose(bank[:, 2 + at // 512, at % 512:at % 512 + P],
                                                      xc[:, k, i * CH:(i + 1) * CH], ident)
                            mm.then_inc(x_done, 1)
                            for g in range(SG):
                                for i in range(NC):
                                    at = (g * NC + i) * NS
                                    mm = pe.transpose(bank[:, 6, at:at + NS], xc[:, KI + g, i * CH:(i + 1) * CH], ident)
                            mm.then_inc(b_done, 1)
                            for g in range(SG):
                                for i in range(NC):
                                    at = (g * NC + i) * CH
                                    mm = pe.matmul(bank[:, 7, at:at + CH], xc[:, KI + g, i * CH:(i + 1) * CH],
                                                   xc[:, KI + SG + g, i * CH:(i + 1) * CH], start=True, stop=True)
                            mm.then_inc(g_done, 1)
                            pe.wait_ge(ea_took, 1)
                            pe.wait_ge(b_took, 1)
                            pe.wait_ge(x_took, 1)
                            for k in range(KI):
                                pe.transpose(bank[0:TS, k // 4, (k % 4) * P:(k % 4 + 1) * P], xc[:, k, TP:T], ident)
                            for g in range(SG):
                                mm = pe.transpose(bank[0:TS, 6, g * NS:(g + 1) * NS], xc[:, KI + g, TP:T], ident)
                            mm.then_inc(sx_done, 1)
                            pe.wait_ge(sx_took, 1)
                            pe.wait_ge(g_took, 1)
                            for g in range(SG):
                                if g:
                                    pe.wait_ge(m_shifted, 1)
                                    pe.wait_ge(cs_exp, 1)
                                    pe.wait_ge(last_ready, 1)
                                for hd in range(HG):
                                    mm = pe.matmul(bank[:, hd // 2, (hd % 2) * TP:(hd % 2 + 1) * TP], sel[:, g * HG + hd, :],
                                                   acum[:, :], start=True, stop=True)
                                mm.then_inc(ac_done, 1)
                                pe.wait_ge(xdd_ready, g + 1)
                                if g:
                                    pe.wait_ge(h_ready6, 1)
                                    pe.wait_ge(y_took, 1)
                                for i in range(NC):
                                    mm = pe.matmul(bank[:, 4 + i, :], b_tm[:, g, i, :],
                                                   xdd[:, i, g * HG:(g + 1) * HG, :].rearrange("p h d -> p (h d)"),
                                                   start=True, stop=True)
                                mm.then_inc(st_done, 1)
                                pe.wait_ge(m_ready, g + 1)
                                pe.wait_ge(cs_ready, g + 1)
                                pe.wait_ge(h_ready6, g + 1)
                                for hd in range(HG):
                                    lo, hh = (hd % 2) * SP_, g * HG + hd
                                    at = (hd // 2) % 2 * TP
                                    out = bank[lo:lo + SP_, 6 + hd // 4, at:at + TP]
                                    pe.matmul(out[:, 0:CH], xdt[:, 0, hh, :], m[:, 0, hd, :], start=True, stop=True)
                                    pe.matmul(out[:, CH:], xdt[:, 1, hh, :], m[:, 1, hd, :], start=True, stop=False)
                                    mm = pe.matmul(out[:, CH:], h1[:, hh, :], cs[:, hd, :], start=False, stop=True)
                                mm.then_inc(y_done6, 1)

                        @block.vector
                        def _(dve):
                            link(dve.tensor_scalar(w4[:, :], dt[:, :], pcol("heads", 0, 1)[0:SH, :], None, ALU.add))
                            link(dve.tensor_scalar(w1[:, :], w4[:, :], -1.0, None, ALU.mult))
                            dve.tensor_tensor(w1[:, :], w1[:, :], w4[:, :], ALU.max).then_inc(abs_ready, 1)
                            dve.wait_ge(exp6, 1)
                            link(dve.tensor_scalar(w3[:, :], w2[:, :], 2.0, None, ALU.add))
                            link(dve.reciprocal(w3[:, :], w3[:, :]))
                            link(dve.tensor_tensor(w3[:, :], w3[:, :], w2[:, :], ALU.mult))
                            link(dve.tensor_tensor(w2[:, :], w3[:, :], w3[:, :], ALU.mult))
                            link(dve.memset(w1[:, :], 0.0))
                            for n in range(9, 0, -1):
                                link(dve.scalar_tensor_tensor(w1[:, :], w1[:, :], 1.0 / (2 * n + 1), w2[:, :], ALU.add, ALU.mult))
                            link(dve.scalar_tensor_tensor(w1[:, :], w1[:, :], 1.0, w3[:, :], ALU.add, ALU.mult))
                            link(dve.tensor_scalar(w4[:, :], w4[:, :], 0.0, None, ALU.max))
                            link(dve.scalar_tensor_tensor(dt[:, :], w1[:, :], 2.0, w4[:, :], ALU.mult, ALU.add))
                            dve.memset(one_row[:, :], 1.0)
                            link(dve.tensor_scalar(a[:, :], dt[:, :], nega[:, 0:1], -1.0, ALU.mult, ALU.mult))
                            for i in range(NC):
                                ins = dve.tensor_tensor_scan(acum[:, i * CH:(i + 1) * CH], one_row[:, 0:CH],
                                                             a[:, i * CH:(i + 1) * CH], 0.0, ALU.mult, ALU.add)
                            ins.then_inc(a_ready, 1)
                            dve.wait_ge(tm_done, 1)
                            dve.tensor_copy(tm[:, 0:4, :], bank[:, 0, 0:4 * SH].rearrange("p (a h) -> p a h", a=4))
                            link(dve.tensor_copy(tm[0:TS, 4, :], bank[0:TS, 0, 4 * SH:5 * SH]))
                            dve.wait_ge(x_done, 1)
                            dve.tensor_tensor(xdt[:, :, :, :].rearrange("p c h d -> p (c h) d"),
                                              bank[:, 2:6, :].rearrange("p b (h d) -> p (b h) d", d=SP_),
                                              tm[:, 0:NC, :].rearrange("p c h -> p (c h)").unsqueeze(2).to_broadcast([P, NC * SH, SP_]),
                                              ALU.mult).then_inc(x_took, 1)
                            dve.wait_ge(g_done, 1)
                            dve.tensor_tensor(g_t[:, :, :, :].rearrange("p g c l -> p (g c) l"),
                                              bank[:, 7, :].rearrange("p (a l) -> p a l", l=CH),
                                              ccol("causal_t").unsqueeze(1).to_broadcast([P, SG * NC, CH]),
                                              ALU.mult).then_inc(g_took, 1)
                            dve.wait_ge(sx_done, 1)
                            dve.tensor_tensor(xdt_s[:, :].rearrange("p (h d) -> p h d", d=SP_),
                                              bank[0:TS, 0:2, :].rearrange("p b (h d) -> p (b h) d", d=SP_),
                                              tm[0:TS, 4, :].unsqueeze(2).to_broadcast([TS, SH, SP_]), ALU.mult)
                            link(dve.tensor_copy(bs_tm[:, :, :], bank[0:TS, 6, 0:SG * NS].rearrange("p (g n) -> p g n", g=SG)))
                            dve.sem_inc(sx_took, 1)
                            dve.tensor_tensor(bm[:, :, :, :].rearrange("p b g n -> p b (g n)"),
                                              bs_tm[:, :, :].rearrange("p g n -> p (g n)").unsqueeze(1).to_broadcast([TS, TS, SG * NS]),
                                              ident[0:TS, 0:TS].unsqueeze(2).to_broadcast([TS, TS, SG * NS]),
                                              ALU.mult).then_inc(bm_ready, 1)
                            for g in range(SG):
                                hs = slice(g * HG, (g + 1) * HG)
                                ac = bank[:, 0:4, :].rearrange("p b (h l) -> p (b h) l", l=TP)
                                dve.wait_ge(ac_done, g + 1)
                                for i in range(NC):
                                    ins = dve.tensor_copy(lastb[:, i, hs], ac[:, :, (i + 1) * CH - 1])
                                link(ins)
                                dve.tensor_tensor(dend[:, :, hs], lastb[:, :, hs], tm[:, 2:4, hs], ALU.subtract).then_inc(last_ready, 1)
                                dve.wait_ge(last_ready, g + 1)
                                if g:
                                    dve.wait_ge(y_done6, 1)
                                for i in range(NC):
                                    for hd in range(HG):
                                        ins = dve.tensor_scalar(m[:, i, hd, :], ac[:, hd, i * CH:(i + 1) * CH],
                                                                tm[:, 2 + i, g * HG + hd:g * HG + hd + 1], 0.0,
                                                                ALU.subtract, ALU.min)
                                ins.then_inc(m_shifted, 1)
                                dve.wait_ge(dec_ready, g + 1)
                                dve.tensor_tensor(xdd[:, :, hs, :], xdt[:, :, hs, :],
                                                  dend[:, :, hs].unsqueeze(3).to_broadcast([P, NC, HG, SP_]),
                                                  ALU.mult).then_inc(xdd_ready, 1)
                                dve.wait_ge(cs_exp, g + 1)
                                dve.tensor_tensor(cs[:, :, :], cs[:, :, :],
                                                  xc[:, KI + SG + g, CH:TP].unsqueeze(1).to_broadcast([P, HG, CH]),
                                                  ALU.mult).then_inc(cs_ready, 1)
                                dve.wait_ge(m_exp, g + 1)
                                dve.tensor_tensor(m[:, :, :, :], m[:, :, :, :],
                                                  g_t[:, g, :, :].unsqueeze(2).to_broadcast([P, NC, HG, CH]),
                                                  ALU.mult).then_inc(m_ready, 1)
                                dve.wait_ge(st_done, g + 1)
                                st = [bank[:, 4 + i, :].rearrange("p (h d) -> p h d", d=SP_) for i in range(NC)]
                                link(dve.tensor_copy(h1[:, hs, :], st[0]))
                                link(dve.tensor_tensor(hf[:, hs, :], h1[:, hs, :],
                                                       lastb[:, 1, hs].unsqueeze(2).to_broadcast([P, HG, SP_]), ALU.mult))
                                dve.tensor_tensor(hf[:, hs, :], hf[:, hs, :], st[1], ALU.add).then_inc(h_ready6, 1)
                                dve.wait_ge(y_done6, g + 1)
                                for j in range(4):
                                    k = g * 4 + j
                                    ins = dve.scalar_tensor_tensor(o_ssd[:, k, 0:TP], xc[:, k, 0:TP], pcol("d_skip", k, 1),
                                                                   bank[:, 6 + j // 2, (j % 2) * TP:(j % 2 + 1) * TP],
                                                                   ALU.mult, ALU.add)
                                ins.then_inc(y_took, 1)
                            dve.wait_ge(stored, n_stored[0])

                st = sb("st", [P, TS, SH, SP_], stack=ph)
                yt = sb("yt", [P, KI, TS], stack=ph)
                gated = sem("gated", ph)
                with nc.Block() as block:
                    @block.sync
                    def _(sp):
                        for b in range(TS):
                            sp.dma_start(st[:, b, :, :], io["state_ssm"][:, b]).then_inc(st_in[b // 2], 16)
                        for b in range(TS):
                            sp.wait_ge(st_ready, b + 1)
                            store(sp, io["ssm_s"][:, b], st[:, b, :, :])

                    @block.tensor
                    def _(pe):
                        def output(b):
                            pe.wait_ge(st_ready, b + 1)
                            for k in range(KI):
                                mm = pe.matmul(bank[:, 4, k * TS + b:k * TS + b + 1],
                                               st[:, b, 2 * k:2 * k + 2, :].rearrange("p h d -> p (h d)"),
                                               xc[:, KI + SG + k // 4, TP + b:TP + b + 1], start=True, stop=True)
                            return mm
                        for b in range(TS):
                            for g in range(SG):
                                mm = pe.matmul(bank[:, (b % 2) * 2 + g, :], bm[:, b, g, :], xdt_s[:, g * 512:(g + 1) * 512],
                                               start=True, stop=True)
                            mm.then_inc(outer_done, 1)
                            if b:
                                output(b - 1)
                        mm = output(TS - 1)
                        mm.then_inc(ys_done, 1)
                        for g in range(SG):
                            pe_norm(3 + g, 4, 5 + g)

                    @block.vector
                    def _(dve):
                        for b in range(TS):
                            dve.wait_ge(st_in[b // 2], 32)
                            link(dve.tensor_tensor(st[:, b, :, :], st[:, b, :, :],
                                                   ea[:, :, b:b + 1].to_broadcast([P, SH, SP_]), ALU.mult))
                            dve.wait_ge(outer_done, b + 1)
                            dve.tensor_tensor(st[:, b, :, :], st[:, b, :, :],
                                              bank[:, (b % 2) * 2:(b % 2) * 2 + 2, :].rearrange("p a (h d) -> p (a h) d", d=SP_),
                                              ALU.add).then_inc(st_ready, 1)
                        link(dve.tensor_tensor(yt[:, :, :], xc[:, 0:KI, TP:T],
                                               pcol("d_skip").unsqueeze(2).to_broadcast([P, KI, TS]), ALU.mult))
                        dve.wait_ge(ys_done, 1)
                        link(dve.tensor_tensor(o_ssd[:, :, TP:T], yt[:, :, :],
                                               bank[:, 4, 0:KI * TS].rearrange("p (k b) -> p k b", b=TS), ALU.add))
                        dve.tensor_tensor(o_ssd[:, :, :], o_ssd[:, :, :], gate_z[:, :, :], ALU.mult).then_inc(gated, 1)
                        dve.wait_ge(gated, 1)
                        for g in range(SG):
                            dve_rstd(3 + g)
                            for k in range(4 * g, 4 * g + 4):
                                ins = dve.scalar_tensor_tensor(o_ssd[:, k, :], o_ssd[:, k, :], pcol("g_ssd", k, 1), rstd[:, :],
                                                               ALU.mult, ALU.mult)
                            link(ins)
                        dve.wait_ge(stored, n_stored[0])

                    @block.scalar
                    def _(act):
                        act.wait_ge(gated, 1)
                        for g in range(SG):
                            act_square(3 + g, o_ssd[:, 4 * g:4 * g + 4, :], 4)
                            act_root(3 + g, DI // SG, 5 + g)

            with ExitStack() as ph:
                merged = sb("merged", [P, KD, T], stack=ph)
                mtmp = sb("mtmp", [P, 2, T], stack=ph)
                mo = sb("mo", [P, KD, T], stack=ph)
                w_out_sb = sb("w_out", [P, 2, UW], stack=ph)
                w_out_in = [sem(f"w_out_in{i}", ph) for i in range(2)]
                oo_done, merged_took, out_done, out_took, x1_ready = (sem("oo_done", ph), sem("merged_took", ph),
                                                                      sem("out_done", ph), sem("out_took", ph), sem("x1_ready", ph))
                mo_ready = sem("mo_ready", ph)
                with nc.Block() as block:
                    @block.gpsimd
                    def _(pool):
                        pool.sem_clear(range(cond_ready.num, exp_in.num + 1))

                    @block.sync
                    def _(sp):
                        for i in range(2):
                            sp.dma_start(w_out_sb[:, i, :], io["w_units"][U_OUT + i]).then_inc(w_out_in[i], 16)
                        load_units(sp, N_UNITS)

                    @block.tensor
                    def _(pe):
                        w_oa = unit(U_OA, "p (k c) -> p k c", k=4, c=D)
                        w_os = [unit(U_OS + i, "p (k c) -> p k c", k=4, c=D) for i in range(2)]
                        w_out = [w_out_sb[:, i, :].rearrange("p (j k c) -> p j k c", j=4, k=KD, c=P) for i in range(2)]
                        for u in (U_OA, U_OS, U_OS + 1):
                            wait_unit(pe, u)
                        for d in range(KD):
                            if d >= 3:
                                pe.wait_ge(merged_took, d - 2)
                            ba, bb = 2 * (d % 3), 2 * (d % 3) + 1
                            for k in range(4):
                                pe.matmul(bank[:, ba, 0:T], w_oa[:, k, d * P:(d + 1) * P], o_attn[:, k, :],
                                          start=(k == 0), stop=(k == 3))
                            for k in range(KI):
                                mm = pe.matmul(bank[:, bb, 0:T], w_os[k // 4][:, k % 4, d * P:(d + 1) * P], o_ssd[:, k, :],
                                               start=(k == 0), stop=(k == KI - 1))
                            mm.then_inc(oo_done, 1)
                        pe.wait_ge(oo_done, KD)
                        pe.sem_inc(unit_used, 3)
                        pe.wait_ge(merged_took, KD)
                        for d in range(KD):
                            if d % 4 == 0:
                                pe.wait_ge(w_out_in[d // 4], 16)
                            if d >= 4:
                                pe.wait_ge(out_took, d - 3)
                            for k in range(KD):
                                mm = pe.matmul(bank[:, d % 4, 0:T], w_out[d // 4][:, d % 4, k, :], merged[:, k, :],
                                               start=(k == 0), stop=(k == KD - 1))
                            mm.then_inc(out_done, 1)
                        pe_norm(5, KD, 4)

                    @block.vector
                    def _(dve):
                        for d in range(KD):
                            dve.wait_ge(oo_done, d + 1)
                            dve.tensor_tensor(mtmp[:, 0, :], gate_a[:, d, :], bank[:, 2 * (d % 3), 0:T], ALU.mult)
                            link(dve.tensor_tensor(mtmp[:, 1, :], gate_b[:, d, :], bank[:, 2 * (d % 3) + 1, 0:T], ALU.mult))
                            dve.tensor_tensor(merged[:, d, :], mtmp[:, 0, :], mtmp[:, 1, :], ALU.add).then_inc(merged_took, 1)
                            dve.wait_ge(merged_took, d + 1)
                        dve_rstd(5)
                        dve_residual(mo[:, :, :], x, pcol("g_post_mix"), 2, x1_ready)

                    @block.scalar
                    def _(act):
                        for d in range(KD):
                            act.wait_ge(out_done, d + 1)
                            act.copy(mo[:, d, :], bank[:, d % 4, 0:T]).then_inc(out_took, 1)
                        act.wait_ge(out_took, KD)
                        act_square(5, mo[:, :, :], KD)
                        act_root(5, D, 4)

        tok_rows = nc.dram_tensor("tok_rows", [T, D], F32, kind="Internal").ap()
        choice_rows = nc.dram_tensor("choice_rows", [T * TOPK, D], F32, kind="Internal").ap()
        lists = nc.dram_tensor("lists", [LB * NBLK, 2], I32, kind="Internal").ap()
        with ExitStack() as moe:
            w6 = sb("w6", [P, NT, TOPK], stack=moe)
            shared = sb("shared", [P, KD, T], stack=moe)
            tab = sb("tab", [LB, NBLK, 2], I32, stack=moe)
            over = sb("over", [1, 1], I32, stack=moe)
            behind = sb("behind", [1, NBLK - NE], stack=moe)
            behind_n = sb("behind_n", [1, NBLK - NE], stack=moe)
            one_r = sb("one_r", [1, NBLK - NE], stack=moe)
            gu_in = [sem(f"gu_in{i}", moe) for i in range(2)]
            dn_in = [sem(f"dn_in{i}", moe) for i in range(2)]
            gu_w = [ring[:, i, :].rearrange("p (k c) -> p k c", k=KD) for i in range(2)]
            dn_w = [ring[:, 2, i * 2048:(i + 1) * 2048].rearrange("p (k c) -> p k c", k=2) for i in range(2)]

            with ExitStack() as ph:
                h2 = sb("h2", [P, KD, T], stack=ph)
                rows = sb("rows", [P, NT, D], stack=ph)
                sg = sb("sg", [P, 2, T], stack=ph)
                hs = sb("hs", [P, 2, T], stack=ph)
                score = sb("score", [P, NT, NE], stack=ph)
                biased = sb("biased", [P, NT, NE], stack=ph)
                vals = sb("vals", [P, NT, TOPK, 2], I32, stack=ph)
                fill = sb("fill", [LB, NBLK, 2], I32, stack=ph)
                m8 = sb("m8", [P, NT, NG, 8], stack=ph)
                gs = sb("gs", [P, NT, NG], stack=ph)
                g8 = sb("g8", [P, NT, 8], stack=ph)
                ga1 = sb("ga1", [P, NT, NG], stack=ph)
                ga2 = sb("ga2", [P, NT, NG], stack=ph)
                ga3 = sb("ga3", [P, NT, NG], stack=ph)
                need = sb("need", [P, NT], stack=ph)
                one_c = sb("one_c", [P, NE], stack=ph)
                e1 = sb("e1", [P, NT, NE], stack=ph)
                e2 = sb("e2", [P, NT, NE], stack=ph)
                e3 = sb("e3", [P, NT, NE], stack=ph)
                chosen = sb("chosen", [P, NT, NE], stack=ph)
                rank = sb("rank", [P, NT, NE], stack=ph)
                pos = sb("pos", [P, NT, NE], stack=ph)
                wgt = sb("wgt", [P, NT, NE], stack=ph)
                ek = sb("ek", [P, NT, TOPK], stack=ph)
                pk = sb("pk", [P, NT, TOPK], stack=ph)
                ck = sb("ck", [P, NT, TOPK], stack=ph)
                addr = sb("addr", [P, NT, TOPK], I32, stack=ph)
                h2_ready, route_in, logits_done, scores_ready = (sem("h2_ready", ph), sem("route_in", ph),
                                                                 sem("logits_done", ph), sem("scores_ready", ph))
                rows_done, rows_took = sem("rows_done", ph), sem("rows_took", ph)
                rows_stored, lists_filled, lists_set, tab_in = (sem("rows_stored", ph), sem("lists_filled", ph),
                                                                sem("lists_set", ph), sem("tab_in", ph))
                sgu_done, sg_ready9, hs_ready, sdn_done = (sem("sgu_done", ph), sem("sg_ready9", ph), sem("hs_ready", ph),
                                                           sem("sdn_done", ph))
                shared_took = sem("shared_took", ph)
                chosen_ready, pos_done, addr_ready = sem("chosen_ready", ph), sem("pos_done", ph), sem("addr_ready", ph)
                with nc.Block() as block:
                    @block.sync
                    def _(sp):
                        sp.dma_start(vals[:, :, :, :], io["vals"]).then_inc(route_in, 16)
                        sp.dma_start(fill[:, :, :], io["fill"]).then_inc(route_in, 16)
                        sp.wait_ge(route_in, 32)
                        sp.dma_start(lists.rearrange("(p b) c -> p b c", p=LB), fill[:, :, :]).then_inc(lists_filled, 16)
                        for i in range(2):
                            sp.dma_start(dn_w[i], io["w_dn"][i]).then_inc(dn_in[i], 16)
                        sp.wait_ge(unit_used, N_UNITS - 1)
                        sp.dma_start(gu_w[0], io["w_gu"][0]).then_inc(gu_in[0], 16)
                        sp.wait_ge(unit_used, N_UNITS)
                        sp.dma_start(gu_w[1], io["w_gu"][1]).then_inc(gu_in[1], 16)
                        for j in range(NT):
                            sp.wait_ge(rows_took, j + 1)
                            n = TILE_ROWS[j]
                            sp.dma_start(tok_rows[j * P:j * P + n, :], rows[0:n, j, :]).then_inc(rows_stored, 16)
                        sp.wait_ge(rows_stored, 16 * NT)
                        sp.wait_ge(lists_set, 16 * NT * TOPK)
                        sp.dma_start(tab[:, :, :], lists.rearrange("(p b) c -> p b c", p=LB)).then_inc(tab_in, 16)
                        sp.wait_ge(tab_in, 16)

                    @block.scalar
                    def _(act):
                        act_square(6, x[:, :, :], KD)
                        act_root(6, D, 0)
                        act.wait_ge(logits_done, 1)
                        act.wait_ge(scores_ready, 1)
                        act.activation(score[:, 0:2, :], bank[:, 1, 0:2 * NE].rearrange("p (a e) -> p a e", a=2), ACT.Sigmoid)
                        act.activation(score[0:TS, 2, :], bank[0:TS, 1, 2 * NE:3 * NE], ACT.Sigmoid).then_inc(scores_ready, 1)
                        for i in range(2):
                            act.wait_ge(sgu_done, i + 1)
                            act.activation(sg[:, i, :], bank[:, 2 + i, 0:T], ACT.Silu).then_inc(sg_ready9, 1)
                        for j in range(NT):
                            n = TILE_ROWS[j]
                            act.wait_ge(rows_done, j + 1)
                            act.copy(rows[0:n, j, :], bank[0:n, 6:8, :].rearrange("p a b -> p (a b)")).then_inc(rows_took, 1)
                        for d in range(KD):
                            act.wait_ge(sdn_done, d + 1)
                            act.copy(shared[:, d, :], bank[:, 2 + d % 4, 0:T]).then_inc(shared_took, 1)

                    @block.tensor
                    def _(pe):
                        pe_norm(6, KD, 0)
                        pe.wait_ge(h2_ready, 1)
                        wr = ring[:, U_SDN % RING, 2 * D:2 * D + KD * NE].rearrange("p (k e) -> p k e", k=KD)
                        wd = ring[:, U_SDN % RING, 0:2 * D].rearrange("p (k c) -> p k c", k=2)
                        wait_unit(pe, U_SDN)
                        for j in range(NT):
                            n = TILE_ROWS[j]
                            for k in range(KD):
                                mm = pe.matmul(bank[0:n, 1, j * NE:(j + 1) * NE], h2[:, k, j * P:j * P + n], wr[:, k, :],
                                               start=(k == 0), stop=(k == KD - 1))
                        mm.then_inc(logits_done, 1)
                        w = unit(U_SGU, "p (j k c) -> p j k c", j=4, k=KD, c=P)
                        wait_unit(pe, U_SGU)
                        for i in range(2):
                            for half in range(2):
                                for k in range(KD):
                                    mm = pe.matmul(bank[:, 2 + i + 2 * half, 0:T], w[:, 2 * half + i, k, :], h2[:, k, :],
                                                   start=(k == 0), stop=(k == KD - 1))
                            mm.then_inc(sgu_done, 1)
                        pe.wait_ge(sgu_done, 2)
                        pe.sem_inc(unit_used, 1)
                        for j in range(NT):
                            n = TILE_ROWS[j]
                            if j:
                                pe.wait_ge(rows_took, j)
                            for k in range(KD):
                                mm = pe.transpose(bank[0:n, 6 + k // 4, (k % 4) * P:(k % 4 + 1) * P], h2[:, k, j * P:j * P + n], ident)
                            mm.then_inc(rows_done, 1)
                        pe.wait_ge(chosen_ready, 1)
                        before = ccol("before")
                        for j in range(NT):
                            for i in range(j):
                                pe.matmul(bank[:, 0, j * NE:(j + 1) * NE], ones, chosen[:, i, :], start=(i == 0), stop=False)
                            pe.matmul(bank[:, 0, j * NE:(j + 1) * NE], before, chosen[:, j, :], start=(j == 0), stop=True)
                        for i in range(NT):
                            mm = pe.matmul(bank[0:1, 0, NT * NE:(NT + 1) * NE], ones[:, 0:1], chosen[:, i, :],
                                           start=(i == 0), stop=(i == NT - 1))
                        mm.then_inc(pos_done, 1)
                        pe.wait_ge(hs_ready, 2)
                        for d in range(KD):
                            if d >= 4:
                                pe.wait_ge(shared_took, d - 3)
                            for k in range(2):
                                mm = pe.matmul(bank[:, 2 + d % 4, 0:T], wd[:, k, d * P:(d + 1) * P], hs[:, k, :],
                                               start=(k == 0), stop=(k == 1))
                            mm.then_inc(sdn_done, 1)
                        pe.wait_ge(sdn_done, KD)
                        pe.sem_inc(unit_used, 1)

                    @block.vector
                    def _(dve):
                        dve.memset(score[:, :, :], 0.0).then_inc(scores_ready, 1)
                        dve.memset(one_c[:, :], 1.0)
                        dve_rstd(6)
                        dve_modulate(x[:, :, :], h2, pcol("g_pre_ffn"), 3, 4, h2_ready)
                        dve.wait_ge(scores_ready, 2)
                        link(dve.tensor_tensor(biased[:, :, :], score[:, :, :],
                                               pcol("b_router").unsqueeze(1).to_broadcast([P, NT, NE]), ALU.add))
                        for j in range(NT):
                            for g in range(NG):
                                ins = dve.max(m8[:, j, g, :], biased[:, j, g * EPG:(g + 1) * EPG])
                        link(ins)
                        link(dve.tensor_tensor(gs[:, :, :], m8[:, :, :, 0], m8[:, :, :, 1], ALU.add))

                        def top(src, a1, a2, a3, n, k, dst):
                            for j in range(NT):
                                ins = dve.max(g8[:, j, :], src[:, j, :])
                            link(ins)
                            kth = g8[:, :, k - 1:k].to_broadcast([P, NT, n])
                            dve.tensor_tensor(a1[:, :, :], src[:, :, :], kth, ALU.is_gt)
                            link(dve.tensor_tensor(a2[:, :, :], src[:, :, :], kth, ALU.is_equal))
                            dve.tensor_reduce(need[:, :], a1[:, :, :], AX.X, ALU.add)
                            for j in range(NT):
                                ins = dve.tensor_tensor_scan(a3[:, j, :], one_c[:, 0:n], a2[:, j, :], 0.0, ALU.mult, ALU.add)
                            link(ins)
                            link(dve.tensor_tensor(a3[:, :, :], a3[:, :, :], need[:, :].unsqueeze(2).to_broadcast([P, NT, n]), ALU.add))
                            link(dve.scalar_tensor_tensor(a3[:, :, :], a3[:, :, :], float(k), a2[:, :, :], ALU.is_le, ALU.mult))
                            link(dve.tensor_tensor(dst[:, :, :], a1[:, :, :], a3[:, :, :], ALU.add))

                        top(gs, ga1, ga2, ga3, NG, TOPG, ga1)
                        link(dve.tensor_scalar(ga2[:, :, :], ga1[:, :, :], BIG, -BIG, ALU.mult, ALU.add))
                        for j in range(NT):
                            link(dve.tensor_tensor(e1[:, j, :].rearrange("p (g e) -> p g e", g=NG),
                                                   biased[:, j, :].rearrange("p (g e) -> p g e", g=NG),
                                                   ga1[:, j, :].unsqueeze(2).to_broadcast([P, NG, EPG]), ALU.mult))
                            ins = dve.tensor_tensor(biased[:, j, :].rearrange("p (g e) -> p g e", g=NG),
                                                    e1[:, j, :].rearrange("p (g e) -> p g e", g=NG),
                                                    ga2[:, j, :].unsqueeze(2).to_broadcast([P, NG, EPG]), ALU.add)
                        link(ins)
                        top(biased, e1, e2, e3, NE, TOPK, chosen)
                        valid = ccol("valid")
                        dve.tensor_tensor(chosen[:, :, :], chosen[:, :, :], valid.unsqueeze(2).to_broadcast([P, NT, NE]),
                                          ALU.mult).then_inc(chosen_ready, 1)
                        dve.wait_ge(chosen_ready, 1)
                        link(dve.tensor_tensor(wgt[:, :, :], chosen[:, :, :], score[:, :, :], ALU.mult))
                        link(dve.tensor_reduce(need[:, :], wgt[:, :, :], AX.X, ALU.add))
                        link(dve.tensor_tensor(need[:, :], need[:, :], valid, ALU.subtract))
                        link(dve.tensor_scalar(need[:, :], need[:, :], 1.0, None, ALU.add))
                        link(dve.reciprocal(need[:, :], need[:, :]))
                        dve.tensor_tensor(wgt[:, :, :], wgt[:, :, :], need[:, :].unsqueeze(2).to_broadcast([P, NT, NE]), ALU.mult)
                        for j in range(NT):
                            ins = dve.tensor_tensor_scan(rank[:, j, :], one_c[:, :], chosen[:, j, :], 0.0, ALU.mult, ALU.add)
                        link(ins)
                        dve.wait_ge(pos_done, 1)
                        link(dve.tensor_copy(pos[:, :, :], bank[:, 0, 0:NT * NE].rearrange("p (a e) -> p a e", a=NT)))
                        expert = ccol("expert").unsqueeze(1).to_broadcast([P, NT, NE])
                        for k in range(TOPK):
                            link(dve.scalar_tensor_tensor(e1[:, :, :], rank[:, :, :], float(k + 1), chosen[:, :, :],
                                                          ALU.is_equal, ALU.mult))
                            for src, dst in ((expert, ek), (pos[:, :, :], pk), (wgt[:, :, :], w6)):
                                link(dve.tensor_tensor(e2[:, :, :], e1[:, :, :], src, ALU.mult))
                                link(dve.tensor_reduce(dst[:, :, k], e2[:, :, :], AX.X, ALU.add))
                        link(dve.tensor_scalar(w6[:, :, :], w6[:, :, :], ROUTE, None, ALU.mult))
                        link(dve.tensor_scalar(ck[:, :, :], pk[:, :, :], float(LB), None, ALU.is_ge))
                        for r in range(2, ROUNDS):
                            link(dve.scalar_tensor_tensor(ck[:, :, :], pk[:, :, :], float(r * LB), ck[:, :, :], ALU.is_ge, ALU.add))
                        link(dve.scalar_tensor_tensor(ek[:, :, :], ck[:, :, :], float(NE - LB * NBLK), ek[:, :, :], ALU.mult, ALU.add))
                        link(dve.scalar_tensor_tensor(ek[:, :, :], pk[:, :, :], float(NBLK), ek[:, :, :], ALU.mult, ALU.add))
                        link(dve.tensor_scalar(need[:, :], valid, -float(SKIP), float(SKIP), ALU.mult, ALU.add))
                        dve.tensor_tensor(addr[:, :, :], ek[:, :, :], need[:, :].unsqueeze(2).to_broadcast([P, NT, TOPK]),
                                          ALU.add).then_inc(addr_ready, 1)
                        dve.memset(one_r[:, :], 1.0)
                        for r in range(1, ROUNDS):
                            ins = dve.tensor_scalar(behind[:, (r - 1) * NE:r * NE], bank[0:1, 0, NT * NE:(NT + 1) * NE],
                                                    float(r * LB), None, ALU.is_gt)
                        link(ins)
                        link(dve.tensor_tensor_scan(behind_n[:, :], one_r[:, :], behind[:, :], 0.0, ALU.mult, ALU.add))
                        link(dve.tensor_copy(over[:, :], behind_n[:, NBLK - NE - 1:]))
                        for i in range(2):
                            dve.wait_ge(sg_ready9, i + 1)
                            dve.tensor_tensor(hs[:, i, :], sg[:, i, :], bank[:, 4 + i, 0:T], ALU.mult).then_inc(hs_ready, 1)

                    @block.gpsimd
                    def _(pool):
                        pool.wait_ge(addr_ready, 1)
                        pool.wait_ge(route_in, 32)
                        pool.wait_ge(lists_filled, 16)
                        for j in range(NT):
                            n = TILE_ROWS[j]
                            for k in range(TOPK):
                                pool.indirect_dma_start(lists, bass.IndirectOffsetOnAxis(ap=addr[0:n, j, k:k + 1].bitcast(U32), axis=0),
                                                        vals[0:n, j, k, :], None, bounds_check=LB * NBLK - 1,
                                                        oob_is_err=False).then_inc(lists_set, 16)

            with ExitStack() as ph:
                xg = [sb(f"xg{i}", [LB, D], stack=ph) for i in range(2)]
                xt = [sb(f"xt{i}", [P, KD, LB], stack=ph) for i in range(2)]
                sg = [sb(f"sg{i}", [LB, FE], stack=ph) for i in range(2)]
                hh = [sb(f"hh{i}", [LB, FE], stack=ph) for i in range(2)]
                ht = [sb(f"ht{i}", [P, 2, LB], stack=ph) for i in range(2)]
                yo = [sb(f"yo{i}", [LB, D], stack=ph) for i in range(2)]
                gi = [sb(f"gi{i}", [LB, 1], I32, stack=ph) for i in range(2)]
                si = [sb(f"si{i}", [LB, 1], I32, stack=ph) for i in range(2)]
                x_in = [sem(f"x_in{i}", ph) for i in range(2)]
                y_out = [sem(f"y_out{i}", ph) for i in range(2)]
                clear, idx_ready = sem("clear", ph), sem("idx_ready", ph)
                xt_done, xt_ready, gu_done, sg_ready, hh_ready = (sem("xt_done", ph), sem("xt_ready", ph), sem("gu_done", ph),
                                                                  sem("sg_ready", ph), sem("hh_ready", ph))
                ht_done, ht_ready, y_done, y_ready = sem("ht_done", ph), sem("ht_ready", ph), sem("y_done", ph), sem("y_ready", ph)

                with nc.Block() as block:
                    @block.sync
                    def _(sp):
                        with sp.Fori(1, NE // 2) as i:
                            for half in range(2):
                                e = 2 * i + half
                                sp.wait_ge(gu_done, e - 1)
                                sp.dma_start(gu_w[half], io["w_gu"][bass.ds(e, 1)].rearrange("a p k c -> (a p) k c")
                                             ).then_inc(gu_in[half], 16)
                                sp.wait_ge(y_done, e - 1)
                                sp.dma_start(dn_w[half], io["w_dn"][bass.ds(e, 1)].rearrange("a p k c -> (a p) k c")
                                             ).then_inc(dn_in[half], 16)

                    @block.gpsimd
                    def _(pool):
                        for half in range(2):
                            pool.memset(xg[half][:, :], 0.0).then_inc(clear, 1)
                        pool.wait_ge(clear, 2)
                        def step(e, half, r, gathers, scatters, count):
                            n = count
                            if gathers:
                                if e >= 2:
                                    pool.wait_ge(xt_done, r - 1)
                                    pool.sem_inc(pool_order, 1)
                                pool.tensor_copy(gi[half][:, :], tab[:, bass.ds(r, 1), 0]).then_inc(idx_ready, 1)
                                n = n + 1
                                pool.wait_ge(idx_ready, n)
                                pool.sem_inc(pool_order, 1)
                                pool.indirect_dma_start(xg[half][:, :], None, tok_rows,
                                                        bass.IndirectOffsetOnAxis(ap=gi[half][:, :].bitcast(U32), axis=0),
                                                        bounds_check=T - 1, oob_is_err=False).then_inc(x_in[half], 16)
                            if scatters:
                                other = 1 - half
                                pool.wait_ge(y_ready, r - 2)
                                pool.sem_inc(pool_order, 1)
                                pool.tensor_copy(si[other][:, :], tab[:, bass.ds(r - 3, 1), 1]).then_inc(idx_ready, 1)
                                n = n + 1
                                pool.wait_ge(idx_ready, n)
                                pool.sem_inc(pool_order, 1)
                                pool.indirect_dma_start(choice_rows,
                                                        bass.IndirectOffsetOnAxis(ap=si[other][:, :].bitcast(U32), axis=0),
                                                        yo[other][:, :], None, bounds_check=T * TOPK - 1,
                                                        oob_is_err=False).then_inc(y_out[other], 16)
                            return n
                        n = 0
                        for e in range(4):
                            n = step(e, e % 2, e, True, e >= 3, n)
                        with pool.Fori(2, NE // 2) as i:
                            for half in range(2):
                                step(4, half, 2 * i + half, True, True, 4 * i + 2 * half - 3)
                        n = 2 * NE - 3
                        for e in range(NE, NE + 3):
                            n = step(e, e % 2, e, False, True, n)
                        for half in range(2):
                            pool.wait_ge(y_out[half], 16 * NE // 2)

                    @block.tensor
                    def _(pe):
                        def turn_rows(e1, half, i1):
                            pe.wait_ge(x_in[half], 16 * i1 + 16)
                            pe.sem_inc(pe_order, 1)
                            for k in range(KD):
                                mm = pe.transpose(bank[:, 2 + half, k * LB:(k + 1) * LB],
                                                  xg[half][:, k * P:(k + 1) * P], ident[0:LB, 0:LB])
                            mm.then_inc(xt_done, 1)

                        def outputs(half, e0, i0):
                            pe.wait_ge(ht_ready, e0 + 1)
                            pe.wait_ge(dn_in[half], 16 * i0 + 16)
                            for k in range(2):
                                for c in range(2):
                                    mm = pe.matmul(bank[c * LB:(c + 1) * LB, 6 + half, :], ht[half][:, k, :],
                                                   dn_w[half][:, k, c * 512:(c + 1) * 512], start=(k == 0), stop=(k == 1))
                            mm.then_inc(y_done, 1)

                        def step(half, e, i, first=False, last=False, second=False):
                            pe.wait_ge(gu_in[half], 16 * i + 16)
                            pe.wait_ge(xt_ready, e + 1)
                            for k in range(KD):
                                for c in range(2):
                                    mm = pe.matmul(bank[c * LB:(c + 1) * LB, half, 0:FE], xt[half][:, k, :],
                                                   gu_w[half][:, k, c * FE:(c + 1) * FE], start=(k == 0), stop=(k == KD - 1))
                            mm.then_inc(gu_done, 1)
                            if not last:
                                turn_rows(e + 1, 1 - half, i + half)
                            if not first:
                                if not second:
                                    pe.wait_ge(y_ready, e - 1)
                                outputs(1 - half, e - 1, i - 1 + half)
                            pe.wait_ge(hh_ready, e + 1)
                            pe.sem_inc(pe_order, 1)
                            for k in range(2):
                                mm = pe.transpose(bank[:, 4, k * LB:(k + 1) * LB], hh[half][:, k * P:(k + 1) * P], ident[0:LB, 0:LB])
                            mm.then_inc(ht_done, 1)
                        pe.wait_ge(clear, 2)
                        turn_rows(0, 0, 0)
                        step(0, 0, 0, first=True)
                        step(1, 1, 0, second=True)
                        with pe.Fori(1, NE // 2 - 1) as i:
                            for half in range(2):
                                step(half, 2 * i + half, i)
                        step(0, NE - 2, NE // 2 - 1)
                        step(1, NE - 1, NE // 2 - 1, last=True)
                        pe.wait_ge(y_ready, NE - 1)
                        outputs(1, NE - 1, NE // 2 - 1)

                    @block.scalar
                    def _(act):
                        def rows_t(half, e):
                            act.wait_ge(xt_done, e + 1)
                            act.copy(xt[half][:, :, :], bank[:, 2 + half, :].rearrange("p (k n) -> p k n", n=LB)).then_inc(xt_ready, 1)

                        def step(half, e, first=False, last=False):
                            act.wait_ge(gu_done, e + 1)
                            if not first:
                                act.wait_ge(hh_ready, e - 1)
                            act.activation(sg[half][:, :], bank[0:LB, half, 0:FE], ACT.Silu).then_inc(sg_ready, 1)
                            if not last:
                                rows_t(1 - half, e + 1)
                        rows_t(0, 0)
                        step(0, 0, first=True)
                        step(1, 1, first=True)
                        with act.Fori(1, NE // 2 - 1) as i:
                            for half in range(2):
                                step(half, 2 * i + half)
                        step(0, NE - 2)
                        step(1, NE - 1, last=True)

                    @block.vector
                    def _(dve):
                        def rows_out(half, e, i, waits):
                            dve.wait_ge(y_done, e + 1)
                            if waits:
                                dve.wait_ge(y_out[half], 16 * i)
                            dve.tensor_copy(yo[half][:, 0:512], bank[0:LB, 6 + half, :])
                            dve.tensor_copy(yo[half][:, 512:], bank[LB:2 * LB, 6 + half, :]).then_inc(y_ready, 1)

                        def step(half, e, i, first=False, early=False):
                            dve.wait_ge(sg_ready, e + 1)
                            if not first and not early:
                                dve.wait_ge(ht_done, e - 1)
                            dve.tensor_tensor(hh[half][:, :], sg[half][:, :], bank[LB:2 * LB, half, 0:FE], ALU.mult).then_inc(hh_ready, 1)
                            if not first:
                                rows_out(1 - half, e - 1, i - 1 + half, not early)
                            dve.wait_ge(ht_done, e + 1)
                            dve.tensor_copy(ht[half][:, :, :], bank[:, 4, 0:2 * LB].rearrange("p (k n) -> p k n", k=2)).then_inc(ht_ready, 1)
                        step(0, 0, 0, first=True)
                        step(1, 1, 0, early=True)
                        dve.wait_ge(sg_ready, 3)
                        dve.wait_ge(ht_done, 1)
                        dve.tensor_tensor(hh[0][:, :], sg[0][:, :], bank[LB:2 * LB, 0, 0:FE], ALU.mult).then_inc(hh_ready, 1)
                        rows_out(1, 1, 0, False)
                        dve.wait_ge(ht_done, 3)
                        dve.tensor_copy(ht[0][:, :, :], bank[:, 4, 0:2 * LB].rearrange("p (k n) -> p k n", k=2)).then_inc(ht_ready, 1)
                        step(1, 3, 1)
                        with dve.Fori(2, NE // 2) as i:
                            for half in range(2):
                                step(half, 2 * i + half, i)
                        rows_out(1, NE - 1, NE // 2 - 1, True)

                blocks = sb("blocks", [1, MAXOVER], I32, stack=ph)
                owners = sb("owners", [1, MAXOVER], I32, stack=ph)
                found = sb("found", [1, MAXOVER], stack=ph)
                found_e = sb("found_e", [1, MAXOVER], stack=ph)
                pick = sb("pick", [1, MAXOVER, NBLK - NE], stack=ph)
                w_in2, x_in2, y_out2 = sem("w_in2", ph), sem("x_in2", ph), sem("y_out2", ph)
                idx2, xt_done2, xt_ready2, gu_done2, sg_ready2, hh_ready2 = (
                    sem("idx2", ph), sem("xt_done2", ph), sem("xt_ready2", ph), sem("gu_done2", ph), sem("sg_ready2", ph),
                    sem("hh_ready2", ph))
                ht_done2, ht_ready2, y_done2, y_ready2 = (sem("ht_done2", ph), sem("ht_ready2", ph), sem("y_done2", ph),
                                                          sem("y_ready2", ph))
                listed, list_order = sem("listed", ph), sem("list_order", ph)

                def behind_first(eng):
                    return eng.value_load(over[0:1, 0:1], min_val=0, max_val=MAXOVER)

                with nc.Block() as block:
                    @block.sync
                    def _(sp):
                        more = behind_first(sp)
                        with sp.If(more > 0):
                            sp.wait_ge(listed, 1)
                            with sp.Fori(0, more) as n:
                                e = sp.value_load(owners[0:1, bass.ds(n, 1)], min_val=0, max_val=NE - 1)
                                sp.dma_start(gu_w[0], io["w_gu"][bass.ds(e, 1)].rearrange("a p k c -> (a p) k c")).then_inc(w_in2, 16)
                                sp.dma_start(dn_w[0], io["w_dn"][bass.ds(e, 1)].rearrange("a p k c -> (a p) k c")).then_inc(w_in2, 16)
                                sp.wait_ge(y_done2, n + 1)
                                sp.sem_inc(sp_order, 1)

                    @block.gpsimd
                    def _(pool):
                        more = behind_first(pool)
                        with pool.If(more > 0):
                            pool.wait_ge(listed, 1)
                            with pool.Fori(0, more) as n:
                                blk = pool.value_load(blocks[0:1, bass.ds(n, 1)], min_val=NE, max_val=NBLK - 1)
                                pool.tensor_copy(gi[0][:, :], tab[:, bass.ds(blk, 1), 0]).then_inc(idx2, 1)
                                pool.tensor_copy(si[0][:, :], tab[:, bass.ds(blk, 1), 1]).then_inc(idx2, 1)
                                pool.wait_ge(idx2, 2 * n + 2)
                                pool.sem_inc(pool_order, 1)
                                pool.indirect_dma_start(xg[0][:, :], None, tok_rows,
                                                        bass.IndirectOffsetOnAxis(ap=gi[0][:, :].bitcast(U32), axis=0),
                                                        bounds_check=T - 1, oob_is_err=False).then_inc(x_in2, 16)
                                pool.wait_ge(y_ready2, n + 1)
                                pool.sem_inc(pool_order, 1)
                                pool.indirect_dma_start(choice_rows,
                                                        bass.IndirectOffsetOnAxis(ap=si[0][:, :].bitcast(U32), axis=0),
                                                        yo[0][:, :], None, bounds_check=T * TOPK - 1,
                                                        oob_is_err=False).then_inc(y_out2, 16)
                                pool.wait_ge(y_out2, 16 * n + 16)
                                pool.sem_inc(pool_order, 1)

                    @block.tensor
                    def _(pe):
                        more = behind_first(pe)
                        with pe.If(more > 0):
                            with pe.Fori(0, more) as n:
                                pe.wait_ge(x_in2, 16 * n + 16)
                                pe.sem_inc(pe_order, 1)
                                for k in range(KD):
                                    mm = pe.transpose(bank[:, 2, k * LB:(k + 1) * LB], xg[0][:, k * P:(k + 1) * P],
                                                      ident[0:LB, 0:LB])
                                mm.then_inc(xt_done2, 1)
                                pe.wait_ge(xt_ready2, n + 1)
                                pe.wait_ge(w_in2, 32 * n + 32)
                                for k in range(KD):
                                    for c in range(2):
                                        mm = pe.matmul(bank[c * LB:(c + 1) * LB, 0, 0:FE], xt[0][:, k, :],
                                                       gu_w[0][:, k, c * FE:(c + 1) * FE], start=(k == 0), stop=(k == KD - 1))
                                mm.then_inc(gu_done2, 1)
                                pe.wait_ge(hh_ready2, n + 1)
                                pe.sem_inc(pe_order, 1)
                                for k in range(2):
                                    mm = pe.transpose(bank[:, 4, k * LB:(k + 1) * LB], hh[0][:, k * P:(k + 1) * P],
                                                      ident[0:LB, 0:LB])
                                mm.then_inc(ht_done2, 1)
                                pe.wait_ge(ht_ready2, n + 1)
                                for k in range(2):
                                    for c in range(2):
                                        mm = pe.matmul(bank[c * LB:(c + 1) * LB, 6, :], ht[0][:, k, :],
                                                       dn_w[0][:, k, c * 512:(c + 1) * 512], start=(k == 0), stop=(k == 1))
                                mm.then_inc(y_done2, 1)

                    @block.scalar
                    def _(act):
                        more = behind_first(act)
                        with act.If(more > 0):
                            with act.Fori(0, more) as n:
                                act.wait_ge(xt_done2, n + 1)
                                act.copy(xt[0][:, :, :], bank[:, 2, :].rearrange("p (k n) -> p k n", n=LB)).then_inc(xt_ready2, 1)
                                act.wait_ge(gu_done2, n + 1)
                                act.activation(sg[0][:, :], bank[0:LB, 0, 0:FE], ACT.Silu).then_inc(sg_ready2, 1)

                    @block.vector
                    def _(dve):
                        more = behind_first(dve)
                        with dve.If(more > 0):
                            later = con[0:1, CONSTS["later"][0]:CONSTS["later"][1]]
                            count = con[0:1, CONSTS["count"][0]:CONSTS["count"][1]]
                            wide = [1, MAXOVER, NBLK - NE]
                            steps = [0]

                            def step2(ins):
                                steps[0] += 1
                                ins.then_inc(list_order, 1)
                                dve.wait_ge(list_order, steps[0])
                            step2(dve.tensor_tensor(pick[:, :, :], behind_n[:, :].unsqueeze(1).to_broadcast(wide),
                                                   count.unsqueeze(2).to_broadcast(wide), ALU.is_equal))
                            step2(dve.tensor_tensor(pick[:, :, :], pick[:, :, :], behind[:, :].unsqueeze(1).to_broadcast(wide), ALU.mult))
                            step2(dve.tensor_tensor(pick[:, :, :], pick[:, :, :], later.unsqueeze(1).to_broadcast(wide), ALU.mult))
                            step2(dve.tensor_reduce(found[:, :], pick[:, :, :], AX.X, ALU.add))
                            step2(dve.tensor_scalar(found_e[:, :], found[:, :], float(NE), None, ALU.subtract))
                            for r in range(2, ROUNDS):
                                step2(dve.tensor_scalar(pick[:, :, 0], found[:, :], float(r * NE), -float(NE), ALU.is_ge, ALU.mult))
                                step2(dve.tensor_tensor(found_e[:, :], found_e[:, :], pick[:, :, 0], ALU.add))
                            dve.tensor_copy(owners[:, :], found_e[:, :])
                            dve.tensor_copy(blocks[:, :], found[:, :]).then_inc(listed, 1)
                            with dve.Fori(0, more) as n:
                                dve.wait_ge(sg_ready2, n + 1)
                                dve.tensor_tensor(hh[0][:, :], sg[0][:, :], bank[LB:2 * LB, 0, 0:FE], ALU.mult).then_inc(hh_ready2, 1)
                                dve.wait_ge(ht_done2, n + 1)
                                dve.tensor_copy(ht[0][:, :, :], bank[:, 4, 0:2 * LB].rearrange("p (k n) -> p k n", k=2)).then_inc(ht_ready2, 1)
                                dve.wait_ge(y_done2, n + 1)
                                dve.tensor_copy(yo[0][:, 0:512], bank[0:LB, 6, :])
                                dve.tensor_copy(yo[0][:, 512:], bank[LB:2 * LB, 6, :]).then_inc(y_ready2, 1)

            with ExitStack() as ph:
                cr = [sb(f"cr{i}", [P, TOPK, D], stack=ph) for i in range(2)]
                cr_s = sb("cr_s", [TS, TOPK, D], stack=ph)
                diag = sb("diag", [P, NT, TOPK, P], stack=ph)
                ff = sb("ff", [P, KD, T], stack=ph)
                y = sb("y", [P, KD, T], stack=ph)
                rows_in = [[sem(f"rows_in{j}_{h}", ph) for h in range(2)] for j in range(NT)]
                diag_ready, sum_done, ff_ready, y_ready11 = (sem("diag_ready", ph), sem("sum_done", ph),
                                                                      sem("ff_ready", ph), sem("y_ready11", ph))
                with nc.Block() as block:
                    @block.sync
                    def _(sp):
                        for j in range(NT):
                            n = TILE_ROWS[j]
                            dst = (cr[0], cr[1], cr_s)[j]
                            for h in range(2):
                                cols = slice(h * D // 2, (h + 1) * D // 2)
                                sp.dma_start(dst[:, :, cols],
                                             choice_rows.rearrange("(t k) d -> t k d", k=TOPK)[j * P:j * P + n, :, cols]
                                             ).then_inc(rows_in[j][h], 16)
                        sp.wait_ge(y_ready11, 1)
                        store(sp, io["y"], y[:, :, :])
                        sp.wait_ge(stored, n_stored[0])

                    @block.vector
                    def _(dve):
                        for j in range(NT):
                            for k in range(TOPK):
                                ins = dve.tensor_scalar(diag[:, j, k, :], ident, w6[:, j, k:k + 1], None, ALU.mult)
                        ins.then_inc(diag_ready, 1)
                        dve.wait_ge(sum_done, 2)
                        dve.tensor_tensor(ff[:, :, 0:TP], bank[:, 0:4, :].rearrange("p a (d t) -> p (a d) t", t=TP),
                                          shared[:, :, 0:TP], ALU.add)
                        dve.wait_ge(sum_done, 3)
                        dve.tensor_tensor(ff[:, :, TP:T], bank[:, 5, 0:KD * TS].rearrange("p (d t) -> p d t", t=TS),
                                          shared[:, :, TP:T], ALU.add).then_inc(ff_ready, 1)
                        dve_rstd(7)
                        dve_residual(ff[:, :, :], y, pcol("g_post_ffn"), 5, y_ready11)

                    @block.scalar
                    def _(act):
                        act.wait_ge(ff_ready, 1)
                        act_square(7, ff[:, :, :], KD)
                        act_root(7, D, 4)

                    @block.tensor
                    def _(pe):
                        pe.wait_ge(diag_ready, 1)
                        for j in range(NT):
                            n = TILE_ROWS[j]
                            src = (cr[0], cr[1], cr_s)[j]
                            for d in range(KD):
                                if d == 0:
                                    pe.wait_ge(rows_in[j][0], 16)
                                if d == KD // 2:
                                    pe.wait_ge(rows_in[j][1], 16)
                                at = d % 2 * TP + j * P
                                out = bank[:, d // 2, at:at + n] if j < 2 else bank[:, 5, d * TS:(d + 1) * TS]
                                for k in range(TOPK):
                                    mm = pe.matmul(out, src[:, k, d * P:(d + 1) * P], diag[0:n, j, k, 0:n],
                                                   start=(k == 0), stop=(k == TOPK - 1))
                            mm.then_inc(sum_done, 1)
                        pe_norm(7, KD, 4)


OUTPUTS = {"y": [P, KD, T], "ckv": [P, 2, T], "kpe": [ROPE, T], "conv_p": [P, KC, CW - 1], "conv_s": [P, KC, CW - 1, TS],
           "ssm_p": [P, SH, SP_], "ssm_s": [P, TS, SH, SP_]}


def tiles_of(w, n, k=KD, c=P):
    return w.reshape(k, P, n, c).transpose(2, 1, 0, 3)


def by_partition(v):
    v = v.reshape(v.shape[:-1] + (v.shape[-1] // P, P))
    return np.moveaxis(v, -1, 0)


def lay_out(i):
    f = {k: np.asarray(v) for k, v in i.items()}
    a = {}
    xs = np.concatenate([f["x_prompt"][0], f["x_sample"][:, 0]], 0)
    a["x_t"] = by_partition(xs).transpose(0, 2, 1)
    a["c_t"] = by_partition(np.concatenate([f["c_prompt"], f["c_sample"]], 0)).transpose(0, 2, 1)
    units = np.zeros((N_UNITS + 2, P, UW), np.float32)
    units[ADA_AT] = tiles_of(f["w_ada"][0], N_ADA, c=4 * P).reshape(N_ADA, P, UW)
    w = f["w_in"][0]
    at = np.cumsum([0, QL, KVL, ROPE, DI, CC, SH, D, D])
    part = [w[:, at[n]:at[n + 1]] for n in range(8)]
    half = ROPE // 2
    kp = part[2]
    kp_sw = np.concatenate([kp[:, half:], kp[:, :half]], 1)
    dt = np.concatenate([part[5], np.zeros((D, P - SH), np.float32)], 1)
    w = np.concatenate([part[0], part[1], kp, kp, kp, kp, kp_sw, kp_sw, kp_sw, kp_sw, dt, part[4], part[3], part[6], part[7]], 1)
    units[WIN_AT] = tiles_of(w, 44).reshape(N_WIN, 4, P, KD * P).transpose(0, 2, 1, 3).reshape(N_WIN, P, UW)
    qb = f["w_q_b"][0].reshape(3, P, NH, QH)
    qb = np.concatenate([qb, qb[..., NOPE + half:], qb[..., NOPE:NOPE + half]], -1)
    uk = f["w_uk"][0].reshape(2, P, NH * NOPE)
    units[U_QB] = np.concatenate([qb.transpose(1, 0, 2, 3).reshape(P, -1), uk.transpose(1, 0, 2).reshape(P, -1)], 1)
    units[U_OA] = f["w_o_attn"][0].reshape(4, P, D).transpose(1, 0, 2).reshape(P, UW)
    units[U_OS:U_OS + 2] = f["w_o_ssd"][0].reshape(2, 4, P, D).transpose(0, 2, 1, 3).reshape(2, P, UW)
    units[U_OUT:U_OUT + 2] = tiles_of(f["w_out"][0], 8).reshape(2, 4, P, KD * P).transpose(0, 2, 1, 3).reshape(2, P, UW)
    sgu = np.concatenate([f["w_gate_s"][0], f["w_up_s"][0]], 1)
    units[U_SGU] = tiles_of(sgu, 4).transpose(1, 0, 2, 3).reshape(P, UW)
    units[U_SDN, :, 0:2 * D] = f["w_down_s"][0].reshape(2, P, D).transpose(1, 0, 2).reshape(P, -1)
    units[U_SDN, :, 2 * D:2 * D + KD * NE] = f["w_router"][0].reshape(KD, P, NE).transpose(1, 0, 2).reshape(P, -1)
    a["w_units"] = units
    a["w_uv"] = f["w_uv"][0].reshape(2, P, NH * VD).transpose(1, 0, 2)
    a["w_ukt"] = f["w_uk"][0].transpose(2, 1, 0)
    a["state_conv"] = by_partition(f["state_conv"][0]).transpose(0, 3, 2, 1)
    a["state_ssm"] = f["state_ssm"][0].transpose(3, 0, 1, 2)
    a["cache"] = np.concatenate([f["cache_ckv"][0], f["cache_kpe"][0]], -1)
    a["page_table"] = f["page_table"].reshape(1, -1)
    a["w_gu"] = np.concatenate([f["w_gate_e"][0].reshape(NE, KD, P, FE), f["w_up_e"][0].reshape(NE, KD, P, FE)],
                               -1).transpose(0, 2, 1, 3)
    a["w_dn"] = f["w_down_e"][0].reshape(NE, 2, P, D).transpose(0, 2, 1, 3)
    par = np.zeros((P, NPAR), np.float32)

    def put(name, v):
        lo, hi = PARAMS[name]
        par[:, lo:hi] = v
    put("b_ada", by_partition(f["b_ada"][0]))
    for name in ("g_pre_mix", "g_post_mix", "g_pre_ffn", "g_post_ffn", "g_q_a", "g_kv_a", "g_ssd"):
        put(name, by_partition(f[name][0]))
    put("d_skip", by_partition(np.repeat(f["d_skip"][0], SP_)))
    put("conv_w", by_partition(f["conv_w"][0]).transpose(0, 2, 1).reshape(P, -1))
    put("conv_b", by_partition(f["conv_b"][0]))
    lo = PARAMS["heads"][0]
    par[0:SH, lo] = f["dt_bias"][0]
    par[0:SH, lo + 1] = f["a_log"][0]
    put("b_router", np.broadcast_to(f["b_router"][0], (P, NE)))
    a["params"] = par
    return a


def constants():
    con = np.zeros((P, NCON), np.float32)

    def put(name, v):
        lo, hi = CONSTS[name]
        con[:, lo:hi] = v
    r = np.arange(P)
    put("ident", np.eye(P))
    put("ones", 1.0)
    put("causal_t", r[:, None] <= r[None, :])
    put("before", r[:, None] < r[None, :])
    put("mask", np.where(r[None, :] <= r[:, None], 0.0, -BIG))
    half = ROPE // 2
    place = np.concatenate([np.arange(TP), np.full(TS, PAST)]).astype(np.float32)
    inv = (np.float32(10000.0) ** (-np.arange(half, dtype=np.float32) / half)).astype(np.float32)
    ang = (place[None, :] * inv[:, None]).astype(np.float32)
    put("cos", np.tile(np.cos(ang), (P // half, 1)))
    put("sin", np.tile(np.concatenate([-np.sin(ang), np.sin(ang)]), (P // ROPE, 1)))
    put("eps", EPS)
    put("expert", np.arange(NE)[None, :])
    put("later", np.arange(NE, NBLK)[None, :])
    put("count", np.arange(1, MAXOVER + 1)[None, :])
    put("same_head", r[:, None] % 32 == np.arange(NH)[None, :])
    put("valid", (np.arange(NT)[None, :] * P + r[:, None] < T))
    sel = np.zeros((SH, SH, P), np.float32)
    for hd in range(SH):
        sel[hd, hd] = 1.0
    tok = np.minimum(np.arange(NT)[None, :] * P + r[:, None], T - 1)
    vals = np.stack([np.broadcast_to(tok[..., None], (P, NT, TOPK)), tok[..., None] * TOPK + np.arange(TOPK)], -1).astype(np.int32)
    return {"consts": con, "sel": sel, "vals": vals, "fill": np.full((LB, NBLK, 2), SKIP, np.int32)}


def kernel(**inputs):
    import concourse.bacc as bacc
    from concourse.bass_utils import run_bass_kernel_spmd

    nc = bacc.Bacc("TRN2", target_bir_lowering=False, num_devices=1)
    arrays = {k: np.ascontiguousarray(v) for k, v in {**lay_out(inputs), **constants()}.items()}
    io = {k: nc.dram_tensor(f"in_{k}", v.shape, mybir.dt.from_np(v.dtype), kind="ExternalInput").ap() for k, v in arrays.items()}
    for k, shape in OUTPUTS.items():
        io[k] = nc.dram_tensor(f"out_{k}", shape, F32, kind="ExternalOutput").ap()
    build(nc, io)
    r = run_bass_kernel_spmd(nc, [{f"in_{k}": v for k, v in arrays.items()}], core_ids=[0]).results[0]
    o = {k: np.asarray(r[f"out_{k}"]) for k in OUTPUTS}

    def rows(v):
        return np.ascontiguousarray(v.transpose(2, 1, 0).reshape(v.shape[2], -1))
    y, ckv = rows(o["y"]), rows(o["ckv"])
    kpe = np.ascontiguousarray(o["kpe"].T)
    conv_p = o["conv_p"].transpose(2, 1, 0).reshape(1, 1, CW - 1, CC)
    conv_s = o["conv_s"].transpose(3, 2, 1, 0).reshape(1, TS, CW - 1, CC)
    ssm_p = o["ssm_p"].transpose(1, 2, 0)[None, None]
    ssm_s = o["ssm_s"].transpose(1, 2, 3, 0)[None]
    return (y[None, 0:TP], y[TP:, None], ckv[None, None, 0:TP], kpe[None, None, 0:TP], np.ascontiguousarray(conv_p),
            np.ascontiguousarray(ssm_p), ckv[None, TP:, None], kpe[None, TP:, None], np.ascontiguousarray(conv_s),
            np.ascontiguousarray(ssm_s))
```
